# Optimizing a Trainium2 kernel written in Bass

```python
import math
import jax, jax.numpy as jnp
from jax import lax
import numpy as np

D_MODEL = 1024
BATCH = 1
SEQ = 2048
DEPTH = 1
DEC_BATCH = 8
DEC_SEQ = 8
PAST_LEN = 4096
PAGE_SIZE = 128

SSM_WIDTH = D_MODEL // 2
SSM_GROUP = 16
N_SSM_GROUPS = SSM_WIDTH // SSM_GROUP
SSM_STATE = 64
ATTN_WIDTH = D_MODEL - SSM_WIDTH
HEAD_DIM = 64
N_HEADS = ATTN_WIDTH // HEAD_DIM
N_KV_HEADS = 2
GQA = N_HEADS // N_KV_HEADS
KV_WIDTH = N_KV_HEADS * HEAD_DIM
IN_WIDTH = SSM_WIDTH + ATTN_WIDTH + 2 * KV_WIDTH
WINDOW = 128
BLOCK = 128
NUM_BUCKETS = 32
MAX_DISTANCE = 128
N_EXPERT_GROUPS = 4
EXPERTS_PER_GROUP = 4
N_EXPERTS = N_EXPERT_GROUPS * EXPERTS_PER_GROUP
TOP_K = 2
D_EXPERT = 256
N_MOD = 6
EPS = 1e-6
NEG_INF = -1e30

kernel_name = "hymba_s5_swa_sink_hmoe_decode_step"

def rms_norm(x, g):
    x32 = x.astype(jnp.float32)
    y = x32 * lax.rsqrt(jnp.mean(x32 * x32, axis=-1, keepdims=True) + EPS)
    return (y * g.astype(jnp.float32)).astype(x.dtype)

def rel_bucket(dist):
    max_exact = NUM_BUCKETS // 2
    d = jnp.maximum(dist, 0)
    log_ratio = jnp.log(jnp.maximum(d, 1).astype(jnp.float32) / max_exact) / math.log(MAX_DISTANCE / max_exact)
    large = jnp.minimum(max_exact + (log_ratio * (NUM_BUCKETS - max_exact)).astype(jnp.int32), NUM_BUCKETS - 1)
    return jnp.where(d < max_exact, d, large)

def rel_bias(dist, table):
    b = table[rel_bucket(dist)].astype(jnp.float32)
    b = jnp.moveaxis(b, -1, 0)
    return b.reshape((N_KV_HEADS, GQA) + dist.shape)

def sink_probs(s, sinks):
    sk = sinks.astype(jnp.float32).reshape(N_KV_HEADS, GQA, 1, 1)
    m = jnp.maximum(jnp.max(s, axis=-1, keepdims=True), sk)
    p = jnp.exp(s - m)
    return p / (jnp.sum(p, axis=-1, keepdims=True) + jnp.exp(sk - m))

def attn_prompt(q, k, v, sinks, table):
    b, s = q.shape[:2]
    nb = s // BLOCK
    qb = q.reshape(b, nb, BLOCK, N_KV_HEADS, GQA, HEAD_DIM)
    kb = k.reshape(b, nb, BLOCK, N_KV_HEADS, HEAD_DIM)
    vb = v.reshape(b, nb, BLOCK, N_KV_HEADS, HEAD_DIM)
    kk = jnp.concatenate([jnp.concatenate([jnp.zeros_like(kb[:, :1]), kb[:, :-1]], axis=1), kb], axis=2)
    vv = jnp.concatenate([jnp.concatenate([jnp.zeros_like(vb[:, :1]), vb[:, :-1]], axis=1), vb], axis=2)
    sc = jnp.einsum('bnqhgd,bnkhd->bnhgqk', qb, kk).astype(jnp.float32) * (HEAD_DIM ** -0.5)
    qi = jnp.arange(BLOCK)[:, None]
    kj = jnp.arange(2 * BLOCK)[None, :]
    dist = qi + BLOCK - kj
    band = (dist >= 0) & (dist <= WINDOW)
    exists = (jnp.arange(nb)[:, None] * BLOCK - BLOCK + kj) >= 0
    valid = band[None] & exists[:, None, :]
    sc = jnp.where(valid[None, :, None, None], sc + rel_bias(dist, table), NEG_INF)
    p = sink_probs(sc, sinks).astype(v.dtype)
    out = jnp.einsum('bnhgqk,bnkhd->bnqhgd', p, vv).reshape(b, s, ATTN_WIDTH)
    w = min(WINDOW, s)
    return out, k[:, s - w:], v[:, s - w:]

def attn_sample(q, k, v, k_cache, v_cache, sinks, table):
    t = q.shape[1]
    w = k_cache.shape[1]
    kk = jnp.concatenate([k_cache.astype(k.dtype), k], axis=1)
    vv = jnp.concatenate([v_cache.astype(v.dtype), v], axis=1)
    sc = jnp.einsum('bqhgd,bkhd->bhgqk', q, kk).astype(jnp.float32) * (HEAD_DIM ** -0.5)
    dist = jnp.arange(t)[:, None] + w - jnp.arange(w + t)[None, :]
    valid = (dist >= 0) & (dist <= WINDOW)
    sc = jnp.where(valid, sc + rel_bias(dist, table), NEG_INF)
    p = sink_probs(sc, sinks).astype(v.dtype)
    out = jnp.einsum('bhgqk,bkhd->bqhgd', p, vv).reshape(q.shape[0], t, ATTN_WIDTH)
    return out, kk[:, t:], vv[:, t:]

def s5_scan(u, lam_re, lam_im, log_dt, b_re, b_im, c_re, c_im, d_skip, h0_re=None, h0_im=None):
    bsz, l = u.shape[:2]
    u32 = u.astype(jnp.float32).reshape(bsz, l, N_SSM_GROUPS, SSM_GROUP)
    lam = lax.complex(lam_re.astype(jnp.float32), lam_im.astype(jnp.float32))
    dt = jnp.exp(log_dt.astype(jnp.float32))[:, None]
    lbar = jnp.exp(lam * dt)
    bbar = ((lbar - 1.0) / lam)[..., None] * lax.complex(b_re.astype(jnp.float32), b_im.astype(jnp.float32))
    cmat = lax.complex(c_re.astype(jnp.float32), c_im.astype(jnp.float32))
    bu = jnp.einsum('blgc,gpc->lbgp', u32.astype(jnp.complex64), bbar)
    if h0_re is not None:
        h0 = lax.complex(h0_re.astype(jnp.float32), h0_im.astype(jnp.float32))
        bu = bu.at[0].add(lbar * h0)
    a = jnp.broadcast_to(lbar, (l, 1) + lbar.shape)

    def combine(e1, e2):
        a1, b1 = e1
        a2, b2 = e2
        return a2 * a1, a2 * b1 + b2

    _, h = lax.associative_scan(combine, (a, bu), axis=0)
    y = jnp.einsum('lbgp,gcp->blgc', h, cmat).real
    y = y + d_skip.astype(jnp.float32).reshape(N_SSM_GROUPS, SSM_GROUP) * u32
    return y.reshape(bsz, l, SSM_WIDTH).astype(u.dtype), h[-1]

def hier_moe(x, w_gr, b_gr, w_er, b_er, w_gate, w_up, w_down):
    shp = x.shape
    xt = x.reshape(-1, D_MODEL)
    g_logits = (xt @ w_gr + b_gr).astype(jnp.float32)
    g_prob = jax.nn.softmax(g_logits, axis=-1)
    g_idx = jnp.argmax(g_logits, axis=-1)
    g_p = jnp.take_along_axis(g_prob, g_idx[:, None], axis=-1)
    e_all = (jnp.einsum('td,dge->tge', xt, w_er) + b_er).astype(jnp.float32)
    e_logits = jnp.take_along_axis(e_all, g_idx[:, None, None], axis=1)[:, 0]
    top_p, top_i = lax.top_k(jax.nn.softmax(e_logits, axis=-1), TOP_K)
    wts = g_p * top_p / jnp.sum(top_p, axis=-1, keepdims=True)
    eid = g_idx[:, None] * EXPERTS_PER_GROUP + top_i
    gates = jnp.sum(jax.nn.one_hot(eid, N_EXPERTS, dtype=jnp.float32) * wts[..., None], axis=1).astype(x.dtype)
    hg = jnp.einsum('td,edf->tef', xt, w_gate)
    hu = jnp.einsum('td,edf->tef', xt, w_up)
    act = jax.nn.silu(hg) * hu * gates[..., None]
    return jnp.einsum('tef,efd->td', act, w_down).reshape(shp)

def layer(x, c, p, table, kv_cache=None, h0=None):
    bsz, l = x.shape[:2]
    mod = (jax.nn.silu(c) @ p['w_ada'] + p['b_ada'])[:, None, :]
    sh1, sc1, gt1, sh2, sc2, gt2 = jnp.split(mod, N_MOD, axis=-1)
    hn = rms_norm(x, p['g_pre_mix']) * (1.0 + sc1) + sh1
    proj = hn @ p['w_in']
    u, q, k, v = jnp.split(proj, [SSM_WIDTH, SSM_WIDTH + ATTN_WIDTH, SSM_WIDTH + ATTN_WIDTH + KV_WIDTH], axis=-1)
    q = q.reshape(bsz, l, N_KV_HEADS, GQA, HEAD_DIM)
    k = k.reshape(bsz, l, N_KV_HEADS, HEAD_DIM)
    v = v.reshape(bsz, l, N_KV_HEADS, HEAD_DIM)
    if kv_cache is None:
        attn, k_st, v_st = attn_prompt(q, k, v, p['attn_sinks'], table)
        ssm_y, h_last = s5_scan(u, p['ssm_lam_re'], p['ssm_lam_im'], p['ssm_log_dt'], p['ssm_b_re'], p['ssm_b_im'],
                                p['ssm_c_re'], p['ssm_c_im'], p['ssm_d'])
    else:
        attn, k_st, v_st = attn_sample(q, k, v, kv_cache[0], kv_cache[1], p['attn_sinks'], table)
        ssm_y, h_last = s5_scan(u, p['ssm_lam_re'], p['ssm_lam_im'], p['ssm_log_dt'], p['ssm_b_re'], p['ssm_b_im'],
                                p['ssm_c_re'], p['ssm_c_im'], p['ssm_d'], h0[0], h0[1])
    z = jax.nn.gelu(ssm_y)
    ssm_out = z * jax.nn.sigmoid(z @ p['w_glu'] + p['b_glu'])
    mixed = jnp.concatenate([rms_norm(ssm_out, p['g_ssm_out']), rms_norm(attn, p['g_attn_out'])], axis=-1) @ p['w_out']
    x = x + gt1 * rms_norm(mixed, p['g_post_mix'])
    hn2 = rms_norm(x, p['g_pre_ffn']) * (1.0 + sc2) + sh2
    ffn = hier_moe(hn2, p['w_group_router'], p['b_group_router'], p['w_expert_router'], p['b_expert_router'],
                   p['w_exp_gate'], p['w_exp_up'], p['w_exp_down'])
    x = x + gt2 * rms_norm(ffn, p['g_post_ffn'])
    return x, k_st, v_st, h_last.real.astype(x.dtype), h_last.imag.astype(x.dtype)

def setup_inputs(seed: int = 0) -> dict:
    key = jax.random.key(seed)
    ks = iter(jax.random.split(key, 48))

    def nrm(shape, scale):
        return jax.random.normal(next(ks), shape, jnp.float32) * scale

    wbuf = min(WINDOW, PAST_LEN)
    lam_im = jnp.broadcast_to(jnp.pi * jnp.arange(SSM_STATE, dtype=jnp.float32), (DEPTH, N_SSM_GROUPS, SSM_STATE))
    return {
        'x_prompt': nrm((BATCH, SEQ, D_MODEL), 1.0),
        'x_sample': nrm((DEC_BATCH, DEC_SEQ, D_MODEL), 1.0),
        'cache_k': nrm((DEPTH, DEC_BATCH, wbuf, N_KV_HEADS, HEAD_DIM), 1.0),
        'cache_v': nrm((DEPTH, DEC_BATCH, wbuf, N_KV_HEADS, HEAD_DIM), 1.0),
        'state_ssm_re': nrm((DEPTH, DEC_BATCH, N_SSM_GROUPS, SSM_STATE), 0.3),
        'state_ssm_im': nrm((DEPTH, DEC_BATCH, N_SSM_GROUPS, SSM_STATE), 0.3),
        'c_prompt': nrm((BATCH, D_MODEL), 1.0),
        'c_sample': nrm((DEC_BATCH, D_MODEL), 1.0),
        'rel_bias_table': nrm((NUM_BUCKETS, N_HEADS), 0.5),
        'w_ada': nrm((DEPTH, D_MODEL, N_MOD * D_MODEL), 0.5 * D_MODEL ** -0.5),
        'b_ada': nrm((DEPTH, N_MOD * D_MODEL), 0.02),
        'g_pre_mix': 1.0 + nrm((DEPTH, D_MODEL), 0.05),
        'g_post_mix': 1.0 + nrm((DEPTH, D_MODEL), 0.05),
        'g_pre_ffn': 1.0 + nrm((DEPTH, D_MODEL), 0.05),
        'g_post_ffn': 1.0 + nrm((DEPTH, D_MODEL), 0.05),
        'w_in': nrm((DEPTH, D_MODEL, IN_WIDTH), D_MODEL ** -0.5),
        'ssm_lam_re': -0.5 + nrm((DEPTH, N_SSM_GROUPS, SSM_STATE), 0.01),
        'ssm_lam_im': lam_im + nrm((DEPTH, N_SSM_GROUPS, SSM_STATE), 0.01),
        'ssm_log_dt': jax.random.uniform(next(ks), (DEPTH, N_SSM_GROUPS), jnp.float32, math.log(1e-3), math.log(1e-1)),
        'ssm_b_re': nrm((DEPTH, N_SSM_GROUPS, SSM_STATE, SSM_GROUP), (2 * SSM_GROUP) ** -0.5),
        'ssm_b_im': nrm((DEPTH, N_SSM_GROUPS, SSM_STATE, SSM_GROUP), (2 * SSM_GROUP) ** -0.5),
        'ssm_c_re': nrm((DEPTH, N_SSM_GROUPS, SSM_GROUP, SSM_STATE), (2 * SSM_STATE) ** -0.5),
        'ssm_c_im': nrm((DEPTH, N_SSM_GROUPS, SSM_GROUP, SSM_STATE), (2 * SSM_STATE) ** -0.5),
        'ssm_d': nrm((DEPTH, SSM_WIDTH), 0.5),
        'w_glu': nrm((DEPTH, SSM_WIDTH, SSM_WIDTH), SSM_WIDTH ** -0.5),
        'b_glu': nrm((DEPTH, SSM_WIDTH), 0.02),
        'attn_sinks': nrm((DEPTH, N_HEADS), 0.5),
        'g_ssm_out': 1.0 + nrm((DEPTH, SSM_WIDTH), 0.05),
        'g_attn_out': 1.0 + nrm((DEPTH, ATTN_WIDTH), 0.05),
        'w_out': nrm((DEPTH, D_MODEL, D_MODEL), D_MODEL ** -0.5),
        'w_group_router': nrm((DEPTH, D_MODEL, N_EXPERT_GROUPS), D_MODEL ** -0.5),
        'b_group_router': nrm((DEPTH, N_EXPERT_GROUPS), 0.01),
        'w_expert_router': nrm((DEPTH, D_MODEL, N_EXPERT_GROUPS, EXPERTS_PER_GROUP), D_MODEL ** -0.5),
        'b_expert_router': nrm((DEPTH, N_EXPERT_GROUPS, EXPERTS_PER_GROUP), 0.01),
        'w_exp_gate': nrm((DEPTH, N_EXPERTS, D_MODEL, D_EXPERT), D_MODEL ** -0.5),
        'w_exp_up': nrm((DEPTH, N_EXPERTS, D_MODEL, D_EXPERT), D_MODEL ** -0.5),
        'w_exp_down': nrm((DEPTH, N_EXPERTS, D_EXPERT, D_MODEL), D_EXPERT ** -0.5),
    }

def reference(x_prompt, x_sample, cache_k, cache_v, state_ssm_re, state_ssm_im, c_prompt, c_sample,
              rel_bias_table, w_ada, b_ada, g_pre_mix, g_post_mix, g_pre_ffn, g_post_ffn, w_in,
              ssm_lam_re, ssm_lam_im, ssm_log_dt, ssm_b_re, ssm_b_im, ssm_c_re, ssm_c_im, ssm_d,
              w_glu, b_glu, attn_sinks, g_ssm_out, g_attn_out, w_out,
              w_group_router, b_group_router, w_expert_router, b_expert_router,
              w_exp_gate, w_exp_up, w_exp_down):
    yp, ys = x_prompt, x_sample
    kp, vp, hrp, hip, ksl, vsl, hrs, his = [], [], [], [], [], [], [], []
    for li in range(DEPTH):
        p = {
            'w_ada': w_ada[li], 'b_ada': b_ada[li],
            'g_pre_mix': g_pre_mix[li], 'g_post_mix': g_post_mix[li],
            'g_pre_ffn': g_pre_ffn[li], 'g_post_ffn': g_post_ffn[li],
            'w_in': w_in[li],
            'ssm_lam_re': ssm_lam_re[li], 'ssm_lam_im': ssm_lam_im[li], 'ssm_log_dt': ssm_log_dt[li],
            'ssm_b_re': ssm_b_re[li], 'ssm_b_im': ssm_b_im[li],
            'ssm_c_re': ssm_c_re[li], 'ssm_c_im': ssm_c_im[li], 'ssm_d': ssm_d[li],
            'w_glu': w_glu[li], 'b_glu': b_glu[li], 'attn_sinks': attn_sinks[li],
            'g_ssm_out': g_ssm_out[li], 'g_attn_out': g_attn_out[li], 'w_out': w_out[li],
            'w_group_router': w_group_router[li], 'b_group_router': b_group_router[li],
            'w_expert_router': w_expert_router[li], 'b_expert_router': b_expert_router[li],
            'w_exp_gate': w_exp_gate[li], 'w_exp_up': w_exp_up[li], 'w_exp_down': w_exp_down[li],
        }
        yp, k1, v1, r1, i1 = layer(yp, c_prompt, p, rel_bias_table)
        ys, k2, v2, r2, i2 = layer(ys, c_sample, p, rel_bias_table,
                                   (cache_k[li], cache_v[li]), (state_ssm_re[li], state_ssm_im[li]))
        kp.append(k1); vp.append(v1); hrp.append(r1); hip.append(i1)
        ksl.append(k2); vsl.append(v2); hrs.append(r2); his.append(i2)
    return (yp, ys, jnp.stack(kp), jnp.stack(vp), jnp.stack(hrp), jnp.stack(hip),
            jnp.stack(ksl), jnp.stack(vsl), jnp.stack(hrs), jnp.stack(his))


_drawn_inputs = setup_inputs


def setup_inputs(seed=0):
    import zlib

    import numpy as np

    out = dict(_drawn_inputs(seed))
    spreads = {}
    factors = {'g_post_ffn': 4.056,
     'ssm_lam_re': 3.645,
     'b_glu': 3.89,
     'attn_sinks': 5.161,
     'b_expert_router': 3.533}
    for name, (base, spread) in spreads.items():
        noise = np.random.default_rng([zlib.crc32(name.encode()), seed]).standard_normal(out[name].shape)
        drawn = base * np.exp(spread * noise) if base else spread * noise
        out[name] = __import__('jax').numpy.asarray(drawn.astype(out[name].dtype))
    for name, factor in factors.items():
        out[name] = (out[name] * factor).astype(out[name].dtype)
    return out
```

```python
import math
from contextlib import ExitStack
import numpy as np
import concourse.bass as bass
from concourse import mybir

F32 = mybir.dt.float32
F32R = mybir.dt.float32r
I32 = mybir.dt.int32
U32 = mybir.dt.uint32
ALU = mybir.AluOpType
ACT = mybir.ActivationFunctionType
AX = mybir.AxisListType

P = 128
D = 1024
KD = D // P
SEQ = 2048
DB, DT = 8, 8
NS = DB * DT
NPT = SEQ // P
NT = NPT + 1
TOK = NT * P
SW = 512
AW = 512
KVW = 128
INW = SW + AW + 2 * KVW
HD = 64
NG, GC, NST = 32, 16, 64
L = 8
NCH = SEQ // L
WIN = 128
NBUCKET = 32
NH, NKV, GQ = 8, 2, 4
NE, EPG, NEG_ = 16, 4, 4
DE = 256
EPS = 1e-6
MASKED = -1e30


class Semaphores:

    def __init__(self, nc):
        self.nc, self.held = nc, []

    def __enter__(self):
        return self

    def get(self, name):
        self.held.append(self.nc.alloc_semaphore(name=name))
        return self.held[-1]

    def __exit__(self, *a):
        self.nc.all_engine_barrier()
        self.nc.clear_and_free_semaphores(self.held)
        self.nc.all_engine_barrier()


class Stage:

    def __init__(self, nc, top, tag):
        self.nc, self.top, self.tag, self.stack = nc, top, tag, ExitStack()

    def __enter__(self):
        return self

    def __exit__(self, *a):
        self.stack.close()

    def sb(self, name, shape, dt=F32):
        return self.stack.enter_context(self.nc.sbuf_tensor(f"{self.tag}_{name}", shape, dt))

    def ps(self, name, shape, dt=F32):
        return self.stack.enter_context(self.nc.psum_tensor(f"{self.tag}_{name}", shape, dt))

    def sem(self, name):
        return self.top.get(f"{self.tag}_{name}")

    def block(self):
        return self.stack.enter_context(self.nc.Block())


class Steps:

    def __init__(self, eng, sem):
        self.eng, self.sem, self.base, self.n = eng, sem, 0, 0

    def then(self, ins):
        ins.then_inc(self.sem, 1)
        self.n += 1
        self.eng.wait_ge(self.sem, self.base + self.n)

    def start(self, base):
        self.base, self.n = base, 0


def modulation(nc, T, top):
    NR = 1 + DB
    NCK = 6 * D // 512
    with Stage(nc, top, "mod") as s:
        c_in, c_act = s.sb("c_in", [NR, D]), s.sb("c_act", [NR, D])
        cT = s.sb("cT", [P, KD, NR])
        ident = s.sb("ident", [P, P])
        w = s.sb("w", [P, 2, KD, 512])
        bias, gains = s.sb("bias", [NR, 6 * D]), s.sb("gains", [NR, 4, D])
        mod, res = s.sb("mod", [NR, 6 * D]), s.sb("res", [NR, 6, D])
        ps_t, ps_m = s.ps("ps_t", [P, KD, 16]), s.ps("ps_m", [P, 2, 512])
        c_loaded, consts_loaded, c_ready = s.sem("c_loaded"), s.sem("consts"), s.sem("c_ready")
        t_done, cT_ready = s.sem("t_done"), s.sem("cT_ready")
        w_even, w_odd, w_free = s.sem("w_even"), s.sem("w_odd"), s.sem("w_free")
        mm_done, ps_free, mod_done = s.sem("mm_done"), s.sem("ps_free"), s.sem("mod_done")
        folded, stored = s.sem("folded"), s.sem("stored")
        blk = s.block()
        wv = T["w_ada"].rearrange("a (k p) n -> p (a k) n", p=P)

        @blk.sync
        def _(sp):
            sp.dma_start(c_in[0:1, :], T["c_prompt"]).then_inc(c_loaded, 16)
            sp.dma_start(c_in[1:NR, :], T["c_sample"]).then_inc(c_loaded, 16)
            sp.dma_start(ident[:, :], T["ident"]).then_inc(c_loaded, 16)
            with sp.Fori(0, NCK // 2) as i:
                for par, arrived in ((0, w_even), (1, w_odd)):
                    sp.wait_ge(w_free, i * 2 + par + 1)
                    sp.dma_start(w[:, par, :, :], wv[:, :, bass.ds((i * 2 + par) * 512, 512)]).then_inc(arrived, 16)
            sp.wait_ge(folded, 6)
            sp.dma_start(T["mods"], res[:, :, :]).then_inc(stored, 16)
            sp.wait_ge(stored, 16)

        @blk.gpsimd
        def _(pool):
            pool.dma_start(bias[:, :], T["b_ada"].partition_broadcast(NR)).then_inc(consts_loaded, 16)
            for n, name in enumerate(("g_pre_mix", "g_post_mix", "g_pre_ffn", "g_post_ffn")):
                pool.dma_start(gains[:, n, :], T[name].partition_broadcast(NR)).then_inc(consts_loaded, 16)

        @blk.scalar
        def _(act):
            act.wait_ge(c_loaded, 48)
            nc.scalar.activation(c_act[:, :], c_in[:, :], ACT.Silu).then_inc(c_ready, 1)

        @blk.tensor
        def _(pe):
            pe.sem_inc(w_free, 2)
            pe.wait_ge(c_ready, 1)
            for k in range(KD):
                last = nc.tensor.transpose(ps_t[:, k, 0:NR], c_act[:, k * P:(k + 1) * P], ident[0:NR, 0:NR])
            last.then_inc(t_done, 1)
            pe.wait_ge(cT_ready, 1)
            with pe.Fori(0, NCK // 2) as i:
                for par, arrived in ((0, w_even), (1, w_odd)):
                    pe.wait_ge(arrived, i * 16 + 16)
                    pe.wait_ge(ps_free, i * 2 + par + 1)
                    for k in range(KD):
                        last = nc.tensor.matmul(ps_m[0:NR, par, :], cT[:, k, :], w[:, par, k, :],
                                                start=(k == 0), stop=(k == KD - 1))
                    last.then_inc(mm_done, 1)
                    pe.wait_ge(mm_done, i * 2 + par + 1)
                    pe.sem_inc(w_free, 1)

        @blk.vector
        def _(dve):
            dve.sem_inc(ps_free, 2)
            dve.wait_ge(t_done, 1)
            nc.vector.tensor_copy(cT[:, :, :], ps_t[:, :, 0:NR]).then_inc(cT_ready, 1)
            dve.wait_ge(consts_loaded, 80)
            with dve.Fori(0, NCK // 2) as i:
                for par in range(2):
                    at = bass.ds((i * 2 + par) * 512, 512)
                    dve.wait_ge(mm_done, i * 2 + par + 1)
                    nc.vector.tensor_tensor(mod[:, at], ps_m[0:NR, par, :], bias[:, at], ALU.add).then_inc(mod_done, 1)
                    dve.wait_ge(mod_done, i * 2 + par + 1)
                    dve.sem_inc(ps_free, 1)
            for h in range(2):
                sh, sc, gt = (mod[:, (3 * h + j) * D:(3 * h + j + 1) * D] for j in range(3))
                nc.vector.scalar_tensor_tensor(res[:, 3 * h, :], sc, 1.0, gains[:, 2 * h, :],
                                               ALU.add, ALU.mult).then_inc(folded, 1)
                nc.vector.tensor_copy(res[:, 3 * h + 1, :], sh).then_inc(folded, 1)
                nc.vector.tensor_tensor(res[:, 3 * h + 2, :], gt, gains[:, 2 * h + 1, :], ALU.mult).then_inc(folded, 1)


def mod_row(T, row, r=0, n=P):
    return T["mods"][r, row, :].partition_broadcast(n)


def load_sample_mod(eng, T, dst, row, arrived):
    for b in range(2 * DB):
        eng.dma_start(dst[b * DT:(b + 1) * DT, :], mod_row(T, row, 1 + b % DB, DT)).then_inc(arrived, 16)
    return 2 * DB * 16


def projection(nc, T, top):
    with Stage(nc, top, "pj") as s:
        x, hn, hnT = s.sb("x", [P, 2, D]), s.sb("hn", [P, 2, D]), s.sb("hnT", [P, 2, KD, P])
        proj, sq = s.sb("proj", [P, 2, INW]), s.sb("sq", [P, 2, D])
        w = s.sb("w", [P, KD, INW])
        mod = s.sb("mod", [P, 2, 2, D])
        ident = s.sb("ident", [P, P])
        st = s.sb("st", [P, 2, 4])
        ps_t, ps_m = s.ps("ps_t", [P, 2, 512]), s.ps("ps_m", [P, 3, 512])
        w_in, mods_in, smods_in = s.sem("w_in"), s.sem("mods_in"), s.sem("smods_in")
        x_even, x_odd, x_free = s.sem("x_even"), s.sem("x_odd"), s.sem("x_free")
        squared, meaned, rooted, rstd_ready = s.sem("squared"), s.sem("meaned"), s.sem("rooted"), s.sem("rstd")
        hn_ready, t_done, moved_a, moved_v = s.sem("hn_ready"), s.sem("t_done"), s.sem("moved_a"), s.sem("moved_v")
        mm_done, out_a, out_v = s.sem("mm_done"), s.sem("out_a"), s.sem("out_v")
        st_even, st_odd = s.sem("st_even"), s.sem("st_odd")
        blk = s.block()
        cols = ((0, 512), (512, 512), (1024, 256))
        xp = T["x_prompt"].rearrange("a (n p) d -> p (a n) d", p=P)
        xs = T["x_sample"].rearrange("b t d -> (b t) d")
        pv = T["proj"].rearrange("(n p) d -> p n d", p=P)
        HALF = NPT // 2

        @blk.sync
        def _(sp):
            def load_x(t, par, arrived):
                sp.wait_ge(x_free, t + 1)
                sp.dma_start(x[:, par, :].unsqueeze(1), xp[:, bass.ds(t, 1), :]).then_inc(arrived, 16)

            def store(t, par, stored):
                sp.wait_ge(out_v, t * 2 + 4)
                sp.wait_ge(out_a, t + 2)
                sp.dma_start(pv[:, bass.ds(t, 1), :], proj[:, par, :].unsqueeze(1)).then_inc(stored, 16)

            sp.sem_inc(st_even, 16)
            sp.sem_inc(st_odd, 16)
            load_x(0, 0, x_even)
            sp.dma_start(ident[:, :], T["ident"]).then_inc(mods_in, 16)
            for r in range(2):
                sp.dma_start(mod[:, 0, r, :], mod_row(T, r)).then_inc(mods_in, 16)
            load_x(1, 1, x_odd)
            for k in range(KD):
                src = T["w_in"][0, k * P:(k + 1) * P, :]
                q_in, q_at = (a[:, SW:SW + AW] for a in (src, w[:, k, :]))
                sp.dma_start(w[:, k, 0:SW], src[:, 0:SW]).then_inc(w_in, 16)
                for kv in range(NKV):
                    sp.dma_start(q_at.rearrange("p (g k d) -> p g k d", g=GQ, k=NKV)[:, :, kv, :],
                                 q_in.rearrange("p (k g d) -> p g k d", g=GQ, k=NKV)[:, :, kv, :]).then_inc(w_in, 16)
                sp.dma_start(w[:, k, SW + AW:], src[:, SW + AW:]).then_inc(w_in, 16)
            with sp.Fori(0, HALF - 1) as i:
                for par, arrived, stored in ((0, x_even, st_even), (1, x_odd, st_odd)):
                    load_x(i * 2 + par + 2, par, arrived)
                    store(i * 2 + par, par, stored)
            sp.wait_ge(x_free, NPT + 1)
            for h in range(2):
                sp.dma_start(x[h * NS:(h + 1) * NS, 0, :], xs).then_inc(x_even, 16)
            store(NPT - 2, 0, st_even)
            store(NPT - 1, 1, st_odd)
            store(NPT, 0, st_even)
            sp.wait_ge(st_even, (HALF + 2) * 16)
            sp.wait_ge(st_odd, (HALF + 1) * 16)

        @blk.gpsimd
        def _(pool):
            for r in range(2):
                load_sample_mod(pool, T, mod[:, 1, r, :], r, smods_in)
        @blk.scalar
        def _(act):
            act.sem_inc(out_a, 1)

            def norm(t, par, arrived, n):
                act.wait_ge(arrived, n)
                nc.scalar.activation(sq[:, par, :], x[:, par, :], ACT.Square, accum_out=st[:, par, 0:1]).then_inc(squared, 1)
                act.wait_ge(meaned, t + 1)
                nc.scalar.activation(st[:, par, 2:3], st[:, par, 1:2], ACT.Sqrt).then_inc(rooted, 1)

            def move(t, par):
                act.wait_ge(t_done, t + 1)
                act.wait_ge(mm_done, t * 3)
                nc.scalar.activation(hnT[:, par, 0:4, :], ps_t[:, 0, :].rearrange("p (k n) -> p k n", k=4),
                                     ACT.Copy).then_inc(moved_a, 1)

            def out(t, par, stored, n):
                act.wait_ge(mm_done, t * 3 + 4)
                act.wait_ge(stored, n)
                nc.scalar.activation(proj[:, par, 0:512], ps_m[:, 0, :], ACT.Copy).then_inc(out_a, 1)

            norm(0, 0, x_even, 16)
            move(0, 0)
            norm(1, 1, x_odd, 16)
            with act.Fori(0, HALF - 1) as i:
                for par, arrived, stored in ((0, x_even, st_even), (1, x_odd, st_odd)):
                    move(i * 2 + par + 1, 1 - par)
                    norm(i * 2 + par + 2, par, arrived, i * 16 + 32)
                    out(i * 2 + par, par, stored, i * 16 + 16)
            move(NPT - 1, 1)
            norm(NPT, 0, x_even, (HALF + 2) * 16)
            out(NPT - 2, 0, st_even, HALF * 16)
            move(NPT, 0)
            out(NPT - 1, 1, st_odd, HALF * 16)
            out(NPT, 0, st_even, (HALF + 1) * 16)

        @blk.vector
        def _(dve):
            dve.sem_inc(x_free, 2)
            dve.sem_inc(out_v, 2)

            def norm(t, par, kind):
                dve.wait_ge(squared, t + 1)
                nc.vector.tensor_scalar(st[:, par, 1:2], st[:, par, 0:1], 1.0 / D, EPS, ALU.mult, ALU.add).then_inc(meaned, 1)
                dve.wait_ge(rooted, t + 1)
                nc.vector.reciprocal(st[:, par, 3:4], st[:, par, 2:3]).then_inc(rstd_ready, 1)
                dve.wait_ge(rstd_ready, t + 1)
                nc.vector.scalar_tensor_tensor(hn[:, par, :], x[:, par, :], st[:, par, 3:4], mod[:, kind, 0, :],
                                               ALU.mult, ALU.mult).then_inc(x_free, 1)
                dve.wait_ge(x_free, t + 3)
                nc.vector.tensor_tensor(hn[:, par, :], hn[:, par, :], mod[:, kind, 1, :], ALU.add).then_inc(hn_ready, 1)

            def move(t, par):
                dve.wait_ge(t_done, t + 1)
                dve.wait_ge(mm_done, t * 3)
                nc.vector.tensor_copy(hnT[:, par, 4:8, :], ps_t[:, 1, :].rearrange("p (k n) -> p k n", k=4)).then_inc(moved_v, 1)

            def out(t, par, stored, n):
                dve.wait_ge(stored, n)
                for c in (1, 2):
                    dve.wait_ge(mm_done, t * 3 + 4 + c)
                    nc.vector.tensor_copy(proj[:, par, cols[c][0]:cols[c][0] + cols[c][1]],
                                          ps_m[:, c, 0:cols[c][1]]).then_inc(out_v, 1)

            dve.wait_ge(mods_in, 48)
            norm(0, 0, 0)
            move(0, 0)
            norm(1, 1, 0)
            with dve.Fori(0, HALF - 1) as i:
                for par, stored in ((0, st_even), (1, st_odd)):
                    move(i * 2 + par + 1, 1 - par)
                    norm(i * 2 + par + 2, par, 0)
                    out(i * 2 + par, par, stored, i * 16 + 16)
            move(NPT - 1, 1)
            dve.wait_ge(smods_in, 4 * DB * 16)
            norm(NPT, 0, 1)
            out(NPT - 2, 0, st_even, HALF * 16)
            move(NPT, 0)
            out(NPT - 1, 1, st_odd, HALF * 16)
            out(NPT, 0, st_even, (HALF + 1) * 16)

        @blk.tensor
        def _(pe):
            def flip(t, par):
                pe.wait_ge(hn_ready, t + 1)
                if not (isinstance(t, int) and t == 0):
                    pe.wait_ge(moved_a, t)
                    pe.wait_ge(moved_v, t)
                for k in range(KD):
                    last = nc.tensor.transpose(ps_t[:, k // 4, k % 4 * P:(k % 4 + 1) * P],
                                               hn[:, par, k * P:(k + 1) * P], ident[:, :])
                last.then_inc(t_done, 1)

            def product(t, par):
                pe.wait_ge(moved_a, t + 1)
                pe.wait_ge(moved_v, t + 1)
                for c, (c0, n) in enumerate(cols):
                    pe.wait_ge(*((out_a, t + 1) if c == 0 else (out_v, t * 2 + c)))
                    for k in range(KD):
                        last = nc.tensor.matmul(ps_m[:, c, 0:n], hnT[:, par, k, :], w[:, k, c0:c0 + n],
                                                start=(k == 0), stop=(k == KD - 1))
                    last.then_inc(mm_done, 1)

            pe.sem_inc(mm_done, 3)
            pe.wait_ge(mods_in, 48)
            flip(0, 0)
            pe.wait_ge(w_in, 4 * KD * 16)
            with pe.Fori(0, HALF) as i:
                for par in range(2):
                    flip(i * 2 + par + 1, 1 - par)
                    product(i * 2 + par, par)
            product(NPT, 0)


REC = {}
_at = 0
for _n, _w in (("N", 192), ("T", 128), ("M", 128), ("MS", 128), ("COS", NCH), ("SIN", NCH), ("H0", DB)):
    REC[_n] = (_at, _w)
    _at += _w
RECW = _at + (-_at) % 8

LN2_HI, MAGIC = 0.693359375, 12582912.0
LN2_LO = math.log(2.0) - LN2_HI
TAU = 2.0 * math.pi
TAU_1 = 6.28125
TAU_2 = float(np.float16(TAU - TAU_1))
TAU_3 = TAU - TAU_1 - TAU_2
PI_BELOW = 3.1415925


def s5_tables(nc, T, top):
    with Stage(nc, top, "st") as s:
        ident = s.sb("ident", [P, P])
        lam_in = s.sb("lam_in", [NG, 2, 2, NST])
        d_in, d_rep = s.sb("d_in", [NG, GC]), s.sb("d_rep", [NG, L, GC])
        c_in = s.sb("c_in", [P, 2, 4, 2, NST])
        h_in = s.sb("h_in", [P, 2, 2, 2, NST])
        sgn = s.sb("sgn", [P, 1])
        v = s.sb("v", [P, 40, NG])
        vi = s.sb("vi", [P, NG], I32)
        Bm, Cm = s.sb("Bm", [P, 2, NG, GC]), s.sb("Cm", [P, 2, NG, GC])
        Bb = s.sb("Bb", [P, 2, NG, GC])
        pw = s.sb("pw", [P, 2, L + 1, NG])
        PP, QQ = s.sb("PP", [P, L + 1, NG]), s.sb("QQ", [P, L + 1, NG])
        t1, t2, t3, t4 = (s.sb(f"t{n}", [P, 2048]) for n in range(1, 5))
        CL, CM = s.sb("CL", [P, NG, L + 1, GC]), s.sb("CM", [P, NG, L, GC])
        NB = s.sb("NB", [P, NG, L, GC])
        N3, TT = s.sb("N3", [P, NG, 192]), s.sb("TT", [P, NG, P])
        kq = s.sb("kq", [GC, NG, P])
        E1, E16 = s.sb("E1", [P, 2, NG, 16]), s.sb("E16", [P, 2, NG, 16])
        cosq, sinq = s.sb("cosq", [P, 8, NCH]), s.sb("sinq", [P, 8, NCH])
        h0, hpre = s.sb("h0", [P, 2, DB, NG]), s.sb("hpre", [P, DB, NG])
        hs = s.sb("hs", [P, NG, DB])
        ps_a, ps_c = s.ps("ps_a", [P, 512]), s.ps("ps_c", [P, 2, 4, P])
        ps_h, ps_n, ps_k = s.ps("ps_h", [P, 2, 2, P]), s.ps("ps_n", [P, 2, 512]), s.ps("ps_k", [P, 2, 512])
        params, bc_in, flipped, sins, mats = s.sem("params"), s.sem("bc_in"), s.sem("flipped"), s.sem("sins"), s.sem("mats")
        reduced = s.sem("reduced")
        step, kq_mm, kq_out, kq_moved = s.sem("step"), s.sem("kq_mm"), s.sem("kq_out"), s.sem("kq_moved")
        n_mm, n_out, tables = s.sem("n_mm"), s.sem("n_out"), s.sem("tables")
        e_ready, cos_ready, sin_ready, pstep = s.sem("e_ready"), s.sem("cos_ready"), s.sem("sin_ready"), s.sem("pstep")
        h0_ready, t_ready, hpre_ready = s.sem("h0_ready"), s.sem("t_ready"), s.sem("hpre_ready")
        cs_even, stored, rec_out = s.sem("cs_even"), s.sem("stored"), s.sem("rec_out")
        tt_zero, d_ready, d_copied = s.sem("tt_zero"), s.sem("d_ready"), s.sem("d_copied")
        blk = s.block()
        slots = {}

        def V(name):
            return v[:, slots.setdefault(name, len(slots)), :]

        rec = T["rec"].rearrange("g q w -> q g w")

        def rec_cols(name):
            a, w = REC[name]
            return rec[:, :, a:a + w]

        @blk.sync
        def _(sp):
            sp.dma_start(ident[:, :], T["ident"]).then_inc(params, 16)
            sp.dma_start(sgn[:, :], T["sgn"]).then_inc(params, 16)
            for h in range(2):
                sp.dma_start(lam_in[:, 0, h, :], T["ssm_lam_re"][0]).then_inc(params, 16)
                sp.dma_start(lam_in[:, 1, h, :], T["ssm_lam_im"][0]).then_inc(params, 16)
            sp.dma_start(V("logdt"), T["ssm_log_dt"][0, :].partition_broadcast(P)).then_inc(params, 16)
            sp.dma_start(d_in[:, :], T["ssm_d"].rearrange("a (g c) -> (a g) c", g=NG)).then_inc(params, 16)
            for r, name in enumerate(("ssm_c_re", "ssm_c_im")):
                cv = T[name].rearrange("a (n g) c p -> (g c) (a n) p", n=4)
                for h in range(2):
                    sp.dma_start(c_in[:, r, :, h, :], cv).then_inc(params, 16)
            for r, name in enumerate(("state_ssm_re", "state_ssm_im")):
                hv = T[name].rearrange("a (n b) g p -> (b g) (a n) p", n=2)
                for x in range(2):
                    sp.dma_start(h_in[:, :, x, r ^ x, :], hv).then_inc(params, 16)
            sp.wait_ge(kq_out, 8)
            sp.wait_ge(tt_zero, 1)
            for j in range(L):
                sp.dma_start(TT[j * GC:(j + 1) * GC, :, j * GC:], kq[:, :, 0:P - j * GC]).then_inc(kq_moved, 16)
            sp.wait_ge(n_out, 16)
            sp.dma_start(rec_cols("N"), N3[:, :, :]).then_inc(rec_out, 16)
            sp.wait_ge(t_ready, 1)
            sp.dma_start(rec_cols("T"), TT[:, :, :]).then_inc(rec_out, 16)
            sp.dma_start(rec_cols("M"), CL[:, :, 1:, :].rearrange("q g t c -> q g (t c)")).then_inc(rec_out, 16)
            sp.dma_start(rec_cols("MS"), CM[:, :, :, :].rearrange("q g t c -> q g (t c)")).then_inc(rec_out, 16)
            sp.wait_ge(hpre_ready, 2)
            sp.dma_start(rec_cols("H0"), hs[:, :, :]).then_inc(rec_out, 16)
            sp.dma_start(T["r8"], V("r8")).then_inc(rec_out, 16)
            sp.dma_start(T["hpre"], hpre[:, :, :].rearrange("q b g -> q (b g)")).then_inc(rec_out, 16)
            a, b = REC["COS"][0], REC["SIN"][0]
            for n in range(4):
                gs = slice(n * 8, n * 8 + 8)
                sp.wait_ge(cos_ready, n + 1)
                sp.dma_start(rec[:, gs, a:a + NCH], cosq[:, :, :]).then_inc(cs_even, 16)
                sp.wait_ge(sin_ready, n + 1)
                sp.dma_start(rec[:, gs, b:b + NCH], sinq[:, :, :]).then_inc(stored, 16)
            sp.wait_ge(cs_even, 64)
            sp.wait_ge(stored, 64)
            sp.wait_ge(rec_out, 7 * 16)

        @blk.gpsimd
        def _(pool):
            nc.gpsimd.memset(TT[:, :, :], 0.0).then_inc(tt_zero, 1)
            for r, name in enumerate(("ssm_b_re", "ssm_b_im")):
                bv = T[name].rearrange("a g p c -> p (a g) c")
                for h in range(2):
                    pool.dma_start(Bm[h * NST:(h + 1) * NST, r, :, :], bv).then_inc(bc_in, 16)
            pool.wait_ge(e_ready, 1)
            st_ = Steps(pool, pstep)
            for n in range(4):
                gs = slice(n * 8, n * 8 + 8)
                hi = [E16[:, r, gs, :].unsqueeze(3).broadcast_to([P, 8, 16, 16]) for r in range(2)]
                lo = [E1[:, r, gs, :].unsqueeze(2).broadcast_to([P, 8, 16, 16]) for r in range(2)]
                a, b = (t[:, :].rearrange("p (g a b) -> p g a b", g=8, a=16) for t in (t3, t4))
                if n:
                    pool.wait_ge(sin_ready, n)
                st_.then(nc.gpsimd.tensor_tensor(a, hi[0], lo[1], ALU.mult))
                st_.then(nc.gpsimd.tensor_tensor(b, hi[1], lo[0], ALU.mult))
                st_.then(nc.gpsimd.tensor_tensor(t3[:, :], t3[:, :], t4[:, :], ALU.add))
                if n:
                    pool.wait_ge(stored, n * 16)
                nc.gpsimd.tensor_scalar(sinq[:, :, :].rearrange("p g n -> p (g n)"), t3[:, :], sgn[:, 0:1], None,
                                        ALU.mult).then_inc(sin_ready, 1)

        @blk.scalar
        def _(act):
            act.wait_ge(reduced, 1)
            nc.scalar.activation(V("sin1"), V("red1"), ACT.Sin).then_inc(sins, 1)
            nc.scalar.activation(V("cos1"), V("cred1"), ACT.Sin).then_inc(sins, 1)
            nc.scalar.activation(V("sin8"), V("red8"), ACT.Sin).then_inc(sins, 1)
            nc.scalar.activation(V("cos8"), V("cred8"), ACT.Sin).then_inc(sins, 1)
            for g4 in range(8):
                act.wait_ge(n_mm, g4 + 1)
                src = ps_n[:, g4 % 2, :].rearrange("p (g n) -> p g n", g=4)
                gs = slice(g4 * 4, g4 * 4 + 4)
                nc.scalar.activation(N3[:, gs, 0:P], src, ACT.Copy).then_inc(n_out, 1)
                nc.scalar.activation(N3[:, gs, P:P + NST], src[:, :, 0:NST], ACT.Copy).then_inc(n_out, 1)
                act.wait_ge(kq_mm, g4 + 1)
                nc.scalar.activation(kq[:, gs, :], ps_k[0:GC, g4 % 2, :].rearrange("p (g n) -> p g n", g=4),
                                     ACT.Copy).then_inc(kq_out, 1)

        @blk.tensor
        def _(pe):
            pe.wait_ge(params, 16 * 16)
            for r in range(2):
                nc.tensor.transpose(ps_a[:, r * NG:(r + 1) * NG], lam_in[:, r, :, :].rearrange("g h p -> g (h p)"), ident[0:NG, 0:NG])
            pe.wait_ge(d_copied, 1)
            nc.tensor.transpose(ps_a[:, 2 * NG:3 * NG], d_rep[:, :, :].rearrange("g j c -> g (j c)"), ident[0:NG, 0:NG])
            for r in range(2):
                for n in range(4):
                    nc.tensor.transpose(ps_c[:, r, n, :], c_in[:, r, n, :, :].rearrange("q h p -> q (h p)"), ident[:, :])
            for n in range(2):
                for x in range(2):
                    last = nc.tensor.transpose(ps_h[:, n, x, :], h_in[:, n, x, :, :].rearrange("q h p -> q (h p)"), ident[:, :])
            last.then_inc(flipped, 1)
            pe.wait_ge(mats, 1)
            for g4 in range(8):
                if g4 >= 2:
                    pe.wait_ge(n_out, 2 * (g4 - 1))
                    pe.wait_ge(kq_out, g4 - 1)
                for n in range(4):
                    g = g4 * 4 + n
                    last = nc.tensor.transpose(ps_n[:, g4 % 2, n * P:(n + 1) * P], NB[:, g, :, :].rearrange("q j c -> q (j c)"), ident[:, :])
                last.then_inc(n_mm, 1)
                for n in range(4):
                    g = g4 * 4 + n
                    last = nc.tensor.matmul(ps_k[0:GC, g4 % 2, n * P:(n + 1) * P], NB[:, g, L - 1, :],
                                            CL[:, g, 0:L, :].rearrange("q t c -> q (t c)"), start=True, stop=True)
                last.then_inc(kq_mm, 1)

        @blk.vector
        def _(dve):
            st_ = Steps(dve, step)
            then = st_.then
            vec = nc.vector

            def ts(out, a, s1, s2, o1, o2):
                then(vec.tensor_scalar(out, a, s1, s2, o1, o2))

            def tt(out, a, b, op):
                then(vec.tensor_tensor(out, a, b, op))

            def stt(out, a, c, b, o1, o2):
                then(vec.scalar_tensor_tensor(out, a, c, b, o1, o2))

            def exp(out, x):
                k, f, p = V("k"), V("f"), V("p")
                ts(k, x, 1.0 / math.log(2.0), MAGIC, ALU.mult, ALU.add)
                ts(k, k, -MAGIC, -126.0, ALU.add, ALU.max)
                ts(k, k, 127.0, None, ALU.min, ALU.bypass)
                stt(f, k, -LN2_HI, x, ALU.mult, ALU.add)
                stt(f, k, -LN2_LO, f, ALU.mult, ALU.add)
                ts(p, f, 1.0 / 5040, 1.0 / 720, ALU.mult, ALU.add)
                tt(p, p, f, ALU.mult)
                for n in (5, 4, 3, 2, 1):
                    stt(p, p, 1.0 / math.factorial(n), f, ALU.add, ALU.mult)
                ts(k, k, 127.0, float(2 ** 23), ALU.add, ALU.mult)
                then(vec.tensor_copy(vi[:, :], k))
                stt(out, p, 1.0, vi[:, :].bitcast(F32), ALU.add, ALU.mult)

            def reduce_angle(name, a):
                n, r, c = V("k"), V("red" + name), V("cred" + name)
                ts(n, a, 1.0 / TAU, MAGIC, ALU.mult, ALU.add)
                ts(n, n, -MAGIC, None, ALU.add, ALU.bypass)
                stt(r, n, -TAU_1, a, ALU.mult, ALU.add)
                stt(r, n, -TAU_2, r, ALU.mult, ALU.add)
                stt(r, n, -TAU_3, r, ALU.mult, ALU.add)
                ts(r, r, PI_BELOW, -PI_BELOW, ALU.min, ALU.max)
                stt(c, r, -1.0, r, ALU.mult, ALU.max)
                ts(c, c, -1.0, math.pi / 2, ALU.mult, ALU.add)

            def cmul(ore, oim, ar, ai, br, bi, x, y):
                then(vec.tensor_tensor(x, ar, br, ALU.mult))
                then(vec.tensor_tensor(y, ai, bi, ALU.mult))
                then(vec.tensor_tensor(x, x, y, ALU.subtract))
                then(vec.tensor_tensor(y, ar, bi, ALU.mult))
                then(vec.tensor_tensor(oim, ai, br, ALU.mult))
                then(vec.tensor_tensor(oim, oim, y, ALU.add))
                then(vec.tensor_copy(ore, x))

            dve.wait_ge(params, 16 * 16)
            for j in range(L):
                last = vec.tensor_copy(d_rep[:, j, :], d_in[:, :])
            last.then_inc(d_copied, 1)
            dve.wait_ge(flipped, 1)
            lr, li, dcol = V("lr"), V("li"), V("dcol")
            then(vec.tensor_copy(lr, ps_a[:, 0:NG]))
            then(vec.tensor_copy(li, ps_a[:, NG:2 * NG]))
            then(vec.tensor_copy(dcol, ps_a[:, 2 * NG:3 * NG]))
            for r in range(2):
                then(vec.tensor_copy(Cm[:, r, :, :].rearrange("q g c -> q (g c)"), ps_c[:, r, :, :].rearrange("q n x -> q (n x)")))
            for x in range(2):
                for n in range(2):
                    then(vec.tensor_copy(h0[:, x, 4 * n:4 * n + 4, :].rearrange("q b g -> q (b g)"), ps_h[:, n, x, :]))
            exp(V("dt"), V("logdt"))
            ar, ai = V("ar"), V("ai")
            tt(ar, lr, V("dt"), ALU.mult)
            tt(ai, li, V("dt"), ALU.mult)
            reduce_angle("1", ai)
            ts(V("ai8"), ai, 8.0, None, ALU.mult, ALU.bypass)
            reduce_angle("8", V("ai8"))
            dve.sem_inc(reduced, 1)
            exp(V("r1"), ar)
            ts(V("ar8"), ar, 8.0, None, ALU.mult, ALU.bypass)
            exp(V("r8"), V("ar8"))
            dve.wait_ge(sins, 4)
            then(vec.memset(pw[:, 0, 0, :], 1.0))
            then(vec.memset(pw[:, 1, 0, :], 0.0))
            tt(pw[:, 0, 1, :], V("r1"), V("cos1"), ALU.mult)
            tt(pw[:, 1, 1, :], V("r1"), V("sin1"), ALU.mult)
            for m in (1, 2, 4):
                dst, src = slice(m + 1, 2 * m + 1), slice(1, m + 1)
                base = [pw[:, r, m, :].unsqueeze(1).broadcast_to([P, m, NG]) for r in range(2)]
                x, y = (t[:, 0:m * NG].rearrange("p (m g) -> p m g", m=m) for t in (t1, t2))
                cmul(pw[:, 0, dst, :], pw[:, 1, dst, :], pw[:, 0, src, :], pw[:, 1, src, :], base[0], base[1], x, y)
            lo, hi = slice(0, NST), slice(NST, P)
            then(vec.tensor_copy(PP[lo, :, :], pw[lo, 0, :, :]))
            then(vec.tensor_copy(PP[hi, :, :], pw[hi, 1, :, :]))
            ts(QQ[lo, :, :], pw[lo, 1, :, :], -1.0, None, ALU.mult, ALU.bypass)
            then(vec.tensor_copy(QQ[hi, :, :], pw[hi, 0, :, :]))
            nr, den, fr, fi, x = V("nr"), V("den"), V("fr"), V("fi"), V("x")
            ts(nr, pw[:, 0, 1, :], -1.0, None, ALU.add, ALU.bypass)
            ni = pw[:, 1, 1, :]
            tt(den, lr, lr, ALU.mult)
            tt(x, li, li, ALU.mult)
            tt(den, den, x, ALU.add)
            then(vec.reciprocal(den, den))
            tt(fr, nr, lr, ALU.mult)
            tt(x, ni, li, ALU.mult)
            tt(fr, fr, x, ALU.add)
            tt(fr, fr, den, ALU.mult)
            tt(fi, ni, lr, ALU.mult)
            tt(x, nr, li, ALU.mult)
            tt(fi, fi, x, ALU.subtract)
            tt(fi, fi, den, ALU.mult)
            dve.wait_ge(bc_in, 64)
            wide = [P, NG, GC]
            x, y = (t[:, 0:NG * GC].rearrange("p (g c) -> p g c", g=NG) for t in (t1, t2))
            cmul(Bb[:, 0], Bb[:, 1], Bm[:, 0], Bm[:, 1], fr.unsqueeze(2).broadcast_to(wide), fi.unsqueeze(2).broadcast_to(wide), x, y)
            for j in range(L):
                p7, q7 = (a[:, L - 1 - j, :].unsqueeze(2).broadcast_to(wide) for a in (PP, QQ))
                tt(x, Bb[:, 0], p7, ALU.mult)
                tt(y, Bb[:, 1], q7, ALU.mult)
                tt(NB[:, :, j, :], x, y, ALU.add)
            for tau in range(L + 1):
                pt, qt = (a[:, tau, :].unsqueeze(2).broadcast_to(wide) for a in (PP, QQ))
                tt(x, Cm[:, 0], pt, ALU.mult)
                tt(y, Cm[:, 1], qt, ALU.mult)
                tt(x, x, y, ALU.add)
                ts(CL[:, :, tau, :], x, sgn[:, 0:1], None, ALU.mult, ALU.bypass)
                if tau:
                    tt(x, Cm[:, 0], qt, ALU.mult)
                    tt(y, Cm[:, 1], pt, ALU.mult)
                    tt(CM[:, :, tau - 1, :], x, y, ALU.subtract)
            dve.sem_inc(mats, 1)
            for E, first in ((E1, None), (E16, E1)):
                then(vec.memset(E[:, 0, :, 0], 1.0))
                then(vec.memset(E[:, 1, :, 0], 0.0))
                if first is None:
                    then(vec.tensor_copy(E[:, 0, :, 1], V("cos8")))
                    then(vec.tensor_copy(E[:, 1, :, 1], V("sin8")))
                else:
                    cmul(E[:, 0, :, 1], E[:, 1, :, 1], E1[:, 0, :, 8], E1[:, 1, :, 8], E1[:, 0, :, 8], E1[:, 1, :, 8],
                         t1[:, 0:NG], t2[:, 0:NG])
                for m in (0, 1, 2, 4, 8):
                    if m:
                        n = min(m, 15 - m)
                        dst, src = slice(m + 1, m + n + 1), slice(1, n + 1)
                        base = [E[:, r, :, m].unsqueeze(2).broadcast_to([P, NG, n]) for r in range(2)]
                        x, y = (t[:, 0:n * NG].rearrange("p (g m) -> p g m", g=NG) for t in (t1, t2))
                        cmul(E[:, 0, :, dst], E[:, 1, :, dst], E[:, 0, :, src], E[:, 1, :, src], base[0], base[1], x, y)
                    else:
                        n, dst = 1, slice(1, 2)
                        x, y = (t[:, 0:NG].rearrange("p (g m) -> p g m", g=NG) for t in (t1, t2))
                    er, ei = E[:, 0, :, dst], E[:, 1, :, dst]
                    tt(x, er, er, ALU.mult)
                    tt(y, ei, ei, ALU.mult)
                    tt(x, x, y, ALU.add)
                    ts(x, x, -0.5, 1.5, ALU.mult, ALU.add)
                    tt(er, er, x, ALU.mult)
                    tt(ei, ei, x, ALU.mult)
            dve.sem_inc(e_ready, 1)
            dve.wait_ge(kq_moved, 8 * 16)
            for n in range(4):
                gs = slice(n * 8, n * 8 + 8)
                x = t1[:, 0:1024].rearrange("p (g n) -> p g n", g=8)
                tt(x, ident[:, :].unsqueeze(1).broadcast_to([P, 8, P]), dcol[:, gs].unsqueeze(2).broadcast_to([P, 8, P]), ALU.mult)
                tt(TT[:, gs, :], TT[:, gs, :], x, ALU.add)
            dve.sem_inc(t_ready, 1)
            wide = [P, DB, NG]
            then(vec.tensor_copy(hs[:, :, :], h0[:, 0, :, :].rearrange("q b g -> q g b")))
            ts(V("si"), pw[:, 1, L, :], sgn[:, 0:1], -1.0, ALU.mult, ALU.mult)
            tt(hpre[:, :, :], h0[:, 0, :, :], pw[:, 0, L, :].unsqueeze(1).broadcast_to(wide), ALU.mult)
            x = t1[:, 0:DB * NG].rearrange("p (b g) -> p b g", b=DB)
            tt(x, h0[:, 1, :, :], V("si").unsqueeze(1).broadcast_to(wide), ALU.mult)
            tt(hpre[:, :, :], hpre[:, :, :], x, ALU.add)
            dve.sem_inc(hpre_ready, 2)
            for n in range(4):
                gs = slice(n * 8, n * 8 + 8)
                hi_ = [E16[:, r, gs, :].unsqueeze(3).broadcast_to([P, 8, 16, 16]) for r in range(2)]
                lo_ = [E1[:, r, gs, :].unsqueeze(2).broadcast_to([P, 8, 16, 16]) for r in range(2)]
                a, b = (t[:, :].rearrange("p (g a b) -> p g a b", g=8, a=16) for t in (t1, t2))
                tt(a, hi_[0], lo_[0], ALU.mult)
                tt(b, hi_[1], lo_[1], ALU.mult)
                if n:
                    dve.wait_ge(cs_even, n * 16)
                nc.vector.tensor_tensor(cosq[:, :, :].rearrange("p g n -> p (g n)"), t1[:, :], t2[:, :], ALU.subtract).then_inc(cos_ready, 1)
                dve.wait_ge(cos_ready, n + 1)


U5 = 4


def s5(nc, T, top):
    with Stage(nc, top, "s5") as s:
        ident, swap = s.sb("ident", [P, P]), s.sb("swap", [P, P])
        u, us = s.sb("u", [P, 2, L, SW]), s.sb("us", [DB, L, SW])
        y, ys = s.sb("y", [P, 2, L, SW]), s.sb("ys", [DB, L, SW])
        rec = s.sb("rec", [P, U5, RECW])
        ug = s.sb("ug", [P, U5, 3, P])
        uT = s.sb("uT", [P, U5, NCH + DB])
        w1, w2, G = s.sb("w1", [P, 2, NCH]), s.sb("w2", [P, 2, NCH]), s.sb("G", [P, 2, NCH])
        A, B = s.sb("A", [P, 2, NCH + 1]), s.sb("B", [P, 2, NCH + 1])
        r8 = s.sb("r8", [P, NG])
        lastA, lastB, ss = s.sb("lastA", [P, NG]), s.sb("lastB", [P, NG]), s.sb("ss", [P, DB, NG])
        hp = s.sb("hp", [P, DB, NG])
        fin, fins = s.sb("fin", [NG, P]), s.sb("fins", [P, 2, P])
        ps_u, ps_s, ps_w = s.ps("ps_u", [P, 3, P]), s.ps("ps_s", [P, 2, 512]), s.ps("ps_w", [P, 2, 512])
        ps_y, ps_f = s.ps("ps_y", [P, 2, 512]), s.ps("ps_f", [P, 512])
        loaded = s.sem("loaded")
        rec_in = [s.sem(f"rec{q}") for q in range(U5)]
        ug_ready, flipped, uT_ready = s.sem("ug_ready"), s.sem("flipped"), s.sem("uT_ready")
        states, y_done, y_out = s.sem("states"), s.sem("y_done"), s.sem("y_out")
        turned, added, g_ready, a_ready, b_ready = (s.sem(n) for n in ("turned", "added", "g_ready", "a_ready", "b_ready"))
        last_ready, edges, fin_mm, fin_out, stored = (s.sem(n) for n in ("last_ready", "edges", "fin_mm", "fin_out", "stored"))
        y_a, edges0, lastb_ready = s.sem("y_a"), s.sem("edges0"), s.sem("lastb_ready")
        blk = s.block()
        up = T["proj"][0:SEQ, 0:SW].rearrange("(i p j) c -> p i j c", i=2, j=L)
        usv = T["proj"][SEQ:SEQ + NS, 0:SW].rearrange("(b j) c -> b j c", j=L)
        yp = T["y"][0:SEQ, :].rearrange("(i p j) c -> p i j c", i=2, j=L)
        ysv = T["y"][SEQ:SEQ + NS, :].rearrange("(b j) c -> b j c", j=L)

        def R(q, name):
            a, w = REC[name]
            return rec[:, q, a:a + w]

        @blk.sync
        def _(sp):
            for dst, name in ((ident, "ident"), (swap, "swap"), (r8, "r8")):
                sp.dma_start(dst[:, :], T[name]).then_inc(loaded, 16)
            sp.dma_start(hp[:, :, :].rearrange("q b g -> q (b g)"), T["hpre"]).then_inc(loaded, 16)
            for i in range(2):
                sp.dma_start(u[:, i, :, :], up[:, i]).then_inc(loaded, 16)
            sp.dma_start(us[:, :, :], usv).then_inc(loaded, 16)
            with sp.Fori(0, NG // U5) as i:
                for q in range(U5):
                    sp.wait_ge(y_done, i * U5 + q + 1)
                    sp.dma_start(rec[:, q, :].unsqueeze(1), T["rec"].rearrange("g q w -> q g w")[:, bass.ds(i * U5 + q, 1), :]).then_inc(rec_in[q], 16)
            sp.wait_ge(y_out, NG + 1)
            sp.dma_start(ysv, ys[:, :, :]).then_inc(stored, 16)
            for i in range(2):
                sp.dma_start(yp[:, i], y[:, i, :, :]).then_inc(stored, 16)
            sp.wait_ge(fin_out, 2)
            for r, part in enumerate(("re", "im")):
                cols = slice(r * NST, (r + 1) * NST)
                sp.dma_start(T[f"o_ssm_{part}_prompt"][0, 0], fin[:, cols]).then_inc(stored, 16)
                for n in range(2):
                    dst = T[f"o_ssm_{part}_sample"].rearrange("a b g p -> (a b g) p")[n * P:(n + 1) * P, :]
                    sp.dma_start(dst, fins[:, n, cols]).then_inc(stored, 16)
            sp.wait_ge(stored, 9 * 16)

        @blk.scalar
        def _(act):
            act.sem_inc(y_out, 1)
            act.wait_ge(loaded, 7 * 16)

            def group(g, q, first=False):
                cols = bass.ds(g * GC, GC)
                if not first:
                    act.wait_ge(flipped, g - U5 + 1)
                nc.scalar.activation(ug[:, q, 0:2, :].rearrange("p i (j c) -> p i j c", j=L), u[:, :, :, cols], ACT.Copy).then_inc(ug_ready, 1)
                nc.scalar.activation(ug[0:DB, q, 2, :].rearrange("p (j c) -> p j c", j=L), us[:, :, cols], ACT.Copy).then_inc(ug_ready, 1)

            def out(g, par):
                cols = bass.ds(g * GC, GC)
                act.wait_ge(y_done, g + U5 + 1)
                nc.scalar.activation(y[:, :, :, cols], ps_y[:, par, 0:2 * P].rearrange("p (i j c) -> p i j c", i=2, j=L), ACT.Copy).then_inc(y_a, 1)
                nc.scalar.activation(ys[:, :, cols], ps_y[0:DB, par, 2 * P:3 * P].rearrange("p (j c) -> p j c", j=L), ACT.Copy).then_inc(y_out, 1)

            for g in range(U5):
                group(g, g, True)
            out(0, 0)
            with act.Fori(0, NG // U5 - 1) as i:
                for q in range(U5):
                    group(i * U5 + q + U5, q)
                    out(i * U5 + q + 1, (q + 1) % 2)
            for g in range(NG - U5 + 1, NG):
                out(g, g % 2)

        @blk.tensor
        def _(pe):
            pe.sem_inc(y_done, U5)
            pe.wait_ge(loaded, 7 * 16)

            def flip(g, q, first=False):
                pe.wait_ge(ug_ready, g * 2 + 2)
                if not first:
                    pe.wait_ge(uT_ready, g)
                for i in range(2):
                    nc.tensor.transpose(ps_u[:, i, :], ug[:, q, i, :], ident[:, :])
                nc.tensor.transpose(ps_u[:, 2, 0:DB], ug[0:DB, q, 2, :], ident[0:DB, 0:DB]).then_inc(flipped, 1)

            def contribute(g, q, n):
                pe.wait_ge(uT_ready, g + 1)
                pe.wait_ge(rec_in[q], n)
                a = REC["N"][0]
                nc.tensor.matmul(ps_s[:, q % 2, 0:NCH + DB], rec[:, q, a:a + P], uT[:, q, :], start=True, stop=True)
                nc.tensor.matmul(ps_w[:, q % 2, 0:NCH + DB], rec[:, q, a + NST:a + NST + P], uT[:, q, :], start=True, stop=True).then_inc(states, 1)

            def back(g, q):
                par = q % 2
                pe.wait_ge(y_out, g)
                pe.wait_ge(a_ready, g + 1)
                pe.wait_ge(b_ready, g + 1)
                for i in range(2):
                    c = slice(i * P, (i + 1) * P)
                    nc.tensor.matmul(ps_y[:, par, c], uT[:, q, c], R(q, "T"), start=True, stop=False)
                    nc.tensor.matmul(ps_y[:, par, c], A[:, par, c], R(q, "M"), start=False, stop=False)
                    nc.tensor.matmul(ps_y[:, par, c], B[:, par, c], R(q, "MS"), start=False, stop=True)
                c = slice(2 * P, 3 * P)
                nc.tensor.matmul(ps_y[0:DB, par, c], uT[:, q, NCH:NCH + DB], R(q, "T"), start=True, stop=False)
                nc.tensor.matmul(ps_y[0:DB, par, c], R(q, "H0"), R(q, "M"), start=False, stop=True).then_inc(y_done, 1)

            flip(0, 0, True)
            contribute(0, 0, 16)
            flip(1, 1)
            contribute(1, 1, 16)
            with pe.Fori(0, NG // U5 - 1) as i:
                for q in range(U5):
                    g, ahead = i * U5 + q, (q + 2) % U5
                    flip(g + 2, ahead)
                    back(g, q)
                    contribute(g + 2, ahead, i * 16 + (16 if q < 2 else 32))
            for g in range(NG - U5, NG):
                if g + 2 < NG:
                    flip(g + 2, (g + 2) % U5)
                back(g, g % U5)
                if g + 2 < NG:
                    contribute(g + 2, (g + 2) % U5, NG // U5 * 16)
            pe.wait_ge(edges, 1)
            nc.tensor.matmul(ps_f[0:NG, 0:P], lastA[:, :], ident[:, :], start=True, stop=False)
            nc.tensor.matmul(ps_f[0:NG, 0:P], lastB[:, :], swap[:, :], start=False, stop=True)
            for n in range(2):
                last = nc.tensor.transpose(ps_f[:, (n + 1) * P:(n + 2) * P], ss[:, 4 * n:4 * n + 4, :].rearrange("q b g -> q (b g)"), ident[:, :])
            last.then_inc(fin_mm, 1)

        @blk.gpsimd
        def _(pool):
            with pool.Fori(0, NG // U5) as i:
                for q in range(U5):
                    g, par = i * U5 + q, q % 2
                    pool.wait_ge(g_ready, g + 1)
                    nc.gpsimd.tensor_tensor(lastB[:, bass.ds(g, 1)], G[:, par, NCH - 1:], R(q, "SIN")[:, NCH - 1:], ALU.mult).then_inc(lastb_ready, 1)
                    nc.gpsimd.tensor_tensor(B[:, par, 1:], G[:, par, :], R(q, "SIN"), ALU.mult).then_inc(b_ready, 1)

        @blk.vector
        def _(dve):
            vec = nc.vector
            vec.memset(A[:, :, 0:1], 0.0)
            vec.memset(B[:, :, 0:1], 0.0).then_inc(edges0, 1)
            dve.wait_ge(edges0, 1)
            dve.wait_ge(loaded, 7 * 16)

            def turn(g, q, first=False):
                dve.wait_ge(flipped, g + 1)
                if not first:
                    dve.wait_ge(y_done, g + 1)
                vec.tensor_copy(uT[:, q, :], ps_u[:, :, :].rearrange("p i n -> p (i n)")[:, 0:NCH + DB]).then_inc(uT_ready, 1)

            def scan(g, q):
                par = q % 2
                dve.wait_ge(states, g + 1)
                vec.tensor_tensor(w1[:, par, :], ps_s[:, par, 0:NCH], R(q, "COS"), ALU.mult).then_inc(turned, 1)
                vec.tensor_tensor(w2[:, par, :], ps_w[:, par, 0:NCH], R(q, "SIN"), ALU.mult).then_inc(turned, 1)
                vec.tensor_copy(ss[:, :, bass.ds(g, 1)], ps_s[:, par, NCH:NCH + DB].unsqueeze(2)).then_inc(turned, 1)
                dve.wait_ge(turned, g * 3 + 3)
                vec.tensor_tensor(w1[:, par, :], w1[:, par, :], w2[:, par, :], ALU.add).then_inc(added, 1)
                dve.wait_ge(added, g + 1)
                vec.tensor_tensor_scan(G[:, par, :], r8[:, bass.ds(g, 1)].broadcast_to([P, NCH]), w1[:, par, :], 0.0, ALU.mult, ALU.add).then_inc(g_ready, 1)
                dve.wait_ge(g_ready, g + 1)
                vec.tensor_tensor(lastA[:, bass.ds(g, 1)], G[:, par, NCH - 1:], R(q, "COS")[:, NCH - 1:], ALU.mult).then_inc(last_ready, 1)
                vec.tensor_tensor(A[:, par, 1:], G[:, par, :], R(q, "COS"), ALU.mult).then_inc(a_ready, 1)

            for g in range(2):
                turn(g, g, True)
            scan(0, 0)
            turn(2, 2, True)
            scan(1, 1)
            turn(3, 3, True)
            with dve.Fori(0, NG // U5 - 1) as i:
                for k in range(2, U5 + 2):
                    scan(i * U5 + k, k % U5)
                    turn(i * U5 + k + 2, (k + 2) % U5)
            scan(NG - 2, U5 - 2)
            scan(NG - 1, U5 - 1)
            dve.wait_ge(last_ready, NG)
            dve.wait_ge(turned, 3 * NG)
            dve.wait_ge(lastb_ready, NG)
            vec.tensor_tensor(ss[:, :, :], ss[:, :, :], hp[:, :, :], ALU.add).then_inc(edges, 1)
            dve.wait_ge(fin_mm, 1)
            vec.tensor_copy(fin[:, :], ps_f[0:NG, 0:P]).then_inc(fin_out, 1)
            vec.tensor_copy(fins[:, :, :], ps_f[:, P:3 * P].rearrange("p (n q) -> p n q", n=2)).then_inc(fin_out, 1)


BW = 3 * WIN
RB = NH * BW


def bucket_onehot():
    out = np.zeros((NBUCKET + 1, BW), np.float32)
    half = NBUCKET // 2
    for m in range(BW):
        d = 2 * WIN - 1 - m
        if 0 <= d <= WIN:
            log = math.log(max(d, 1) / half) / math.log(WIN / half)
            out[d if d < half else min(half + int(log * (NBUCKET - half)), NBUCKET - 1), m] = 1.0
        else:
            out[NBUCKET, m] = 1.0
    return out


def attention_bias(nc, T, top):
    with Stage(nc, top, "ab") as s:
        tab, wide, hot = s.sb("tab", [NBUCKET + 1, NH]), s.sb("wide", [NBUCKET + 1, NH, P]), s.sb("hot", [NBUCKET + 1, BW])
        rows = s.sb("rows", [P, NH, BW])
        ps = s.ps("ps", [P, NH, 512])
        loaded, masked, widened, done, moved, stored = (s.sem(n) for n in ("loaded", "masked", "widened", "done", "moved", "stored"))
        blk = s.block()

        @blk.sync
        def _(sp):
            sp.dma_start(tab[0:NBUCKET, :], T["rel_bias_table"]).then_inc(loaded, 16)
            sp.dma_start(hot[:, :], T["onehot"]).then_inc(loaded, 16)
            sp.wait_ge(moved, NH)
            sp.dma_start(T["bias_rows"], rows[:, :, :].rearrange("p h m -> p (h m)")).then_inc(stored, 16)
            for n, name in enumerate("kv"):
                c0 = SW + AW + n * KVW
                cut = T["proj"][:, c0:c0 + KVW]
                sp.dma_start(T[f"o_{name}_prompt"].rearrange("a b w h d -> (a b w) (h d)"), cut[SEQ - WIN:SEQ, :]).then_inc(stored, 16)
                old = T[f"cache_{name}"].rearrange("a b w h d -> (a b) w (h d)")
                new = T[f"o_{name}_sample"].rearrange("a b w h d -> (a b) w (h d)")
                sp.dma_start(new[:, 0:WIN - DT, :], old[:, DT:WIN, :]).then_inc(stored, 16)
                sp.dma_start(new[:, WIN - DT:WIN, :], cut[SEQ:SEQ + NS, :].rearrange("(b t) c -> b t c", t=DT)).then_inc(stored, 16)
            sp.wait_ge(stored, 7 * 16)

        @blk.vector
        def _(dve):
            nc.vector.memset(tab[NBUCKET:NBUCKET + 1, :], MASKED).then_inc(masked, 1)
            dve.wait_ge(loaded, 32)
            dve.wait_ge(masked, 1)
            nc.vector.tensor_copy(wide[:, :, :], tab[:, :].unsqueeze(2).broadcast_to([NBUCKET + 1, NH, P])).then_inc(widened, 1)
            for h in range(NH):
                dve.wait_ge(done, h + 1)
                nc.vector.tensor_copy(rows[:, h, :], ps[:, h, 0:BW]).then_inc(moved, 1)

        @blk.tensor
        def _(pe):
            pe.wait_ge(widened, 1)
            for h in range(NH):
                nc.tensor.matmul(ps[:, h, 0:BW], wide[:, h, :], hot[:, :], start=True, stop=True).then_inc(done, 1)


def bias_view(T, rows, head, keys):
    flat = T["bias_rows"].rearrange("p m -> (p m)")[P - 1:P - 1 + rows * (RB - 1)]
    return flat.rearrange("(q m) -> q m", m=RB - 1)[:, head * BW:head * BW + keys]


def prompt_attention(nc, T, top):
    QKV = AW + 2 * KVW
    with Stage(nc, top, "at") as s:
        ident = s.sb("ident", [P, P])
        bias = s.sb("bias", [P, NH, 2 * WIN])
        sink, nsink = s.sb("sink", [P, NH]), s.sb("nsink", [P, NH])
        qkv, v = s.sb("qkv", [P, 2, QKV]), s.sb("v", [P, 2, KVW])
        qT, kT = s.sb("qT", [P, GQ, P]), s.sb("kT", [P, 2, P])
        sc, pT = s.sb("sc", [P, 2, NH, 2 * WIN]), s.sb("pT", [P, NH, 2, P])
        mx, nm, ds = s.sb("mx", [P, 2, NH]), s.sb("nm", [P, 2, NH]), s.sb("ds", [P, 2, NH])
        sm, es, rd = s.sb("sm", [P, 2, NH]), s.sb("es", [P, 2, NH]), s.sb("rd", [P, 2, NH])
        o = s.sb("o", [P, 2, AW])
        ps_s, ps_q, ps_t, ps_o = s.ps("ps_s", [P, 4, 512]), s.ps("ps_q", [P, 512]), s.ps("ps_t", [P, 2, 512]), s.ps("ps_o", [P, 512])
        (consts, in_even, in_odd, sunk, flipped, q_moved, k_moved, v_moved, scored, biased, negated, shifted, exped, es_ready,
         turned, pt_a, pt_v, attended, den, rden, o_out, st_even, st_odd) = (s.sem(n) for n in (
             "consts", "in_even", "in_odd", "sunk", "flipped", "q_moved", "k_moved", "v_moved", "scored", "biased", "negated",
             "shifted", "exped", "es_ready", "turned", "pt_a", "pt_v", "attended", "den", "rden", "o_out", "st_even", "st_odd"))
        passed = s.sem("passed")
        blk = s.block()
        pv = T["proj"][:, SW:].rearrange("(n p) d -> p n d", p=P)
        av = T["attn"].rearrange("(n p) d -> p n d", p=P)
        HALF = NPT // 2

        @blk.sync
        def _(sp):
            def load(t, par, arrived):
                sp.dma_start(qkv[:, par, :].unsqueeze(1), pv[:, bass.ds(t, 1), :]).then_inc(arrived, 16)

            def store(t, par, stored):
                sp.wait_ge(o_out, t + 2)
                sp.dma_start(av[:, bass.ds(t, 1), :], o[:, par, :].unsqueeze(1)).then_inc(stored, 16)

            sp.sem_inc(st_even, 16)
            sp.sem_inc(st_odd, 16)
            sp.dma_start(ident[:, :], T["ident"]).then_inc(consts, 16)
            sp.dma_start(sink[:, :], T["attn_sinks"][0, :].partition_broadcast(P)).then_inc(consts, 16)
            load(0, 0, in_even)
            load(1, 1, in_odd)
            for h in range(NH):
                sp.dma_start(bias[:, h, :], bias_view(T, P, h, 2 * WIN)).then_inc(consts, 16)
            with sp.Fori(0, HALF - 1) as i:
                for par, arrived, stored in ((0, in_even, st_even), (1, in_odd, st_odd)):
                    sp.wait_ge(flipped, i * 2 + par + 1)
                    sp.wait_ge(v_moved, i * 2 + par + 1)
                    load(i * 2 + par + 2, par, arrived)
                    store(i * 2 + par, par, stored)
            store(NPT - 2, 0, st_even)
            store(NPT - 1, 1, st_odd)
            sp.wait_ge(st_even, (HALF + 1) * 16)
            sp.wait_ge(st_odd, (HALF + 1) * 16)

        @blk.scalar
        def _(act):
            def queries(t, par):
                act.wait_ge(flipped, t + 1)
                nc.scalar.activation(qT[:, :, :].rearrange("p g n -> p (g n)"), ps_q[:, :], ACT.Copy, scale=HD ** -0.5).then_inc(q_moved, 1)

            def exps(t, par, k0):
                act.wait_ge(negated, t + 1)
                for h in range(NH):
                    nc.scalar.activation(sc[:, par, h, k0:], sc[:, par, h, k0:], ACT.Exp, bias=nm[:, par, h:h + 1],
                                         accum_out=sm[:, par, h:h + 1]).then_inc(exped, 1)
                act.wait_ge(shifted, t + 1)
                nc.scalar.activation(es[:, par, :], ds[:, par, :], ACT.Exp).then_inc(es_ready, 1)

            def probs(t, k0):
                for b in (0, 2):
                    act.wait_ge(turned, t * 4 + b + 1)
                    src = ps_t[:, 0, :].rearrange("p (h k n) -> p h k n", h=2, k=2)
                    nc.scalar.activation(pT[:, 2 * b:2 * b + 2, k0 // WIN:, :], src[:, :, k0 // WIN:, :], ACT.Copy).then_inc(pt_a, 1)

            queries(0, 0)
            exps(0, 0, WIN)
            queries(1, 1)
            probs(0, WIN)
            exps(1, 1, 0)
            with act.Fori(0, HALF - 1) as i:
                for par in (1, 0):
                    t = i * 2 + 2 - par
                    queries(t + 1, 1 - par)
                    probs(t, 0)
                    exps(t + 1, 1 - par, 0)
            probs(NPT - 1, 0)

        @blk.vector
        def _(dve):
            vec = nc.vector
            dve.sem_inc(biased, 8)
            dve.sem_inc(o_out, 1)
            dve.wait_ge(consts, 10 * 16)
            vec.tensor_scalar(nsink[:, :], sink[:, :], -1.0, None, ALU.mult).then_inc(sunk, 1)
            dve.wait_ge(sunk, 1)

            def keys(t, par):
                dve.wait_ge(flipped, t + 1)
                vec.tensor_copy(kT[:, par, :], ps_t[:, 0, 0:P]).then_inc(k_moved, 1)

            def maxima(t, par, k0):
                for h in range(NH):
                    if h % 2 == 0:
                        dve.wait_ge(scored, t * 4 + h // 2 + 1)
                        dve.sem_inc(passed, 1)
                    at = h % 2 * 2 * WIN
                    vec.tensor_tensor_reduce(out=sc[:, par, h, k0:], in0=ps_s[:, h // 2, at + k0:at + 2 * WIN], in1=bias[:, h, k0:],
                                             scale=1.0, scalar=MASKED, op0=ALU.add, op1=ALU.max,
                                             accum_out=mx[:, par, h:h + 1]).then_inc(biased, 1)
                dve.wait_ge(biased, t * 8 + 16)
                vec.scalar_tensor_tensor(nm[:, par, :], mx[:, par, :], -1.0, nsink[:, :], ALU.mult, ALU.min).then_inc(negated, 1)
                dve.wait_ge(negated, t + 1)
                vec.tensor_tensor(ds[:, par, :], sink[:, :], nm[:, par, :], ALU.add).then_inc(shifted, 1)

            def probs(t, k0):
                for b in (1, 3):
                    dve.wait_ge(turned, t * 4 + b + 1)
                    src = ps_t[:, 1, :].rearrange("p (h k n) -> p h k n", h=2, k=2)
                    vec.tensor_copy(pT[:, 2 * b:2 * b + 2, k0 // WIN:, :], src[:, :, k0 // WIN:, :]).then_inc(pt_v, 1)

            def out(t, par, stored, n):
                dve.wait_ge(es_ready, t + 1)
                vec.tensor_tensor(sm[:, par, :], sm[:, par, :], es[:, par, :], ALU.add).then_inc(den, 1)
                dve.wait_ge(den, t + 1)
                vec.reciprocal(rd[:, par, :], sm[:, par, :]).then_inc(rden, 1)
                dve.wait_ge(rden, t + 1)
                dve.wait_ge(attended, t + 2)
                dve.wait_ge(stored, n)
                vec.tensor_tensor(o[:, par, :].rearrange("p (h d) -> p h d", h=NH), ps_o[:, :].rearrange("p (h d) -> p h d", h=NH),
                                  rd[:, par, :].unsqueeze(2).broadcast_to([P, NH, HD]), ALU.mult).then_inc(o_out, 1)

            def values(t, par, arrived, n):
                dve.wait_ge(arrived, n)
                vec.tensor_copy(v[:, par, :], qkv[:, par, AW + KVW:]).then_inc(v_moved, 1)

            keys(0, 0)
            maxima(0, 0, WIN)
            values(0, 0, in_even, 16)
            keys(1, 1)
            maxima(1, 1, 0)
            probs(0, WIN)
            out(0, 0, st_even, 16)
            values(1, 1, in_odd, 16)
            with dve.Fori(0, HALF - 1) as i:
                for par, stored in ((1, st_odd), (0, st_even)):
                    t = i * 2 + 2 - par
                    keys(t + 1, 1 - par)
                    maxima(t + 1, 1 - par, 0)
                    probs(t, 0)
                    out(t, par, stored, i * 16 + (16 if par else 32))
                    values(t + 1, 1 - par, in_even if par else in_odd, i * 16 + 32)
            probs(NPT - 1, 0)
            out(NPT - 1, 1, st_odd, HALF * 16)

        @blk.tensor
        def _(pe):
            pe.sem_inc(attended, 1)
            pe.wait_ge(consts, 10 * 16)

            def flip(t, par, arrived, n, first):
                pe.wait_ge(arrived, n)
                if not first:
                    pe.wait_ge(q_moved, t)
                for g in range(GQ):
                    nc.tensor.transpose(ps_q[:, g * P:(g + 1) * P], qkv[:, par, g * P:(g + 1) * P], ident[:, :])
                nc.tensor.transpose(ps_t[:, 0, 0:P], qkv[:, par, AW:AW + KVW], ident[:, :]).then_inc(flipped, 1)

            def scores(t, par, blocks):
                pe.wait_ge(q_moved, t + 1)
                pe.wait_ge(k_moved, t + 1)
                for h in range(NH):
                    kv, g = divmod(h, GQ)
                    rows = slice(kv * HD, (kv + 1) * HD)
                    if h % 2 == 0:
                        pe.wait_ge(biased, t * 8 + h + 2)
                    for k in blocks:
                        slot = par if k else 1 - par
                        at = (h % 2 * 2 + k) * WIN
                        last = nc.tensor.matmul(ps_s[:, h // 2, at:at + WIN], qT[rows, g, :], kT[rows, slot, :], start=True, stop=True)
                    if h % 2:
                        last.then_inc(scored, 1)

            def turn(t, par, blocks):
                for b in range(4):
                    pe.wait_ge(exped, t * 8 + 2 * b + 2)
                    if b >= 2:
                        pe.wait_ge(*((pt_a, t * 2 + 1) if b == 2 else (pt_v, t * 2 + 1)))
                    for h in (2 * b, 2 * b + 1):
                        for k in blocks:
                            at = (h % 2 * 2 + k) * P
                            last = nc.tensor.transpose(ps_t[:, b % 2, at:at + P], sc[:, par, h, k * WIN:(k + 1) * WIN], ident[:, :])
                    last.then_inc(turned, 1)

            def attend(t, par, blocks):
                pe.wait_ge(v_moved, t + 1)
                pe.wait_ge(o_out, t + 1)
                for h in range(NH):
                    if h % 4 == 0:
                        pe.wait_ge(pt_a, t * 2 + 1 + h // 4)
                    if h % 4 == 2:
                        pe.wait_ge(pt_v, t * 2 + 1 + h // 4)
                    kv = h // GQ
                    for k in blocks:
                        slot = par if k else 1 - par
                        last = nc.tensor.matmul(ps_o[:, h * HD:(h + 1) * HD], pT[:, h, k, :], v[:, slot, kv * HD:(kv + 1) * HD],
                                                start=(k == blocks[0]), stop=(k == blocks[-1]))
                last.then_inc(attended, 1)

            flip(0, 0, in_even, 16, True)
            scores(0, 0, (1,))
            flip(1, 1, in_odd, 16, False)
            scores(1, 1, (0, 1))
            turn(0, 0, (1,))
            attend(0, 0, (1,))
            with pe.Fori(0, HALF - 1) as i:
                for par, arrived in ((1, in_even), (0, in_odd)):
                    t = i * 2 + 2 - par
                    flip(t + 1, 1 - par, arrived, i * 16 + 32, False)
                    scores(t + 1, 1 - par, (0, 1))
                    turn(t, par, (0, 1))
                    attend(t, par, (0, 1))
            turn(NPT - 1, 1, (0, 1))
            attend(NPT - 1, 1, (0, 1))


def sample_attention(nc, T, top):
    QKV = AW + 2 * KVW
    NB = 2 * NKV
    KEYS = WIN + DT
    G4 = GQ * DT
    with Stage(nc, top, "as") as s:
        ident = s.sb("ident", [P, P])
        bias = s.sb("bias", [P, NKV, KEYS])
        hsel, sink_c, sink, nsink = s.sb("hsel", [NH, NKV, P]), s.sb("sink_c", [NH, 1]), s.sb("sink", [P, NB]), s.sb("nsink", [P, NB])
        qkv = s.sb("qkv", [NS, QKV])
        kc, vc, vn = s.sb("kc", [P, DB, KVW]), s.sb("vc", [P, DB, KVW]), s.sb("vn", [DT, DB, KVW])
        qT, kT = s.sb("qT", [P, DB, GQ, DT]), s.sb("kT", [P, DB, KEYS])
        sc, pc, pn = s.sb("sc", [P, NB, KEYS]), s.sb("pc", [P, NB, P]), s.sb("pn", [DT, NB, P])
        mx, nm, ds, sm, es, rd = (s.sb(n, [P, NB]) for n in ("mx", "nm", "ds", "sm", "es", "rd"))
        o = s.sb("o", [P, NB, HD])
        ps_k, ps_q, ps_s, ps_o, ps_h = s.ps("ps_k", [P, 2, 512]), s.ps("ps_q", [P, 512]), s.ps("ps_s", [P, 2, 512]), s.ps("ps_o", [P, 512]), s.ps("ps_h", [P, 512])
        (loaded, biases, copied, flipped, moved, scored, step, negated, shifted, exped, turned, pmoved, attended, o_out, stored) = (
            s.sem(n) for n in ("loaded", "biases", "copied", "flipped", "moved", "scored", "step", "negated", "shifted", "exped",
                               "turned", "pmoved", "attended", "o_out", "stored"))
        blk = s.block()

        def store(eng, half):
            for b in range(half * 4, half * 4 + 4):
                for kv in range(NKV):
                    for g in range(GQ):
                        r, row, c = b % 4 * G4 + g * DT, SEQ + b * DT, (kv * GQ + g) * HD
                        eng.dma_start(T["attn"][row:row + DT, c:c + HD], o[r:r + DT, b // 4 * NKV + kv, :]).then_inc(stored, 16)

        @blk.sync
        def _(sp):
            sp.dma_start(ident[:, :], T["ident"]).then_inc(loaded, 16)
            sp.dma_start(hsel[:, :, :], T["hsel"]).then_inc(loaded, 16)
            sp.dma_start(sink_c[:, :], T["attn_sinks"].rearrange("a h -> h a"), allow_slow_non_contiguous=True).then_inc(loaded, 16)
            new = T["proj"][SEQ:SEQ + NS, :]
            sp.dma_start(qkv[:, :], new[:, SW:]).then_inc(loaded, 16)
            sp.dma_start(kc[:, :, :], T["cache_k"].rearrange("a b w h d -> w (a b) (h d)")).then_inc(loaded, 16)
            sp.dma_start(vc[:, :, :], T["cache_v"].rearrange("a b w h d -> w (a b) (h d)")).then_inc(loaded, 16)
            sp.dma_start(vn[:, :, :], new[:, SW + AW + KVW:].rearrange("(b t) c -> t b c", t=DT)).then_inc(loaded, 16)
            for kv in range(NKV):
                for g in range(GQ):
                    sp.dma_start(bias[g * DT:(g + 1) * DT, kv, :], bias_view(T, DT, kv * GQ + g, KEYS)).then_inc(biases, 16)
            sp.wait_ge(biases, NH * 16)
            for n in range(1, 4):
                sp.dma_start(bias[n * G4:(n + 1) * G4, :, :], bias[0:G4, :, :]).then_inc(copied, 16)
            sp.wait_ge(o_out, 1)
            store(sp, 0)
            sp.wait_ge(stored, DB * NH * 16)

        @blk.scalar
        def _(act):
            act.wait_ge(flipped, 1)
            nc.scalar.activation(qT[:, :, :, :].rearrange("p b g t -> p g b t"), ps_q[:, 0:GQ * NS].rearrange("p (g b t) -> p g b t", g=GQ, b=DB),
                                 ACT.Copy, scale=HD ** -0.5).then_inc(moved, 1)
            act.wait_ge(negated, 1)
            for n in range(NB):
                nc.scalar.activation(sc[:, n, :], sc[:, n, :], ACT.Exp, bias=nm[:, n:n + 1], accum_out=sm[:, n:n + 1]).then_inc(exped, 1)
            act.wait_ge(shifted, 1)
            nc.scalar.activation(es[:, :], ds[:, :], ACT.Exp).then_inc(exped, 1)
            act.wait_ge(o_out, 1)
            store(act, 1)

        @blk.vector
        def _(dve):
            vec = nc.vector
            st_ = Steps(dve, step)
            dve.wait_ge(flipped, 1)
            vec.tensor_copy(kT[:, :, 0:WIN], ps_k[:, :, :].rearrange("p b (c n) -> p (b c) n", c=4)).then_inc(moved, 1)
            vec.tensor_copy(kT[:, :, WIN:], ps_h[:, 0:NS].rearrange("p (b t) -> p b t", b=DB)).then_inc(moved, 1)
            for n in range(2):
                st_.then(vec.tensor_copy(sink[:, n * NKV:(n + 1) * NKV], ps_h[:, 64:64 + NKV]))
            st_.then(vec.tensor_scalar(nsink[:, :], sink[:, :], -1.0, None, ALU.mult))
            dve.wait_ge(copied, 3 * 16)
            dve.wait_ge(scored, 1)
            for n in range(NB):
                st_.then(vec.tensor_tensor_reduce(out=sc[:, n, :], in0=ps_s[:, n % 2, n // 2 * 256:n // 2 * 256 + KEYS], in1=bias[:, n % 2, :],
                                                  scale=1.0, scalar=MASKED, op0=ALU.add, op1=ALU.max, accum_out=mx[:, n:n + 1]))
            vec.scalar_tensor_tensor(nm[:, :], mx[:, :], -1.0, nsink[:, :], ALU.mult, ALU.min).then_inc(negated, 1)
            dve.wait_ge(negated, 1)
            vec.tensor_tensor(ds[:, :], sink[:, :], nm[:, :], ALU.add).then_inc(shifted, 1)
            dve.wait_ge(turned, 1)
            vec.tensor_copy(pc[:, :, :], ps_q[:, :].rearrange("p (n r) -> p n r", n=NB)).then_inc(pmoved, 1)
            vec.tensor_copy(pn[:, :, :], ps_k[0:DT, 0, :].rearrange("p (n r) -> p n r", n=NB)).then_inc(pmoved, 1)
            dve.wait_ge(exped, NB + 1)
            st_.then(vec.tensor_tensor(sm[:, :], sm[:, :], es[:, :], ALU.add))
            st_.then(vec.reciprocal(rd[:, :], sm[:, :]))
            dve.wait_ge(attended, 1)
            vec.tensor_tensor(o[:, :, :], ps_o[:, 0:NB * HD].rearrange("p (n d) -> p n d", n=NB), rd[:, :].unsqueeze(2).broadcast_to([P, NB, HD]),
                              ALU.mult).then_inc(o_out, 1)

        @blk.tensor
        def _(pe):
            pe.wait_ge(loaded, 7 * 16)
            for b in range(DB):
                nc.tensor.transpose(ps_k[:, b // 4, b % 4 * P:(b % 4 + 1) * P], kc[:, b, :], ident[:, :])
            for g in range(GQ):
                nc.tensor.transpose(ps_q[:, g * NS:(g + 1) * NS], qkv[:, g * P:(g + 1) * P], ident[0:NS, 0:NS])
            nc.tensor.transpose(ps_h[:, 0:NS], qkv[:, AW:AW + KVW], ident[0:NS, 0:NS])
            for kv in range(NKV):
                last = nc.tensor.matmul(ps_h[:, 64 + kv:65 + kv], hsel[:, kv, :], sink_c[:, :], start=True, stop=True)
            last.then_inc(flipped, 1)
            pe.wait_ge(moved, 3)
            for b in range(DB):
                for kv in range(NKV):
                    rows, r0 = slice(kv * HD, (kv + 1) * HD), b % 4 * G4
                    last = nc.tensor.matmul(ps_s[r0:r0 + G4, kv, b // 4 * 256:b // 4 * 256 + KEYS], qT[rows, b, :, :].rearrange("p g t -> p (g t)"),
                                            kT[rows, b, :], start=True, stop=True)
            last.then_inc(scored, 1)
            pe.wait_ge(exped, NB)
            for n in range(NB):
                nc.tensor.transpose(ps_q[:, n * P:(n + 1) * P], sc[:, n, 0:WIN], ident[:, :])
                last = nc.tensor.transpose(ps_k[0:DT, 0, n * P:(n + 1) * P], sc[:, n, WIN:], ident[:, :])
            last.then_inc(turned, 1)
            pe.wait_ge(pmoved, 2)
            for b in range(DB):
                for kv in range(NKV):
                    n, r0, cv = b // 4 * NKV + kv, b % 4 * G4, slice(kv * HD, (kv + 1) * HD)
                    dst = ps_o[r0:r0 + G4, n * HD:(n + 1) * HD]
                    nc.tensor.matmul(dst, pc[:, n, r0:r0 + G4], vc[:, b, cv], start=True, stop=False)
                    last = nc.tensor.matmul(dst, pn[:, n, r0:r0 + G4], vn[:, b, cv], start=False, stop=True)
            last.then_inc(attended, 1)


NR = NEG_ + NE
GELU_C = 2.0 * math.sqrt(2.0 / math.pi) / 2.0


def mixing(nc, T, top):
    with Stage(nc, top, "mx") as s:
        ident = s.sb("ident", [P, P])
        w_glu, w_out, w_rt = s.sb("w_glu", [P, 4, SW]), s.sb("w_out", [P, KD, D]), s.sb("w_rt", [P, KD, NR])
        b_glu, g_s, g_a = s.sb("b_glu", [P, SW]), s.sb("g_s", [P, SW]), s.sb("g_a", [P, AW])
        mod = s.sb("mod", [P, 2, 3, D])
        y, at, x = s.sb("y", [P, 2, SW]), s.sb("at", [P, 2, AW]), s.sb("x", [P, 2, D])
        sq, gq, gw, th1 = s.sb("sq", [P, SW]), s.sb("gq", [P, SW]), s.sb("gw", [P, SW]), s.sb("th1", [P, SW])
        z2, zT = s.sb("z2", [P, 2, SW]), s.sb("zT", [P, 4, P])
        gv, th2, o4 = s.sb("gv", [P, SW]), s.sb("th2", [P, SW]), s.sb("o4", [P, SW])
        j1, j2, j3, j4 = s.sb("j1", [P, D]), s.sb("j2", [P, D]), s.sb("j3", [P, SW]), s.sb("j4", [P, AW])
        hc, hT = s.sb("hc", [P, 2, D]), s.sb("hT", [P, KD, P])
        tmp, hn, hnT = s.sb("tmp", [P, D]), s.sb("hn", [P, 2, D]), s.sb("hnT", [P, KD, P])
        st = s.sb("st", [P, 2, 12])
        half = s.sb("half", [P, 2])
        lg = s.sb("lg", [P, NT, NR])
        ps_t, ps_g, ps_m, ps_r = s.ps("ps_t", [P, 2, 512]), s.ps("ps_g", [P, 512]), s.ps("ps_m", [P, 2, D]), s.ps("ps_r", [P, 512])
        names = ("in_even in_odd x_even x_odd stx_even stx_odd sth_even sth_odd consts w_in smods sq_ready g_step w_ready th1_ready "
                 "z_ready z_flipped z_moved glu_done glu_used th2_ready o_ready ss34 p3 r34 hc_ready hc_part h_flipped h_moved_a h_moved_v mix_done "
                 "ss1 p1 r1 mix_used x2_ready ss2 p2 r2 hn_part hn_ready n_flipped n_moved_a n_moved_v routed lg_used passed halved scaled lg_stored").split()
        S = {n: s.sem(n) for n in names}
        blk = s.block()
        HALF = NPT // 2
        LAST = NT - 1
        NCONST, NW = 8, 3

        class Tile:

            def __init__(self, i, k):
                self.t, self.par, self.q = i * 2 + k, k % 2, i + k // 2
                self.last = isinstance(i, int) and self.t == LAST

            def sem(self, name):
                return S[f"{name}_{'odd' if self.par else 'even'}"]

        def run(eng, step, pairs=HALF - 1):
            around = lambda i, k: [Tile(i, k + d) if not isinstance(i, int) or 0 <= i * 2 + k + d <= LAST else None for d in (-1, 0, 1, 2)]
            step(*around(0, 0))
            with eng.Fori(0, pairs) as i:
                for k in (1, 2):
                    step(*around(i, k))
            for t in range(2 * pairs + 1, NT):
                step(*around(0, t))

        tiles = lambda a: a.rearrange("(n p) d -> p n d", p=P)
        yv, av, x2v, hnv = tiles(T["y"]), tiles(T["attn"]), tiles(T["x2"]), tiles(T["hn2"])
        xp = T["x_prompt"].rearrange("a (n p) d -> p (a n) d", p=P)
        xs = T["x_sample"].rearrange("b t d -> (b t) d")

        @blk.sync
        def _(sp):
            def load_ya(u, first=False):
                if not first:
                    sp.wait_ge(S["hc_ready"], u.t - 1)
                if u.last:
                    for h in range(2):
                        rows = slice(h * NS, (h + 1) * NS)
                        sp.dma_start(y[rows, u.par, :], T["y"][SEQ:SEQ + NS, :]).then_inc(u.sem("in"), 16)
                        sp.dma_start(at[rows, u.par, :], T["attn"][SEQ:SEQ + NS, :]).then_inc(u.sem("in"), 16)
                else:
                    sp.dma_start(y[:, u.par, :].unsqueeze(1), yv[:, bass.ds(u.t, 1), :]).then_inc(u.sem("in"), 16)
                    sp.dma_start(at[:, u.par, :].unsqueeze(1), av[:, bass.ds(u.t, 1), :]).then_inc(u.sem("in"), 16)

            def load_x(u):
                sp.wait_ge(u.sem("stx"), u.q * 16 + 16)
                if u.last:
                    for h in range(2):
                        sp.dma_start(x[h * NS:(h + 1) * NS, u.par, :], xs).then_inc(u.sem("x"), 16)
                else:
                    sp.dma_start(x[:, u.par, :].unsqueeze(1), xp[:, bass.ds(u.t, 1), :]).then_inc(u.sem("x"), 16)

            def store(u):
                sp.wait_ge(S["hn_ready"], u.t + 1)
                sp.dma_start(x2v[:, bass.ds(u.t, 1), :], x[:, u.par, :].unsqueeze(1)).then_inc(u.sem("stx"), 16)
                sp.dma_start(hnv[:, bass.ds(u.t, 1), :], hn[:, u.par, :].unsqueeze(1)).then_inc(u.sem("sth"), 16)

            def step(before, tile, after, after2):
                if after2:
                    load_ya(after2)
                if before:
                    store(before)
                    if after:
                        load_x(after)

            for n in ("stx_even", "stx_odd", "sth_even", "sth_odd"):
                sp.sem_inc(S[n], 16)
            load_ya(Tile(0, 0), True)
            load_ya(Tile(0, 1), True)
            sp.dma_start(ident[:, :], T["ident"]).then_inc(S["consts"], 16)
            for dst, name in ((b_glu, "b_glu"), (g_s, "g_ssm_out"), (g_a, "g_attn_out")):
                sp.dma_start(dst[:, :], T[name][0, :].partition_broadcast(P)).then_inc(S["consts"], 16)
            sp.dma_start(w_glu[:, :, :], T["w_glu"].rearrange("a (k p) n -> p (a k) n", p=P)).then_inc(S["consts"], 16)
            load_x(Tile(0, 0))
            load_x(Tile(0, 1))
            for r in range(3):
                sp.dma_start(mod[:, 0, r, :], mod_row(T, 2 + r)).then_inc(S["consts"], 16)
            sp.dma_start(w_out[:, :, :], T["w_out"].rearrange("a (k p) n -> p (a k) n", p=P)).then_inc(S["w_in"], 16)
            sp.dma_start(w_rt[:, :, 0:NEG_], T["w_group_router"].rearrange("a (k p) n -> p (a k) n", p=P)).then_inc(S["w_in"], 16)
            sp.dma_start(w_rt[:, :, NEG_:], T["w_expert_router"].rearrange("a (k p) g e -> p (a k) (g e)", p=P)).then_inc(S["w_in"], 16)
            run(sp, step, HALF - 2)
            store(Tile(0, LAST))
            sp.wait_ge(S["lg_used"], NT + 1)
            sp.dma_start(T["logits"], lg[:, :, :].rearrange("p t r -> p (t r)")).then_inc(S["lg_stored"], 16)
            sp.wait_ge(S["lg_stored"], 16)
            for n in ("stx", "sth"):
                sp.wait_ge(S[n + "_even"], (HALF + 2) * 16)
                sp.wait_ge(S[n + "_odd"], (HALF + 1) * 16)

        @blk.gpsimd
        def _(pool):
            nc.gpsimd.memset(half[:, :], -0.5).then_inc(S["halved"], 1)
            for r in range(3):
                load_sample_mod(pool, T, mod[:, 1, r, :], 2 + r, S["smods"])
            pool.wait_ge(S["halved"], 1)

            def power(u, src, col, n, scales, part, ready):
                pool.wait_ge(S[src], u.t + 1)
                pool.sem_inc(S["passed"], 1)
                a = st[:, u.par, :]
                for m, c in enumerate(scales):
                    last = nc.gpsimd.tensor_scalar(a[:, col + m:col + m + 1], a[:, col + m:col + m + 1], c, EPS, ALU.mult, ALU.add)
                    last.then_inc(S[part], 1)
                pool.wait_ge(S[part], u.t * len(scales) + len(scales))
                nc.gpsimd.tensor_tensor(a[:, col + n:col + 2 * n], a[:, col:col + n], half[:, 0:n], ALU.pow).then_inc(S[ready], 1)

            def norms_out(u):
                power(u, "ss1", 0, 1, (1.0 / D,), "p1", "r1")
                power(u, "ss2", 2, 1, (1.0 / D,), "p2", "r2")

            def norms_in(u):
                power(u, "ss34", 4, 2, (1.0 / (16 * SW), 1.0 / AW), "p3", "r34")

            def step(before, tile, after, after2):
                if before:
                    norms_out(before)
                if after:
                    norms_in(after)

            norms_in(Tile(0, 0))
            run(pool, step)
            norms_out(Tile(0, LAST))

        @blk.scalar
        def _(act):
            A = nc.scalar.activation

            def gelu(u):
                act.wait_ge(u.sem("in"), (HALF + 2) * 32 if u.last else u.q * 32 + 32)
                A(sq[:, :], y[:, u.par, :], ACT.Square).then_inc(S["sq_ready"], 1)
                act.wait_ge(S["w_ready"], u.t + 1)
                A(th1[:, :], gw[:, :], ACT.Tanh).then_inc(S["th1_ready"], 1)

            def glu(u):
                act.wait_ge(S["glu_used"], u.t + 2)
                A(th2[:, :], gv[:, :], ACT.Tanh, scale=0.5).then_inc(S["th2_ready"], 1)
                A(j4[:, :], at[:, u.par, :], ACT.Square, accum_out=st[:, u.par, 5:6])
                act.wait_ge(S["o_ready"], u.t + 1)
                A(j3[:, :], o4[:, :], ACT.Square, accum_out=st[:, u.par, 4:5]).then_inc(S["ss34"], 1)

            def residual(u):
                act.wait_ge(S["mix_done"], u.t + 1)
                A(j1[:, :], ps_m[:, u.par, :], ACT.Square, accum_out=st[:, u.par, 0:1]).then_inc(S["ss1"], 1)
                act.wait_ge(S["x2_ready"], u.t + 1)
                A(j2[:, :], x[:, u.par, :], ACT.Square, accum_out=st[:, u.par, 2:3]).then_inc(S["ss2"], 1)

            def move(u, dst, flipped, moved):
                act.wait_ge(S[flipped], u.t + 1)
                A(dst[:, 0:4, :], ps_t[:, 0, :].rearrange("p (k n) -> p k n", k=4), ACT.Copy).then_inc(S[moved], 1)

            def step(before, tile, after, after2):
                if before:
                    residual(before)
                if after:
                    glu(after)
                if before:
                    move(before, hnT, "n_flipped", "n_moved_a")
                if after2:
                    gelu(after2)
                if after:
                    move(after, hT, "h_flipped", "h_moved_a")

            gelu(Tile(0, 0))
            glu(Tile(0, 0))
            gelu(Tile(0, 1))
            move(Tile(0, 0), hT, "h_flipped", "h_moved_a")
            run(act, step, HALF - 2)
            residual(Tile(0, LAST))
            move(Tile(0, LAST), hnT, "n_flipped", "n_moved_a")

        @blk.vector
        def _(dve):
            vec = nc.vector

            def gelu(u):
                dve.wait_ge(S["sq_ready"], u.t + 1)
                vec.tensor_scalar(gq[:, :], sq[:, :], GELU_C * 0.044715, GELU_C, ALU.mult, ALU.add).then_inc(S["g_step"], 1)
                dve.wait_ge(S["g_step"], u.t + 1)
                vec.tensor_tensor(gw[:, :], gq[:, :], y[:, u.par, :], ALU.mult).then_inc(S["w_ready"], 1)
                dve.wait_ge(S["th1_ready"], u.t + 1)
                vec.scalar_tensor_tensor(z2[:, u.par, :], th1[:, :], 1.0, y[:, u.par, :], ALU.add, ALU.mult).then_inc(S["z_ready"], 1)

            def move_z(u):
                dve.wait_ge(S["z_flipped"], u.t + 1)
                vec.tensor_copy(zT[:, :, :], ps_t[:, 0, :].rearrange("p (k n) -> p k n", k=4)).then_inc(S["z_moved"], 1)

            def glu(u):
                dve.wait_ge(S["glu_done"], u.t + 1)
                vec.scalar_tensor_tensor(gv[:, :], ps_g[:, :], 0.5, b_glu[:, :], ALU.mult, ALU.add).then_inc(S["glu_used"], 1)
                dve.wait_ge(S["th2_ready"], u.t + 1)
                vec.scalar_tensor_tensor(o4[:, :], th2[:, :], 1.0, z2[:, u.par, :], ALU.add, ALU.mult).then_inc(S["o_ready"], 1)
                dve.wait_ge(S["r34"], u.t + 1)
                vec.scalar_tensor_tensor(hc[:, u.par, 0:SW], o4[:, :], st[:, u.par, 6:7], g_s[:, :], ALU.mult, ALU.mult)
                vec.scalar_tensor_tensor(hc[:, u.par, SW:], at[:, u.par, :], st[:, u.par, 7:8], g_a[:, :], ALU.mult, ALU.mult).then_inc(S["hc_ready"], 1)

            def residual(u):
                kind = 1 if u.last else 0
                dve.wait_ge(S["r1"], u.t + 1)
                vec.scalar_tensor_tensor(tmp[:, :], ps_m[:, u.par, :], st[:, u.par, 1:2], mod[:, kind, 0, :], ALU.mult, ALU.mult).then_inc(S["mix_used"], 1)
                dve.wait_ge(S["mix_used"], u.t + 3)
                dve.wait_ge(u.sem("x"), (HALF + 2) * 16 if u.last else u.q * 16 + 16)
                vec.tensor_tensor(x[:, u.par, :], x[:, u.par, :], tmp[:, :], ALU.add).then_inc(S["x2_ready"], 1)
                dve.wait_ge(S["r2"], u.t + 1)
                dve.wait_ge(u.sem("sth"), u.q * 16 + 16)
                vec.scalar_tensor_tensor(hn[:, u.par, :], x[:, u.par, :], st[:, u.par, 3:4], mod[:, kind, 1, :], ALU.mult, ALU.mult).then_inc(S["hn_part"], 1)
                dve.wait_ge(S["hn_part"], u.t + 1)
                vec.tensor_tensor(hn[:, u.par, :], hn[:, u.par, :], mod[:, kind, 2, :], ALU.add).then_inc(S["hn_ready"], 1)

            def move(u, dst, flipped, moved):
                dve.wait_ge(S[flipped], u.t + 1)
                vec.tensor_copy(dst[:, 4:8, :], ps_t[:, 1, :].rearrange("p (k n) -> p k n", k=4)).then_inc(S[moved], 1)

            def logits(u):
                dve.wait_ge(S["routed"], u.t + 1)
                vec.tensor_copy(lg[:, bass.ds(u.t, 1), :], ps_r[:, 0:NR].unsqueeze(1)).then_inc(S["lg_used"], 1)

            def step(before, tile, after, after2):
                if after:
                    move_z(after)
                if before:
                    residual(before)
                if after:
                    glu(after)
                if before:
                    move(before, hnT, "n_flipped", "n_moved_v")
                if after2:
                    gelu(after2)
                if before:
                    logits(before)
                if after:
                    move(after, hT, "h_flipped", "h_moved_v")

            for n, k in (("glu_used", 1), ("mix_used", 2), ("lg_used", 1)):
                dve.sem_inc(S[n], k)
            first = Tile(0, 0)
            gelu(first)
            dve.wait_ge(S["consts"], NCONST * 16)
            vec.tensor_scalar(g_s[:, :], g_s[:, :], 0.25, None, ALU.mult).then_inc(S["scaled"], 1)
            dve.wait_ge(S["scaled"], 1)
            move_z(first)
            glu(first)
            gelu(Tile(0, 1))
            move(first, hT, "h_flipped", "h_moved_v")
            dve.wait_ge(S["smods"], 3 * 2 * DB * 16)
            run(dve, step, HALF - 2)
            residual(Tile(0, LAST))
            move(Tile(0, LAST), hnT, "n_flipped", "n_moved_v")
            logits(Tile(0, LAST))

        @blk.tensor
        def _(pe):
            def flip(src, u, flipped):
                for k in range(KD):
                    last = nc.tensor.transpose(ps_t[:, k // 4, k % 4 * P:(k % 4 + 1) * P], src[:, u.par, k * P:(k + 1) * P], ident[:, :])
                last.then_inc(S[flipped], 1)

            def glu(u, first=False):
                pe.wait_ge(S["z_ready"], u.t + 1)
                if not first:
                    pe.wait_ge(S["h_moved_a"], u.t)
                for k in range(4):
                    last = nc.tensor.transpose(ps_t[:, 0, k * P:(k + 1) * P], z2[:, u.par, k * P:(k + 1) * P], ident[:, :])
                last.then_inc(S["z_flipped"], 1)
                pe.wait_ge(S["z_moved"], u.t + 1)
                pe.wait_ge(S["glu_used"], u.t + 1)
                for k in range(4):
                    last = nc.tensor.matmul(ps_g[:, :], zT[:, k, :], w_glu[:, k, :], start=(k == 0), stop=(k == 3))
                last.then_inc(S["glu_done"], 1)

            def flip_h(u):
                pe.wait_ge(S["hc_ready"], u.t + 1)
                flip(hc, u, "h_flipped")

            def mix(u, c):
                if c == 0:
                    pe.wait_ge(S["h_moved_a"], u.t + 1)
                    pe.wait_ge(S["h_moved_v"], u.t + 1)
                    pe.wait_ge(S["mix_used"], u.t + 1)
                at_ = slice(c * 512, (c + 1) * 512)
                for k in range(KD):
                    last = nc.tensor.matmul(ps_m[:, u.par, at_], hT[:, k, :], w_out[:, k, at_], start=(k == 0), stop=(k == KD - 1))
                if c == 1:
                    last.then_inc(S["mix_done"], 1)

            def flip_n(u, later=True):
                pe.wait_ge(S["hn_ready"], u.t + 1)
                if later:
                    pe.wait_ge(S["h_moved_v"], u.t + 2)
                flip(hn, u, "n_flipped")

            def route(u):
                pe.wait_ge(S["n_moved_a"], u.t + 1)
                pe.wait_ge(S["n_moved_v"], u.t + 1)
                pe.wait_ge(S["lg_used"], u.t + 1)
                for k in range(KD):
                    last = nc.tensor.matmul(ps_r[:, 0:NR], hnT[:, k, :], w_rt[:, k, :], start=(k == 0), stop=(k == KD - 1))
                last.then_inc(S["routed"], 1)

            def step(before, tile, after, after2):
                if after:
                    glu(after)
                mix(tile, 0)
                if before:
                    flip_n(before)
                mix(tile, 1)
                if before:
                    route(before)
                if after:
                    flip_h(after)

            pe.wait_ge(S["consts"], NCONST * 16)
            glu(Tile(0, 0), True)
            flip_h(Tile(0, 0))
            pe.wait_ge(S["w_in"], NW * 16)
            run(pe, step)
            flip_n(Tile(0, LAST), False)
            route(Tile(0, LAST))


PAIRS = 2 * (SEQ + NS)
NTILE = (PAIRS + NE * (P - 1)) // P
NSLOT = NTILE * P
NSL = 3
U = 4
NSLOT_ALL = NSLOT + 2 * P


def routing(nc, T, top):
    E16 = [P, NT, NE]
    with Stage(nc, top, "rt") as s:
        lg, bias = s.sb("lg", [P, NT, NR]), s.sb("bias", [P, NR])
        ident, before, ones = s.sb("ident", [P, P]), s.sb("before", [P, P]), s.sb("ones", [P, P])
        valid, dump, tokens, tau = s.sb("valid", [P, NT]), s.sb("dump", [P, 2, NT]), s.sb("tokens", [P, NT]), s.sb("tau", [1, NTILE])
        f17 = {n: s.sb(n, [P, NT]) for n in ("mg", "gp", "m1", "m2", "e2", "den", "taken")}
        f68 = {n: s.sb(n, [P, NT, 4]) for n in ("ohg", "eq", "ex", "sel", "tmp", "oh1", "oh2")}
        OH, A, slot, prod = s.sb("OH", [P, 2, NT, NE]), s.sb("A", E16), s.sb("slot", E16), s.sb("prod", E16)
        tp = s.sb("tp", [P, NT + 1, NE])
        nt, end, base = s.sb("nt", [P, NE]), s.sb("end", [P, NE]), s.sb("base", [P, NE])
        sf, su = s.sb("sf", [P, 2, NT]), s.sb("su", [P, 2, NT], U32)
        wts = s.sb("wts", [P, 2, NT])
        zero, smap, tok_u = s.sb("zero", [P, NSLOT_ALL // P]), s.sb("smap", [NTILE, P]), s.sb("tok_u", [P, NTILE], U32)
        cmp, et, et_i = s.sb("cmp", [1, NTILE, NE]), s.sb("et", [1, 3, NTILE]), s.sb("et_i", [1, 3, NTILE], I32)
        et_n = s.sb("et_n", [1, NTILE])
        ps_r, ps_c, ps_s = s.ps("ps_r", [P, 512]), s.ps("ps_c", [P, 512]), s.ps("ps_s", [P, 512])
        (loaded, zeroed, cleared, step, de, exped, hot, counted, slots, scattered, read, turned, tiles_out, stored) = (
            s.sem(n) for n in ("loaded", "zeroed", "cleared", "step", "de", "exped", "hot", "counted", "slots", "scattered",
                               "read", "turned", "tiles_out", "stored"))
        blk = s.block()
        srcs = [(lg[:, :, :].rearrange("p t r -> p (t r)"), T["logits"]), (ident[:, :], T["ident"]), (before[:, :], T["before"]),
                (valid[:, :], T["valid"]), (dump[:, :, :], T["dump"]), (tokens[:, :], T["tokens"]), (tau[:, :], T["tau"]),
                (bias[:, 0:NEG_], T["b_group_router"][0, :].partition_broadcast(P)),
                (bias[:, NEG_:], T["b_expert_router"].rearrange("a g e -> (a g e)").partition_broadcast(P))]

        @blk.sync
        def _(sp):
            for dst, src in srcs:
                sp.dma_start(dst, src).then_inc(loaded, 16)
            sp.wait_ge(zeroed, 1)
            sp.dma_start(T["slotmap"].rearrange("(p n) a -> p (n a)", p=P), zero[:, :]).then_inc(cleared, 16)
            sp.wait_ge(slots, 1)
            sp.dma_start(T["slots"], su[:, :, :].rearrange("p k t -> p (k t)")).then_inc(stored, 16)
            sp.dma_start(T["weights"], wts[:, :, :].rearrange("p k t -> p (k t)")).then_inc(stored, 16)
            sp.wait_ge(scattered, 2 * NT * 16)
            sp.dma_start(smap[:, :], T["slotmap"][0:NSLOT, :].rearrange("(n p) a -> n (p a)", p=P)).then_inc(read, 16)
            sp.wait_ge(tiles_out, 2)
            sp.dma_start(T["tile_tokens"], tok_u[:, :]).then_inc(stored, 16)
            sp.dma_start(T["tile_plan"], et_i[:, :, :]).then_inc(stored, 16)
            sp.wait_ge(stored, 4 * 16)

        @blk.gpsimd
        def _(pool):
            pool.wait_ge(cleared, 16)
            pool.wait_ge(slots, 1)
            for k in range(2):
                for t in range(NT):
                    pool.indirect_dma_start(T["slotmap"], bass.IndirectOffsetOnAxis(su[:, k, t:t + 1], 0), tokens[:, t:t + 1], None).then_inc(scattered, 16)
            pool.wait_ge(scattered, 2 * NT * 16)

        @blk.scalar
        def _(act):
            act.wait_ge(de, 1)
            nc.scalar.activation(f68["ex"][:, :, :], f68["ex"][:, :, :], ACT.Exp).then_inc(exped, 1)
            act.wait_ge(de, 2)
            nc.scalar.activation(f17["e2"][:, :], f17["e2"][:, :], ACT.Exp).then_inc(exped, 1)

        @blk.tensor
        def _(pe):
            pe.wait_ge(hot, 1)
            a = A[:, :, :].rearrange("p t e -> p (t e)")
            nc.tensor.matmul(ps_r[:, 0:NT * NE], before[:, :], a, start=True, stop=True)
            nc.tensor.matmul(ps_c[:, 0:NT * NE], ones[:, :], a, start=True, stop=True).then_inc(counted, 1)
            pe.wait_ge(read, 16)
            nc.tensor.transpose(ps_s[:, 0:NTILE], smap[:, :], ident[0:NTILE, 0:NTILE]).then_inc(turned, 1)

        @blk.vector
        def _(dve):
            vec = nc.vector
            st_ = Steps(dve, step)
            tt = lambda o, a, b, op: st_.then(vec.tensor_tensor(o, a, b, op))
            ts = lambda o, a, x, y, p, q: st_.then(vec.tensor_scalar(o, a, x, y, p, q))
            red = lambda o, a, op: st_.then(vec.tensor_reduce(o, a, AX.X, op))
            vec.memset(zero[:, :], 0.0).then_inc(zeroed, 1)
            st_.then(vec.memset(ones[:, :], 1.0))
            dve.wait_ge(loaded, len(srcs) * 16)
            mg, gp, m1, m2, e2, den, taken = (f17[n][:, :] for n in ("mg", "gp", "m1", "m2", "e2", "den", "taken"))
            ohg, eq, ex, sel, tmp, oh1, oh2 = (f68[n] for n in ("ohg", "eq", "ex", "sel", "tmp", "oh1", "oh2"))
            over4 = lambda a: a.unsqueeze(2).broadcast_to([P, NT, 4])

            def first_max(out, vals, m):
                red(m, vals, ALU.max)
                tt(eq[:, :, :], vals, over4(m), ALU.is_equal)
                st_.then(vec.tensor_copy(out[:, :, 0:1], eq[:, :, 0:1]))
                st_.then(vec.tensor_copy(taken.unsqueeze(2), eq[:, :, 0:1]))
                for k in range(1, 4):
                    tt(out[:, :, k:k + 1], eq[:, :, k:k + 1], taken.unsqueeze(2), ALU.is_gt)
                    if k < 3:
                        tt(taken.unsqueeze(2), eq[:, :, k:k + 1], taken.unsqueeze(2), ALU.max)

            tt(lg[:, :, :], lg[:, :, :], bias[:, :].unsqueeze(1).broadcast_to([P, NT, NR]), ALU.add)
            gl, el = lg[:, :, 0:NEG_], lg[:, :, NEG_:]
            first_max(ohg, gl, mg)
            vec.tensor_tensor(ex[:, :, :], gl, over4(mg), ALU.subtract).then_inc(de, 1)
            dve.wait_ge(exped, 1)
            red(gp, ex[:, :, :], ALU.add)
            st_.then(vec.reciprocal(gp, gp))
            for g in range(NEG_):
                dst = sel if g == 0 else tmp
                tt(dst[:, :, :], el[:, :, g * EPG:(g + 1) * EPG], over4(ohg[:, :, g]), ALU.mult)
                if g:
                    tt(sel[:, :, :], sel[:, :, :], tmp[:, :, :], ALU.add)
            first_max(oh1, sel[:, :, :], m1)
            st_.then(vec.scalar_tensor_tensor(tmp[:, :, :], oh1[:, :, :], MASKED, sel[:, :, :], ALU.mult, ALU.add))
            first_max(oh2, tmp[:, :, :], m2)
            vec.tensor_tensor(e2, m2, m1, ALU.subtract).then_inc(de, 1)
            for k, oh in enumerate((oh1, oh2)):
                o = OH[:, k, :, :].rearrange("p t (g e) -> p t g e", g=NEG_)
                wide = [P, NT, NEG_, EPG]
                tt(o, ohg[:, :, :].unsqueeze(3).broadcast_to(wide), oh[:, :, :].unsqueeze(2).broadcast_to(wide), ALU.mult)
                tt(OH[:, k, :, :], OH[:, k, :, :], valid[:, :].unsqueeze(2).broadcast_to(E16), ALU.mult)
            vec.tensor_tensor(A[:, :, :], OH[:, 0, :, :], OH[:, 1, :, :], ALU.add).then_inc(hot, 1)
            dve.wait_ge(exped, 2)
            ts(den, e2, 1.0, None, ALU.add, ALU.bypass)
            st_.then(vec.reciprocal(den, den))
            tt(wts[:, 0, :], gp, den, ALU.mult)
            tt(wts[:, 1, :], wts[:, 0, :], e2, ALU.mult)
            dve.wait_ge(counted, 1)
            st_.then(vec.memset(tp[:, 0, :], 0.0))
            for t in range(NT):
                tt(tp[:, t + 1, :], tp[:, t, :], ps_c[:, t * NE:(t + 1) * NE], ALU.add)
            ts(nt[:, :], tp[:, NT, :], 1.0 / P, (P - 1.0) / P - 0.5 + 0.5 / P, ALU.mult, ALU.add)
            ts(nt[:, :], nt[:, :], MAGIC, None, ALU.add, ALU.bypass)
            ts(nt[:, :], nt[:, :], -MAGIC, None, ALU.add, ALU.bypass)
            st_.then(vec.tensor_tensor_scan(end[:, :], ones[:, 0:NE], nt[:, :], 0.0, ALU.mult, ALU.add))
            tt(base[:, :], end[:, :], nt[:, :], ALU.subtract)
            ts(base[:, :], base[:, :], float(P), None, ALU.mult, ALU.bypass)
            tt(slot[:, :, :], tp[:, 0:NT, :], ps_r[:, 0:NT * NE].rearrange("p (t e) -> p t e", t=NT), ALU.add)
            tt(slot[:, :, :], slot[:, :, :], base[:, :].unsqueeze(1).broadcast_to(E16), ALU.add)
            for k in range(2):
                tt(prod[:, :, :], OH[:, k, :, :], slot[:, :, :], ALU.mult)
                red(sf[:, k, :], prod[:, :, :], ALU.add)
            tt(sf[:, :, :], sf[:, :, :], dump[:, :, :], ALU.add)
            vec.tensor_copy(su[:, :, :], sf[:, :, :]).then_inc(slots, 1)
            tt(cmp[:, :, :], tau[:, :].unsqueeze(2).broadcast_to([1, NTILE, NE]), end[0:1, :].unsqueeze(1).broadcast_to([1, NTILE, NE]), ALU.is_ge)
            expert, fresh, slot_w = (et[:, n, :] for n in range(3))
            red(expert, cmp[:, :, :], ALU.add)
            ts(expert, expert, NE - 1.0, None, ALU.min, ALU.bypass)
            st_.then(vec.memset(fresh[:, 0:1], 1.0))
            tt(fresh[:, 1:], expert[:, 1:], expert[:, 0:NTILE - 1], ALU.not_equal)
            st_.then(vec.tensor_tensor_scan(et_n[:, :], ones[0:1, 0:NTILE], fresh, -1.0, ALU.mult, ALU.add))
            ts(slot_w, et_n[:, :], 1.0 / NSL, 0.5 / NSL - 0.5, ALU.mult, ALU.add)
            ts(slot_w, slot_w, MAGIC, None, ALU.add, ALU.bypass)
            ts(slot_w, slot_w, -MAGIC, None, ALU.add, ALU.bypass)
            st_.then(vec.scalar_tensor_tensor(slot_w, slot_w, -float(NSL), et_n[:, :], ALU.mult, ALU.add))
            vec.tensor_copy(et_i[:, :, :], et[:, :, :]).then_inc(tiles_out, 1)
            dve.wait_ge(turned, 1)
            vec.tensor_copy(tok_u[:, :], ps_s[:, 0:NTILE]).then_inc(tiles_out, 1)


def experts(nc, T, top):
    with Stage(nc, top, "ex") as s:
        ident, tok, plan = s.sb("ident", [P, P]), s.sb("tok", [P, NTILE], U32), s.sb("plan", [1, 3, NTILE], I32)
        wgu, wd = s.sb("wgu", [P, NSL * KD * 2 * DE]), s.sb("wd", [P, NSL * 2 * D])
        idx = s.sb("idx", [P, U], U32)
        x, xT = s.sb("x", [P, U, D]), s.sb("xT", [P, KD, P])
        th, sg, a, aT = s.sb("th", [P, DE]), s.sb("sg", [P, DE]), s.sb("a", [P, DE]), s.sb("aT", [P, 2, P])
        o = s.sb("o", [P, 2, D])
        ps_t, ps_h, ps_a, ps_o = s.ps("ps_t", [P, 2, 512]), s.ps("ps_h", [P, 2, 512]), s.ps("ps_a", [P, 512]), s.ps("ps_o", [P, D])
        names = ("loaded picked passed x_flipped x_moved_a x_moved_v gu_done th_ready "
                 "sg_ready a_ready a_flipped a_moved d_done o_out_a o_out_v st_even st_odd").split()
        S = {n: s.sem(n) for n in names}
        blk = s.block()
        for n in range(U):
            for name in ("gu", "d", "x"):
                S[name, n] = s.sem(f"{name}{n}")
        HT = NTILE // 2
        sem = lambda name, par: S[f"{name}_{'odd' if par else 'even'}"]
        gv, uv = (T[n].rearrange("a e (k p) f -> p (a e) k f", p=P) for n in ("w_exp_gate", "w_exp_up"))
        dv = T["w_exp_down"].rearrange("a e (k p) n -> p (a e) k n", p=P)
        gu_slots = wgu[:, :].rearrange("p (s k f) -> p s k f", s=NSL, k=KD)
        d_slots = wd[:, :].rearrange("p (s k f) -> p s k f", s=NSL, k=2)
        ov = T["moe"].rearrange("(n p) d -> p n d", p=P)

        @blk.sync
        def _(sp):
            sp.dma_start(ident[:, :], T["ident"]).then_inc(S["loaded"], 16)
            sp.dma_start(tok[:, :], T["tile_tokens"]).then_inc(S["loaded"], 16)
            sp.dma_start(plan[:, :, :], T["tile_plan"]).then_inc(S["loaded"], 16)
            sp.wait_ge(S["loaded"], 48)
            with sp.Fori(0, NTILE // U) as i:
                for n in range(U):
                    t = i * U + n
                    e = sp.value_load(plan[0:1, 0, bass.ds(t, 1)], min_val=0, max_val=NE - 1)
                    fresh = sp.value_load(plan[0:1, 1, bass.ds(t, 1)], min_val=0, max_val=1)
                    slot = sp.value_load(plan[0:1, 2, bass.ds(t, 1)], min_val=0, max_val=NSL - 1)
                    sp.wait_ge(S["gu_done"], t + 1)
                    for half, view in enumerate((gv, uv)):
                        sp.dma_start(gu_slots[:, bass.ds(slot, 1), :, half * DE:(half + 1) * DE], view[:, bass.ds(e, 1), :, :], cond=fresh).then_inc(S["gu", n], 16)
                    sp.wait_ge(S["d_done"], t + 1)
                    sp.dma_start(d_slots[:, bass.ds(slot, 1), :, :], dv[:, bass.ds(e, 1), :, :], cond=fresh).then_inc(S["d", n], 16)

        @blk.gpsimd
        def _(pool):
            pool.wait_ge(S["loaded"], 48)

            def gather(t, n):
                nc.gpsimd.tensor_copy(idx[:, n:n + 1], tok[:, bass.ds(t, 1)]).then_inc(S["picked"], 1)
                pool.wait_ge(S["picked"], t + 1)
                pool.sem_inc(S["passed"], 1)
                pool.indirect_dma_start(x[:, n, :], None, T["hn2"], bass.IndirectOffsetOnAxis(idx[:, n:n + 1], 0)).then_inc(S["x", n], 16)

            for n in range(U):
                gather(n, n)
            with pool.Fori(0, NTILE // U - 1) as i:
                for n in range(U):
                    pool.wait_ge(S["x_flipped"], i * U + n + 1)
                    pool.sem_inc(S["passed"], 1)
                    gather(i * U + n + U, n)

        @blk.scalar
        def _(act):
            act.sem_inc(S["o_out_a"], 1)
            act.sem_inc(S["st_even"], 16)
            act.sem_inc(S["st_odd"], 16)
            A = nc.scalar.activation

            def move_x(t):
                act.wait_ge(S["x_flipped"], t + 1)
                A(xT[:, 0:4, :], ps_t[:, 0, :].rearrange("p (k n) -> p k n", k=4), ACT.Copy).then_inc(S["x_moved_a"], 1)

            def gate(t, par):
                act.wait_ge(S["gu_done"], t + NSL + 1)
                A(th[:, :], ps_h[:, par, 0:DE], ACT.Tanh, scale=0.5).then_inc(S["th_ready"], 1)

            def move_a(t):
                act.wait_ge(S["a_flipped"], t + 1)
                A(aT[:, :, :], ps_a[:, 0:2 * P].rearrange("p (k n) -> p k n", k=2), ACT.Copy, scale=0.5).then_inc(S["a_moved"], 1)

            def out(t, par, q):
                act.wait_ge(S["d_done"], t + NSL + 1)
                act.wait_ge(sem("st", par), q * 16 + 16)
                A(o[:, par, 0:512], ps_o[:, 0:512], ACT.Copy).then_inc(S["o_out_a"], 1)
                act.wait_ge(S["o_out_v"], t + 2)
                act.wait_ge(S["o_out_a"], t + 2)
                act.dma_start(ov[:, bass.ds(t, 1), :], o[:, par, :].unsqueeze(1)).then_inc(sem("st", par), 16)

            move_x(0)
            gate(0, 0)
            move_x(1)
            move_a(0)
            def step(t, k, i):
                par = k % 2
                gate(t, par)
                move_x(t + 1)
                out(t - 1, 1 - par, i * (U // 2) + (k - 1) // 2)
                move_a(t)

            with act.Fori(0, NTILE // U - 1) as i:
                for k in range(1, U + 1):
                    step(i * U + k, k, i)
            for k in range(1, U - 1):
                step(NTILE - U + k, k, NTILE // U - 1)
            gate(NTILE - 1, 1)
            out(NTILE - 2, 0, HT - 1)
            move_a(NTILE - 1)
            out(NTILE - 1, 1, HT - 1)
            act.wait_ge(S["st_even"], (HT + 1) * 16)
            act.wait_ge(S["st_odd"], (HT + 1) * 16)

        @blk.vector
        def _(dve):
            vec = nc.vector
            dve.sem_inc(S["o_out_v"], 1)

            def move_x(t):
                dve.wait_ge(S["x_flipped"], t + 1)
                vec.tensor_copy(xT[:, 4:8, :], ps_t[:, 1, :].rearrange("p (k n) -> p k n", k=4)).then_inc(S["x_moved_v"], 1)

            def gate(t, par):
                dve.wait_ge(S["th_ready"], t + 1)
                vec.scalar_tensor_tensor(sg[:, :], th[:, :], 1.0, ps_h[:, par, 0:DE], ALU.add, ALU.mult).then_inc(S["sg_ready"], 1)
                dve.wait_ge(S["sg_ready"], t + 1)
                vec.tensor_tensor(a[:, :], sg[:, :], ps_h[:, par, DE:], ALU.mult).then_inc(S["a_ready"], 1)

            def out(t, par, q):
                dve.wait_ge(S["d_done"], t + NSL + 1)
                dve.wait_ge(sem("st", par), q * 16 + 16)
                vec.tensor_copy(o[:, par, 512:], ps_o[:, 512:]).then_inc(S["o_out_v"], 1)

            move_x(0)
            gate(0, 0)
            move_x(1)
            def step(t, k, i):
                par = k % 2
                gate(t, par)
                move_x(t + 1)
                out(t - 1, 1 - par, i * (U // 2) + (k - 1) // 2)

            with dve.Fori(0, NTILE // U - 1) as i:
                for k in range(1, U + 1):
                    step(i * U + k, k, i)
            for k in range(1, U - 1):
                step(NTILE - U + k, k, NTILE // U - 1)
            gate(NTILE - 1, 1)
            out(NTILE - 2, 0, HT - 1)
            out(NTILE - 1, 1, HT - 1)

        @blk.tensor
        def _(pe):
            pe.sem_inc(S["gu_done"], NSL)
            pe.sem_inc(S["d_done"], NSL)
            pe.wait_ge(S["loaded"], 48)

            def flip_x(t, n, q, first=False):
                pe.wait_ge(S["x", n], q * 16 + 16)
                if not first:
                    pe.wait_ge(S["x_moved_a"], t)
                    pe.wait_ge(S["x_moved_v"], t)
                for k in range(KD):
                    last = nc.tensor.transpose(ps_t[:, k // 4, k % 4 * P:(k % 4 + 1) * P], x[:, n, k * P:(k + 1) * P], ident[:, :])
                last.then_inc(S["x_flipped"], 1)

            def gate_up(t, n, q, slot):
                pe.wait_ge(S["x_moved_a"], t + 1)
                pe.wait_ge(S["x_moved_v"], t + 1)
                pe.wait_ge(S["gu", n], q * 32 + 32)
                for k in range(KD):
                    last = nc.tensor.matmul(ps_h[:, n % 2, :], xT[:, k, :], wgu[:, bass.ds((slot * KD + k) * 2 * DE, 2 * DE)],
                                            start=(k == 0), stop=(k == KD - 1))
                last.then_inc(S["gu_done"], 1)

            def flip_a(t):
                pe.wait_ge(S["a_ready"], t + 1)
                for k in range(2):
                    last = nc.tensor.transpose(ps_a[:, k * P:(k + 1) * P], a[:, k * P:(k + 1) * P], ident[:, :])
                last.then_inc(S["a_flipped"], 1)

            def down(t, n, q, slot):
                pe.wait_ge(S["a_moved"], t + 1)
                pe.wait_ge(S["d", n], q * 16 + 16)
                pe.wait_ge(S["o_out_a"], t + 1)
                pe.wait_ge(S["o_out_v"], t + 1)
                for c in range(2):
                    for k in range(2):
                        last = nc.tensor.matmul(ps_o[:, c * 512:(c + 1) * 512], aT[:, k, :], wd[:, bass.ds((slot * 2 + k) * D + c * 512, 512)], start=(k == 0), stop=(k == 1))
                last.then_inc(S["d_done"], 1)

            def slot_of(t):
                return pe.value_load(plan[0:1, 2, bass.ds(t, 1)], min_val=0, max_val=NSL - 1)

            def steps(t0, i, n):
                slot = {0: slot_of(t0), 1: slot_of(t0 + 1)}
                for k in range(1, n + 1):
                    gate_up(t0 + k, k % U, i + k // U, slot[k])
                    if k < n or n < U:
                        slot[k + 1] = slot_of(t0 + k + 1)
                    flip_x(t0 + k + 1, (k + 1) % U, i + (k + 1) // U)
                    down(t0 + k - 1, k - 1, i, slot[k - 1])
                    flip_a(t0 + k)
                return slot

            flip_x(0, 0, 0, True)
            gate_up(0, 0, 0, slot_of(0))
            flip_x(1, 1, 0)
            flip_a(0)
            with pe.Fori(0, NTILE // U - 1) as i:
                steps(i * U, i, U)
            last_i = NTILE // U - 1
            slot = steps(NTILE - U, last_i, U - 2)
            gate_up(NTILE - 1, U - 1, last_i, slot[U - 1])
            down(NTILE - 2, U - 2, last_i, slot[U - 2])
            flip_a(NTILE - 1)
            down(NTILE - 1, U - 1, last_i, slot[U - 1])


def combine(nc, T, top):
    with Stage(nc, top, "cb") as s:
        slots, wts = s.sb("slots", [P, 2, NT], U32), s.sb("wts", [P, 2, NT])
        G2, idx = s.sb("G2", [P, 2, D]), s.sb("idx", [P, 2, 2], U32)
        r, x = s.sb("r", [P, 2, 2, D]), s.sb("x", [P, 2, D])
        f1, f, j, g = s.sb("f1", [P, D]), s.sb("f", [P, D]), s.sb("j", [P, D]), s.sb("g", [P, D])
        o = s.sb("o", [P, 2, D])
        st, half = s.sb("st", [P, 4]), s.sb("half", [P, 1])
        names = "loaded picked smods halved r_even r_odd x_even x_odd step1 f_ready squared passed p1 rstd g_ready o_ready st_even st_odd".split()
        S = {n: s.sem(n) for n in names}
        blk = s.block()
        HALF, LAST = NPT // 2, NT - 1
        sem = lambda name, par: S[f"{name}_{'odd' if par else 'even'}"]
        x2v = T["x2"].rearrange("(n p) d -> p n d", p=P)
        ov = T["o_y_prompt"].rearrange("a (n p) d -> p (a n) d", p=P)

        @blk.sync
        def _(sp):
            def load(t, par):
                sp.dma_start(x[:, par, :].unsqueeze(1), x2v[:, bass.ds(t, 1), :]).then_inc(sem("x", par), 16)

            sp.dma_start(slots[:, :, :].rearrange("p k t -> p (k t)"), T["slots"]).then_inc(S["loaded"], 16)
            sp.dma_start(wts[:, :, :].rearrange("p k t -> p (k t)"), T["weights"]).then_inc(S["loaded"], 16)
            sp.dma_start(G2[:, 0, :], mod_row(T, 5)).then_inc(S["loaded"], 16)
            load(0, 0)
            load(1, 1)
            sp.sem_inc(S["st_even"], 16)
            sp.sem_inc(S["st_odd"], 16)
            load_sample_mod(sp, T, G2[:, 1, :], 5, S["smods"])

            def store(t, par):
                sp.wait_ge(S["o_ready"], t + 1)
                sp.dma_start(ov[:, bass.ds(t, 1), :], o[:, par, :].unsqueeze(1)).then_inc(sem("st", par), 16)

            with sp.Fori(0, HALF - 1) as i:
                for par in range(2):
                    store(i * 2 + par, par)
                    load(i * 2 + par + 2, par)
            store(NPT - 2, 0)
            load(LAST, 0)
            store(NPT - 1, 1)
            sp.wait_ge(S["o_ready"], NT)
            sp.dma_start(T["o_y_sample"].rearrange("b t d -> (b t) d"), o[0:NS, 0, :]).then_inc(S["st_even"], 16)
            sp.wait_ge(S["st_even"], (HALF + 2) * 16)
            sp.wait_ge(S["st_odd"], (HALF + 1) * 16)

        @blk.gpsimd
        def _(pool):
            nc.gpsimd.memset(half[:, :], -0.5).then_inc(S["halved"], 1)
            pool.wait_ge(S["halved"], 1)
            pool.wait_ge(S["loaded"], 48)

            def gather(t, par, rows=P):
                nc.gpsimd.tensor_copy(idx[0:rows, par, :], slots[0:rows, :, bass.ds(t, 1)].rearrange("p k a -> p (k a)")).then_inc(S["picked"], 1)
                pool.wait_ge(S["picked"], t + 1)
                pool.sem_inc(S["passed"], 1)
                for k in range(2):
                    pool.indirect_dma_start(r[0:rows, par, k, :], None, T["moe"],
                                            bass.IndirectOffsetOnAxis(idx[0:rows, par, k:k + 1], 0)).then_inc(sem("r", par), 16)

            def power(t, rows=P):
                pool.wait_ge(S["squared"], t + 1)
                pool.sem_inc(S["passed"], 1)
                nc.gpsimd.tensor_scalar(st[0:rows, 1:2], st[0:rows, 0:1], 1.0 / D, EPS, ALU.mult, ALU.add).then_inc(S["p1"], 1)
                pool.wait_ge(S["p1"], t + 1)
                nc.gpsimd.tensor_tensor(st[0:rows, 2:3], st[0:rows, 1:2], half[0:rows, :], ALU.pow).then_inc(S["rstd"], 1)

            gather(0, 0)
            gather(1, 1)
            with pool.Fori(0, HALF - 1) as i:
                for par in range(2):
                    t = i * 2 + par
                    power(t)
                    gather(t + 2, par)
            power(NPT - 2)
            gather(LAST, 0, NS)
            power(NPT - 1)
            power(LAST, NS)

        @blk.scalar
        def _(act):
            def square(t, rows=P):
                act.wait_ge(S["f_ready"], t + 1)
                nc.scalar.activation(j[0:rows, :], f[0:rows, :], ACT.Square, accum_out=st[0:rows, 0:1]).then_inc(S["squared"], 1)

            with act.Fori(0, NPT) as t:
                square(t)
            square(LAST, NS)

        @blk.vector
        def _(dve):
            vec = nc.vector
            dve.wait_ge(S["loaded"], 48)

            def tile_(t, par, q, rows=P, kind=0):
                R = slice(0, rows)
                dve.wait_ge(sem("r", par), q * 32 + 32)
                vec.tensor_scalar(f1[R, :], r[R, par, 0, :], wts[R, 0, bass.ds(t, 1)], None, ALU.mult).then_inc(S["step1"], 1)
                dve.wait_ge(S["step1"], t + 1)
                vec.scalar_tensor_tensor(f[R, :], r[R, par, 1, :], wts[R, 1, bass.ds(t, 1)], f1[R, :], ALU.mult, ALU.add).then_inc(S["f_ready"], 1)
                dve.wait_ge(S["rstd"], t + 1)
                vec.scalar_tensor_tensor(g[R, :], f[R, :], st[R, 2:3], G2[R, kind, :], ALU.mult, ALU.mult).then_inc(S["g_ready"], 1)
                dve.wait_ge(S["g_ready"], t + 1)
                dve.wait_ge(sem("x", par), q * 16 + 16)
                dve.wait_ge(sem("st", par), q * 16 + 16)
                vec.tensor_tensor(o[R, par, :], g[R, :], x[R, par, :], ALU.add).then_inc(S["o_ready"], 1)

            with dve.Fori(0, HALF) as i:
                for par in range(2):
                    tile_(i * 2 + par, par, i)
            dve.wait_ge(S["smods"], 2 * DB * 16)
            tile_(LAST, 0, HALF, NS, 1)


def constants():
    q = np.arange(P)
    swap = np.zeros((P, P), np.float32)
    swap[q, (q + NST) % P] = 1
    hsel = np.zeros((NH, NKV, P), np.float32)
    for r in range(P):
        for kv in range(NKV):
            hsel[kv * GQ + r // DT % GQ, kv, r] = 1
    valid = np.ones((P, NT), np.float32)
    valid[NS:, NT - 1] = 0
    dump = np.zeros((P, 2, NT), np.float32)
    for k in range(2):
        dump[NS:, k, NT - 1] = NSLOT + k * P + q[NS:]
    return {"ident": np.eye(P, dtype=np.float32), "swap": swap, "sgn": np.where(q < NST, 1, -1).astype(np.float32)[:, None],
            "onehot": bucket_onehot(), "hsel": hsel, "before": (q[:, None] < q[None, :]).astype(np.float32), "valid": valid, "dump": dump,
            "tokens": (np.arange(NT)[None, :] * P + q[:, None]).astype(np.float32), "tau": np.arange(NTILE, dtype=np.float32)[None, :]}


SCRATCH = {"mods": ((1 + DB, 6, D), F32), "proj": ((TOK, INW), F32), "rec": ((NG, P, RECW), F32),
           "hpre": ((P, NG * DB), F32), "r8": ((P, NG), F32), "y": ((TOK, SW), F32), "bias_rows": ((P, RB), F32),
           "attn": ((TOK, AW), F32), "x2": ((TOK, D), F32), "hn2": ((TOK, D), F32), "logits": ((P, NT * NR), F32),
           "slotmap": ((NSLOT_ALL, 1), F32), "slots": ((P, 2 * NT), U32), "weights": ((P, 2 * NT), F32),
           "tile_tokens": ((P, NTILE), U32), "tile_plan": ((1, 3, NTILE), I32), "moe": ((NSLOT, D), F32)}


def hybrid_layer(nc, T):
    for name, (shape, dt) in SCRATCH.items():
        T[name] = nc.dram_tensor(f"scratch_{name}", shape, dt).ap()
    with Semaphores(nc) as top:
        modulation(nc, T, top)
        projection(nc, T, top)
        s5_tables(nc, T, top)
        s5(nc, T, top)
        attention_bias(nc, T, top)
        prompt_attention(nc, T, top)
        sample_attention(nc, T, top)
    with Semaphores(nc) as top:
        mixing(nc, T, top)
        routing(nc, T, top)
        experts(nc, T, top)
        combine(nc, T, top)


INS = ["x_prompt", "x_sample", "cache_k", "cache_v", "state_ssm_re", "state_ssm_im", "c_prompt", "c_sample",
       "rel_bias_table", "w_ada", "b_ada", "g_pre_mix", "g_post_mix", "g_pre_ffn", "g_post_ffn", "w_in",
       "ssm_lam_re", "ssm_lam_im", "ssm_log_dt", "ssm_b_re", "ssm_b_im", "ssm_c_re", "ssm_c_im", "ssm_d",
       "w_glu", "b_glu", "attn_sinks", "g_ssm_out", "g_attn_out", "w_out", "w_group_router", "b_group_router",
       "w_expert_router", "b_expert_router", "w_exp_gate", "w_exp_up", "w_exp_down"]
OUTS = [("y_prompt", (1, SEQ, D)), ("y_sample", (DB, DT, D)),
        ("k_prompt", (1, 1, WIN, NKV, HD)), ("v_prompt", (1, 1, WIN, NKV, HD)),
        ("ssm_re_prompt", (1, 1, NG, NST)), ("ssm_im_prompt", (1, 1, NG, NST)),
        ("k_sample", (1, DB, WIN, NKV, HD)), ("v_sample", (1, DB, WIN, NKV, HD)),
        ("ssm_re_sample", (1, DB, NG, NST)), ("ssm_im_sample", (1, DB, NG, NST))]


def kernel(**inputs):
    import concourse.bacc as bacc
    from concourse.bass_utils import run_bass_kernel_spmd

    nc = bacc.Bacc("TRN2", target_bir_lowering=False, num_devices=1)
    arrays, T = {}, {}
    for name, a in {**{n: inputs[n] for n in INS}, **constants()}.items():
        a = np.ascontiguousarray(a)
        arrays[f"in_{name}_dram"] = a
        T[name] = nc.dram_tensor(f"in_{name}_dram", a.shape, mybir.dt.from_np(a.dtype), kind="ExternalInput").ap()
    for name, shape in OUTS:
        T["o_" + name] = nc.dram_tensor(f"out_{name}_dram", shape, F32, kind="ExternalOutput").ap()
    hybrid_layer(nc, T)
    r = run_bass_kernel_spmd(nc, [arrays], core_ids=[0])
    return tuple(r.results[0][f"out_{name}_dram"] for name, _ in OUTS)
```

```python
import math
from contextlib import ExitStack
import numpy as np
import concourse.bass as bass
from concourse import mybir

F32 = mybir.dt.float32
F32R = mybir.dt.float32r
BF16 = mybir.dt.bfloat16
I32 = mybir.dt.int32
U32 = mybir.dt.uint32
ALU = mybir.AluOpType
ACT = mybir.ActivationFunctionType
AX = mybir.AxisListType

P = 128
D = 1024
KD = D // P
SEQ = 2048
DB, DT = 8, 8
NS = DB * DT
NPT = SEQ // P
NT = NPT + 1
TOK = NT * P
SW = 512
AW = 512
KVW = 128
INW = SW + AW + 2 * KVW
HD = 64
NG, GC, NST = 32, 16, 64
L = 8
NCH = SEQ // L
WIN = 128
NBUCKET = 32
NH, NKV, GQ = 8, 2, 4
NE, EPG, NEG_ = 16, 4, 4
DE = 256
EPS = 1e-6
MASKED = -1e30


class Semaphores:

    def __init__(self, nc):
        self.nc, self.held = nc, []

    def __enter__(self):
        return self

    def get(self, name):
        self.held.append(self.nc.alloc_semaphore(name=name))
        return self.held[-1]

    def __exit__(self, *a):
        self.nc.all_engine_barrier()
        self.nc.clear_and_free_semaphores(self.held)
        self.nc.all_engine_barrier()


class Stage:

    def __init__(self, nc, top, tag):
        self.nc, self.top, self.tag, self.stack = nc, top, tag, ExitStack()

    def __enter__(self):
        return self

    def __exit__(self, *a):
        self.stack.close()

    def sb(self, name, shape, dt=F32):
        return self.stack.enter_context(self.nc.sbuf_tensor(f"{self.tag}_{name}", shape, dt))

    def ps(self, name, shape, dt=F32):
        return self.stack.enter_context(self.nc.psum_tensor(f"{self.tag}_{name}", shape, dt))

    def sem(self, name):
        return self.top.get(f"{self.tag}_{name}")

    def block(self):
        return self.stack.enter_context(self.nc.Block())


class Steps:

    def __init__(self, eng, sem):
        self.eng, self.sem, self.base, self.n = eng, sem, 0, 0

    def then(self, ins):
        ins.then_inc(self.sem, 1)
        self.n += 1
        self.eng.wait_ge(self.sem, self.base + self.n)

    def mark(self, ins):
        ins.then_inc(self.sem, 1)
        self.n += 1


def three_products(nc, out, hi, lo, w_hi, w_lo, first, final):
    nc.tensor.matmul(out, hi, w_hi, start=first, stop=False)
    nc.tensor.matmul(out, hi, w_lo, start=False, stop=False)
    return nc.tensor.matmul(out, lo, w_hi, start=False, stop=final)


class InputWeights:

    def __init__(self, held):
        self.hi, self.lo = held.sb("hi", [P, KD, INW], F32R), held.sb("lo", [P, KD, INW], F32R)
        self.raw = None
        self.even, self.odd, self.rounded, self.rest = (held.sem(n) for n in ("w_even", "w_odd", "rounded", "rest"))

    def load(self, act, T, k):
        arrived = self.odd if k % 2 else self.even
        src, dst = T["w_in"][0, k * P:(k + 1) * P, :], self.raw[:, k % 2, :]
        q_in, q_at = (a[:, SW:SW + AW] for a in (src, dst))
        act.dma_start(dst[:, 0:SW], src[:, 0:SW]).then_inc(arrived, 16)
        for kv in range(NKV):
            act.dma_start(q_at.rearrange("p (g k d) -> p g k d", g=GQ, k=NKV)[:, :, kv, :],
                          q_in.rearrange("p (k g d) -> p g k d", g=GQ, k=NKV)[:, :, kv, :]).then_inc(arrived, 16)
        act.dma_start(dst[:, SW + AW:], src[:, SW + AW:]).then_inc(arrived, 16)

    def round(self, nc, act, T):
        self.load(act, T, 0)
        self.load(act, T, 1)
        for k in range(KD):
            act.wait_ge(self.odd if k % 2 else self.even, (k // 2 + 1) * 64)
            nc.scalar.activation(self.hi[:, k, :], self.raw[:, k % 2, :], ACT.Copy).then_inc(self.rounded, 1)
            if k + 2 < KD:
                act.wait_ge(self.rest, k + 1)
                self.load(act, T, k + 2)

    def subtract(self, nc, pool):
        for k in range(KD):
            pool.wait_ge(self.rounded, k + 1)
            nc.gpsimd.tensor_tensor(self.lo[:, k, :], self.raw[:, k % 2, :], self.hi[:, k, :].bitcast(F32), ALU.subtract).then_inc(self.rest, 1)
        pool.wait_ge(self.rest, KD)


def modulation(nc, T, top, win):
    NR = 1 + DB
    NCK = 6 * D // 512
    with Stage(nc, top, "mod") as s:
        c_in, c_act = s.sb("c_in", [NR, D]), s.sb("c_act", [NR, D])
        cT = s.sb("cT", [P, KD, NR])
        ident = s.sb("ident", [P, P])
        w = s.sb("w", [P, 2, KD, 512])
        gains = s.sb("gains", [NR, 4, D])
        mod = s.sb("mod", [NR, 6 * D])
        win.raw = s.sb("w_in", [P, 2, INW])
        ps_t, ps_m = s.ps("ps_t", [P, KD, 16]), s.ps("ps_m", [P, 2, 512])
        c_loaded, consts_loaded, c_ready = s.sem("c_loaded"), s.sem("consts"), s.sem("c_ready")
        t_done, cT_ready = s.sem("t_done"), s.sem("cT_ready")
        w_even, w_odd = s.sem("w_even"), s.sem("w_odd")
        mm_done, ps_free, mod_done = s.sem("mm_done"), s.sem("ps_free"), s.sem("mod_done")
        folded, stored = s.sem("folded"), s.sem("stored")
        blk = s.block()
        wv = T["w_ada"].rearrange("a (k p) n -> p (a k) n", p=P)

        @blk.sync
        def _(sp):
            sp.dma_start(c_in[0:1, :], T["c_prompt"]).then_inc(c_loaded, 16)
            sp.dma_start(c_in[1:NR, :], T["c_sample"]).then_inc(c_loaded, 16)
            sp.dma_start(ident[:, :], T["ident"]).then_inc(c_loaded, 16)
            with sp.Fori(0, NCK // 2) as i:
                for par, arrived in ((0, w_even), (1, w_odd)):
                    sp.wait_ge(mm_done, i * 2 + par + 1)
                    sp.dma_start(w[:, par, :, :], wv[:, :, bass.ds((i * 2 + par) * 512, 512)]).then_inc(arrived, 16)
            sp.wait_ge(folded, 4)
            for h in range(2):
                for at, j in ((1, 0), (0, 1), (2, 2)):
                    sp.dma_start(T["mods"][:, 3 * h + at, :], mod[:, (3 * h + j) * D:(3 * h + j + 1) * D]).then_inc(stored, 16)
            sp.wait_ge(stored, 6 * 16)

        @blk.gpsimd
        def _(pool):
            pool.dma_start(mod[:, :], T["b_ada"].partition_broadcast(NR)).then_inc(consts_loaded, 16)
            for n, name in enumerate(("g_pre_mix", "g_post_mix", "g_pre_ffn", "g_post_ffn")):
                pool.dma_start(gains[:, n, :], T[name].partition_broadcast(NR)).then_inc(consts_loaded, 16)
            win.subtract(nc, pool)

        @blk.scalar
        def _(act):
            act.wait_ge(c_loaded, 48)
            nc.scalar.activation(c_act[:, :], c_in[:, :], ACT.Silu).then_inc(c_ready, 1)
            win.round(nc, act, T)

        @blk.tensor
        def _(pe):
            pe.sem_inc(mm_done, 2)
            pe.wait_ge(c_ready, 1)
            for k in range(KD):
                last = nc.tensor.transpose(ps_t[:, k, 0:NR], c_act[:, k * P:(k + 1) * P], ident[0:NR, 0:NR])
            last.then_inc(t_done, 1)
            pe.wait_ge(cT_ready, 1)
            with pe.Fori(0, NCK // 2) as i:
                for par, arrived in ((0, w_even), (1, w_odd)):
                    pe.wait_ge(arrived, i * 16 + 16)
                    pe.wait_ge(ps_free, i * 2 + par + 1)
                    for k in range(KD):
                        last = nc.tensor.matmul(ps_m[0:NR, par, :], cT[:, k, :], w[:, par, k, :],
                                                start=(k == 0), stop=(k == KD - 1))
                    last.then_inc(mm_done, 1)

        @blk.vector
        def _(dve):
            dve.sem_inc(ps_free, 2)
            dve.wait_ge(t_done, 1)
            nc.vector.tensor_copy(cT[:, :, :], ps_t[:, :, 0:NR]).then_inc(cT_ready, 1)
            dve.wait_ge(consts_loaded, 80)
            with dve.Fori(0, NCK // 2) as i:
                for par in range(2):
                    at = bass.ds((i * 2 + par) * 512, 512)
                    dve.wait_ge(mm_done, i * 2 + par + 3)
                    nc.vector.tensor_tensor(mod[:, at], ps_m[0:NR, par, :], mod[:, at], ALU.add).then_inc(mod_done, 1)
                    dve.wait_ge(mod_done, i * 2 + par + 1)
                    dve.sem_inc(ps_free, 1)
            for h in range(2):
                sh, sc, gt = (mod[:, (3 * h + j) * D:(3 * h + j + 1) * D] for j in range(3))
                nc.vector.scalar_tensor_tensor(sc, sc, 1.0, gains[:, 2 * h, :], ALU.add, ALU.mult).then_inc(folded, 1)
                nc.vector.tensor_tensor(gt, gt, gains[:, 2 * h + 1, :], ALU.mult).then_inc(folded, 1)


def mod_row(T, row, r=0, n=P):
    return T["mods"][r, row, :].partition_broadcast(n)


def load_sample_mod(eng, T, dst, row, arrived):
    for b in range(2 * DB):
        eng.dma_start(dst[b * DT:(b + 1) * DT, :], mod_row(T, row, 1 + b % DB, DT)).then_inc(arrived, 16)
    return 2 * DB * 16


def projection(nc, T, top, win):
    with Stage(nc, top, "pj") as s:
        x, hn = s.sb("x", [P, 2, D]), s.sb("hn", [P, 2, D])
        hi, lo = s.sb("hi", [P, 2, KD, P], F32R), s.sb("lo", [P, 2, KD, P], F32R)
        proj, sq = s.sb("proj", [P, 2, INW]), s.sb("sq", [P, 2, D])
        mod = s.sb("mod", [P, 2, 2, D])
        ident = s.sb("ident", [P, P])
        st = s.sb("st", [P, 2, 4])
        ps_t, ps_m = s.ps("ps_t", [P, 2, 512]), s.ps("ps_m", [P, 3, 512])
        mods_in, smods_in = s.sem("mods_in"), s.sem("smods_in")
        x_even, x_odd, x_free = s.sem("x_even"), s.sem("x_odd"), s.sem("x_free")
        squared, meaned, rooted, rstd_ready = s.sem("squared"), s.sem("meaned"), s.sem("rooted"), s.sem("rstd")
        hn_ready, t_done, moved_a, moved_v = s.sem("hn_ready"), s.sem("t_done"), s.sem("moved_a"), s.sem("moved_v")
        mm_done, out_a, out_v = s.sem("mm_done"), s.sem("out_a"), s.sem("out_v")
        st_even, st_odd = s.sem("st_even"), s.sem("st_odd")
        blk = s.block()
        cols = ((0, 512), (512, 512), (1024, 256))
        xp = T["x_prompt"].rearrange("a (n p) d -> p (a n) d", p=P)
        xs = T["x_sample"].rearrange("b t d -> (b t) d")
        pv = T["proj"].rearrange("(n p) d -> p n d", p=P)
        HALF = NPT // 2

        @blk.sync
        def _(sp):
            def load_x(t, par, arrived):
                sp.wait_ge(x_free, t + 1)
                sp.dma_start(x[:, par, :].unsqueeze(1), xp[:, bass.ds(t, 1), :]).then_inc(arrived, 16)

            def store(t, par, stored):
                sp.wait_ge(out_v, t * 2 + 4)
                sp.wait_ge(out_a, t + 2)
                sp.dma_start(pv[:, bass.ds(t, 1), :], proj[:, par, :].unsqueeze(1)).then_inc(stored, 16)

            sp.sem_inc(st_even, 16)
            sp.sem_inc(st_odd, 16)
            load_x(0, 0, x_even)
            sp.dma_start(ident[:, :], T["ident"]).then_inc(mods_in, 16)
            for r in range(2):
                sp.dma_start(mod[:, 0, r, :], mod_row(T, r)).then_inc(mods_in, 16)
            load_x(1, 1, x_odd)
            with sp.Fori(0, HALF - 1) as i:
                for par, arrived, stored in ((0, x_even, st_even), (1, x_odd, st_odd)):
                    load_x(i * 2 + par + 2, par, arrived)
                    store(i * 2 + par, par, stored)
            sp.wait_ge(x_free, NPT + 1)
            for h in range(2):
                sp.dma_start(x[h * NS:(h + 1) * NS, 0, :], xs).then_inc(x_even, 16)
            store(NPT - 2, 0, st_even)
            store(NPT - 1, 1, st_odd)
            store(NPT, 0, st_even)
            sp.wait_ge(st_even, (HALF + 2) * 16)
            sp.wait_ge(st_odd, (HALF + 1) * 16)

        @blk.gpsimd
        def _(pool):
            for r in range(2):
                load_sample_mod(pool, T, mod[:, 1, r, :], r, smods_in)
        @blk.scalar
        def _(act):
            act.sem_inc(out_a, 1)

            def norm(t, par, arrived, n):
                act.wait_ge(arrived, n)
                nc.scalar.activation(sq[:, par, :], x[:, par, :], ACT.Square, accum_out=st[:, par, 0:1]).then_inc(squared, 1)
                act.wait_ge(meaned, t + 1)
                nc.scalar.activation(st[:, par, 2:3], st[:, par, 1:2], ACT.Sqrt).then_inc(rooted, 1)

            def move(t, par):
                act.wait_ge(t_done, t + 1)
                act.wait_ge(mm_done, t * 3)
                for h in range(2):
                    nc.scalar.activation(hi[:, par, 4 * h:4 * h + 4, :], ps_t[:, h, :].rearrange("p (k n) -> p k n", k=4),
                                         ACT.Copy).then_inc(moved_a, 1)

            def out(t, par, stored, n):
                act.wait_ge(mm_done, t * 3 + 4)
                act.wait_ge(stored, n)
                nc.scalar.activation(proj[:, par, 0:512], ps_m[:, 0, :], ACT.Copy).then_inc(out_a, 1)

            norm(0, 0, x_even, 16)
            move(0, 0)
            norm(1, 1, x_odd, 16)
            with act.Fori(0, HALF - 1) as i:
                for par, arrived, stored in ((0, x_even, st_even), (1, x_odd, st_odd)):
                    move(i * 2 + par + 1, 1 - par)
                    norm(i * 2 + par + 2, par, arrived, i * 16 + 32)
                    out(i * 2 + par, par, stored, i * 16 + 16)
            move(NPT - 1, 1)
            norm(NPT, 0, x_even, (HALF + 2) * 16)
            out(NPT - 2, 0, st_even, HALF * 16)
            move(NPT, 0)
            out(NPT - 1, 1, st_odd, HALF * 16)
            out(NPT, 0, st_even, (HALF + 1) * 16)

        @blk.vector
        def _(dve):
            dve.sem_inc(x_free, 2)
            dve.sem_inc(out_v, 2)

            def norm(t, par, kind):
                dve.wait_ge(squared, t + 1)
                nc.vector.tensor_scalar(st[:, par, 1:2], st[:, par, 0:1], 1.0 / D, EPS, ALU.mult, ALU.add).then_inc(meaned, 1)
                dve.wait_ge(rooted, t + 1)
                nc.vector.reciprocal(st[:, par, 3:4], st[:, par, 2:3]).then_inc(rstd_ready, 1)
                dve.wait_ge(rstd_ready, t + 1)
                nc.vector.scalar_tensor_tensor(hn[:, par, :], x[:, par, :], st[:, par, 3:4], mod[:, kind, 0, :],
                                               ALU.mult, ALU.mult).then_inc(x_free, 1)
                dve.wait_ge(x_free, t + 3)
                nc.vector.tensor_tensor(hn[:, par, :], hn[:, par, :], mod[:, kind, 1, :], ALU.add).then_inc(hn_ready, 1)

            def move(t, par):
                for h in range(2):
                    part = slice(4 * h, 4 * h + 4)
                    dve.wait_ge(moved_a, t * 2 + h + 1)
                    nc.vector.tensor_tensor(lo[:, par, part, :], ps_t[:, h, :].rearrange("p (k n) -> p k n", k=4),
                                            hi[:, par, part, :].bitcast(F32), ALU.subtract).then_inc(moved_v, 1)

            def out(t, par, stored, n):
                dve.wait_ge(stored, n)
                for c in (1, 2):
                    dve.wait_ge(mm_done, t * 3 + 4 + c)
                    nc.vector.tensor_copy(proj[:, par, cols[c][0]:cols[c][0] + cols[c][1]],
                                          ps_m[:, c, 0:cols[c][1]]).then_inc(out_v, 1)

            dve.wait_ge(mods_in, 48)
            norm(0, 0, 0)
            move(0, 0)
            norm(1, 1, 0)
            with dve.Fori(0, HALF - 1) as i:
                for par, stored in ((0, st_even), (1, st_odd)):
                    move(i * 2 + par + 1, 1 - par)
                    norm(i * 2 + par + 2, par, 0)
                    out(i * 2 + par, par, stored, i * 16 + 16)
            move(NPT - 1, 1)
            dve.wait_ge(smods_in, 4 * DB * 16)
            norm(NPT, 0, 1)
            out(NPT - 2, 0, st_even, HALF * 16)
            move(NPT, 0)
            out(NPT - 1, 1, st_odd, HALF * 16)
            out(NPT, 0, st_even, (HALF + 1) * 16)

        @blk.tensor
        def _(pe):
            def flip(t, par):
                pe.wait_ge(hn_ready, t + 1)
                if not (isinstance(t, int) and t == 0):
                    pe.wait_ge(moved_v, t * 2)
                for k in range(KD):
                    last = nc.tensor.transpose(ps_t[:, k // 4, k % 4 * P:(k % 4 + 1) * P],
                                               hn[:, par, k * P:(k + 1) * P], ident[:, :])
                last.then_inc(t_done, 1)

            def product(t, par):
                pe.wait_ge(moved_v, t * 2 + 2)
                for c, (c0, n) in enumerate(cols):
                    pe.wait_ge(*((out_a, t + 1) if c == 0 else (out_v, t * 2 + c)))
                    for k in range(KD):
                        last = three_products(nc, ps_m[:, c, 0:n], hi[:, par, k, :], lo[:, par, k, :], win.hi[:, k, c0:c0 + n],
                                              win.lo[:, k, c0:c0 + n], k == 0, k == KD - 1)
                    last.then_inc(mm_done, 1)

            pe.sem_inc(mm_done, 3)
            pe.wait_ge(mods_in, 48)
            flip(0, 0)
            with pe.Fori(0, HALF) as i:
                for par in range(2):
                    flip(i * 2 + par + 1, 1 - par)
                    product(i * 2 + par, par)
            product(NPT, 0)


REC = {}
_at = 0
for _n, _w in (("N", 192), ("T", 128), ("M", 128), ("MS", 128), ("COS", NCH), ("SIN", NCH), ("H0", DB)):
    REC[_n] = (_at, _w)
    _at += _w
RECW = _at + (-_at) % 8

LN2_HI, MAGIC = 0.693359375, 12582912.0
LN2_LO = math.log(2.0) - LN2_HI
TAU = 2.0 * math.pi
TAU_1 = 6.28125
TAU_2 = float(np.float16(TAU - TAU_1))
TAU_3 = TAU - TAU_1 - TAU_2
PI_BELOW = 3.1415925


def s5_tables(nc, T, top):
    with Stage(nc, top, "st") as s:
        ident = s.sb("ident", [P, P])
        lam_in = s.sb("lam_in", [NG, 2, 2, NST])
        d_in, d_rep = s.sb("d_in", [NG, GC]), s.sb("d_rep", [NG, L, GC])
        c_in = s.sb("c_in", [P, 2, 4, 2, NST])
        h_in = s.sb("h_in", [P, 2, 2, 2, NST])
        sgn = s.sb("sgn", [P, 1])
        v = s.sb("v", [P, 40, NG])
        vi = s.sb("vi", [P, NG], I32)
        Bm, Cm = s.sb("Bm", [P, 2, NG, GC]), s.sb("Cm", [P, 2, NG, GC])
        Bb = s.sb("Bb", [P, 2, NG, GC])
        pw = s.sb("pw", [P, 2, L + 1, NG])
        PP, QQ = s.sb("PP", [P, L + 1, NG]), s.sb("QQ", [P, L + 1, NG])
        PS, QS = s.sb("PS", [P, L + 1, NG]), s.sb("QS", [P, L + 1, NG])
        PR, QR = s.sb("PR", [P, L, NG]), s.sb("QR", [P, L, NG])
        t1, t2, t3, t4 = (s.sb(f"t{n}", [P, 2048]) for n in range(1, 5))
        CL, CM = s.sb("CL", [P, NG, L + 1, GC]), s.sb("CM", [P, NG, L, GC])
        NB = s.sb("NB", [P, NG, L, GC])
        N3, TT = s.sb("N3", [P, NG, P]), s.sb("TT", [P, NG, P])
        kq = s.sb("kq", [GC, NG, P])
        E1, E16 = s.sb("E1", [P, 2, NG, 16]), s.sb("E16", [P, 2, NG, 16])
        ES = s.sb("ES", [P, 2, NG, 16])
        phv, php = s.sb("phv", [P, 2, 8, NCH]), s.sb("php", [P, 8, NCH])
        h0, hpre = s.sb("h0", [P, 2, DB, NG]), s.sb("hpre", [P, DB, NG])
        hs = s.sb("hs", [P, NG, DB])
        ps_a, ps_c = s.ps("ps_a", [P, 512]), s.ps("ps_c", [P, 2, 4, P])
        ps_h, ps_n, ps_k = s.ps("ps_h", [P, 2, 2, P]), s.ps("ps_n", [P, 2, 512]), s.ps("ps_k", [P, 2, 512])
        params, bc_in, flipped, sins, mats = s.sem("params"), s.sem("bc_in"), s.sem("flipped"), s.sem("sins"), s.sem("mats")
        reduced = s.sem("reduced")
        step, kq_mm, kq_out, kq_moved = s.sem("step"), s.sem("kq_mm"), s.sem("kq_out"), s.sem("kq_moved")
        n_mm, n_out, tables = s.sem("n_mm"), s.sem("n_out"), s.sem("tables")
        e_ready, phv_ready, php_ready, pstep = s.sem("e_ready"), s.sem("phv_ready"), s.sem("php_ready"), s.sem("pstep")
        powers, cm_ready, even_out, odd_out, php_out = (s.sem(n) for n in ("powers", "cm_ready", "even_out", "odd_out", "php_out"))
        h0_ready, t_ready, hpre_ready = s.sem("h0_ready"), s.sem("t_ready"), s.sem("hpre_ready")
        rec_out = s.sem("rec_out")
        tt_zero, d_ready, d_copied = s.sem("tt_zero"), s.sem("d_ready"), s.sem("d_copied")
        blk = s.block()
        slots = {}

        def V(name):
            return v[:, slots.setdefault(name, len(slots)), :]

        rec = T["rec"].rearrange("g q w -> q g w")

        def rec_cols(name):
            a, w = REC[name]
            return rec[:, :, a:a + w]

        by_vector = [(name, n) for n in range(3) for name in ("COS", "SIN")]
        by_pool = [("COS", 3), ("SIN", 3)]

        def phases(st, eng, name, n, a, b, out, slot_free):
            gs = slice(n * 8, n * 8 + 8)
            e16, flip = (E16, 0) if name == "COS" else (ES, 1)
            hi = [e16[:, r, gs, :].unsqueeze(3).broadcast_to([P, 8, 16, 16]) for r in range(2)]
            lo = [E1[:, r, gs, :].unsqueeze(2).broadcast_to([P, 8, 16, 16]) for r in range(2)]
            a4, b4 = (t[:, :].rearrange("p (g a b) -> p g a b", g=8, a=16) for t in (a, b))
            st.mark(eng.tensor_tensor(a4, hi[0], lo[flip], ALU.mult))
            st.then(eng.tensor_tensor(b4, hi[1], lo[1 - flip], ALU.mult))
            slot_free()
            return eng.tensor_tensor(out.rearrange("p g n -> p (g n)"), a[:, :], b[:, :], ALU.add if flip else ALU.subtract)

        @blk.sync
        def _(sp):
            sp.dma_start(ident[:, :], T["ident"]).then_inc(params, 16)
            sp.dma_start(sgn[:, :], T["sgn"]).then_inc(params, 16)
            for h in range(2):
                sp.dma_start(lam_in[:, 0, h, :], T["ssm_lam_re"][0]).then_inc(params, 16)
                sp.dma_start(lam_in[:, 1, h, :], T["ssm_lam_im"][0]).then_inc(params, 16)
            sp.dma_start(V("logdt"), T["ssm_log_dt"][0, :].partition_broadcast(P)).then_inc(params, 16)
            sp.dma_start(d_in[:, :], T["ssm_d"].rearrange("a (g c) -> (a g) c", g=NG)).then_inc(params, 16)
            for r, name in enumerate(("ssm_c_re", "ssm_c_im")):
                cv = T[name].rearrange("a (n g) c p -> (g c) (a n) p", n=4)
                for h in range(2):
                    sp.dma_start(c_in[:, r, :, h, :], cv).then_inc(params, 16)
            for r, name in enumerate(("state_ssm_re", "state_ssm_im")):
                hv = T[name].rearrange("a (n b) g p -> (b g) (a n) p", n=2)
                for x in range(2):
                    sp.dma_start(h_in[:, :, x, r ^ x, :], hv).then_inc(params, 16)
            sp.wait_ge(kq_out, 8)
            sp.wait_ge(tt_zero, 1)
            for j in range(L):
                sp.dma_start(TT[j * GC:(j + 1) * GC, :, j * GC:], kq[:, :, 0:P - j * GC]).then_inc(kq_moved, 16)
            sp.wait_ge(n_out, 8)
            at = REC["N"][0]
            sp.dma_start(rec[:, :, at:at + P], N3[:, :, :]).then_inc(rec_out, 16)
            sp.dma_start(rec[:, :, at + P:at + P + NST], N3[:, :, 0:NST]).then_inc(rec_out, 16)
            sp.dma_start(rec_cols("M"), CL[:, :, 1:, :].rearrange("q g t c -> q g (t c)")).then_inc(rec_out, 16)
            sp.wait_ge(cm_ready, 2)
            sp.dma_start(rec_cols("MS"), CM[:, :, :, :].rearrange("q g t c -> q g (t c)")).then_inc(rec_out, 16)
            sp.wait_ge(hpre_ready, 2)
            sp.dma_start(rec_cols("H0"), hs[:, :, :]).then_inc(rec_out, 16)
            sp.dma_start(T["r8"], V("r8")).then_inc(rec_out, 16)
            sp.dma_start(T["hpre"], hpre[:, :, :].rearrange("q b g -> q (b g)")).then_inc(rec_out, 16)
            for u, (name, n) in enumerate(by_vector):
                if u == 4:
                    sp.wait_ge(t_ready, 1)
                    sp.dma_start(rec_cols("T"), TT[:, :, :]).then_inc(rec_out, 16)
                sp.wait_ge(phv_ready, u + 1)
                sp.dma_start(rec_cols(name)[:, n * 8:n * 8 + 8, :], phv[:, u % 2, :, :]).then_inc(odd_out if u % 2 else even_out, 16)
            sp.wait_ge(even_out, 3 * 16)
            sp.wait_ge(odd_out, 3 * 16)
            sp.wait_ge(rec_out, 8 * 16)

        @blk.gpsimd
        def _(pool):
            nc.gpsimd.memset(TT[:, :, :], 0.0).then_inc(tt_zero, 1)
            for r, name in enumerate(("ssm_b_re", "ssm_b_im")):
                bv = T[name].rearrange("a g p c -> p (a g) c")
                for h in range(2):
                    pool.dma_start(Bm[h * NST:(h + 1) * NST, r, :, :], bv).then_inc(bc_in, 16)
            st_ = Steps(pool, pstep)
            pool.wait_ge(powers, 1)
            for tau in (1, 1 + L // 2):
                wide = [P, NG, L // 2, GC]
                x, y = (t[:, :].rearrange("p (g t c) -> p g t c", g=NG, t=L // 2) for t in (t3, t4))
                p, q = (a[:, tau:tau + L // 2, :].rearrange("p t g -> p g t").unsqueeze(3).broadcast_to(wide) for a in (PP, QQ))
                c0, c1 = (Cm[:, r, :, :].unsqueeze(2).broadcast_to(wide) for r in range(2))
                st_.mark(nc.gpsimd.tensor_tensor(x, c0, q, ALU.mult))
                st_.then(nc.gpsimd.tensor_tensor(y, c1, p, ALU.mult))
                nc.gpsimd.tensor_tensor(CM[:, :, tau - 1:tau - 1 + L // 2, :], x, y, ALU.subtract).then_inc(cm_ready, 1)
                pool.wait_ge(cm_ready, 1 if tau == 1 else 2)
            pool.wait_ge(e_ready, 1)
            for u, (name, n) in enumerate(by_pool):
                phases(st_, nc.gpsimd, name, n, t3, t4, php[:, :, :],
                       lambda: pool.wait_ge(php_out, 16) if u else None).then_inc(php_ready, 1)
                pool.wait_ge(php_ready, u + 1)

        @blk.scalar
        def _(act):
            act.wait_ge(reduced, 1)
            nc.scalar.activation(V("sin1"), V("red1"), ACT.Sin).then_inc(sins, 1)
            nc.scalar.activation(V("cos1"), V("cred1"), ACT.Sin).then_inc(sins, 1)
            nc.scalar.activation(V("sin8"), V("red8"), ACT.Sin).then_inc(sins, 1)
            nc.scalar.activation(V("cos8"), V("cred8"), ACT.Sin).then_inc(sins, 1)
            for g4 in range(8):
                act.wait_ge(n_mm, g4 + 1)
                src = ps_n[:, g4 % 2, :].rearrange("p (g n) -> p g n", g=4)
                gs = slice(g4 * 4, g4 * 4 + 4)
                nc.scalar.activation(N3[:, gs, :], src, ACT.Copy).then_inc(n_out, 1)
                act.wait_ge(kq_mm, g4 + 1)
                nc.scalar.activation(kq[:, gs, :], ps_k[0:GC, g4 % 2, :].rearrange("p (g n) -> p g n", g=4),
                                     ACT.Copy).then_inc(kq_out, 1)
            for u, (name, n) in enumerate(by_pool):
                act.wait_ge(php_ready, u + 1)
                act.dma_start(rec_cols(name)[:, n * 8:n * 8 + 8, :], php[:, :, :]).then_inc(php_out, 16)
            act.wait_ge(php_out, 2 * 16)

        @blk.tensor
        def _(pe):
            pe.wait_ge(params, 16 * 16)
            for r in range(2):
                nc.tensor.transpose(ps_a[:, r * NG:(r + 1) * NG], lam_in[:, r, :, :].rearrange("g h p -> g (h p)"), ident[0:NG, 0:NG])
            pe.wait_ge(d_copied, 1)
            nc.tensor.transpose(ps_a[:, 2 * NG:3 * NG], d_rep[:, :, :].rearrange("g j c -> g (j c)"), ident[0:NG, 0:NG])
            for r in range(2):
                for n in range(4):
                    nc.tensor.transpose(ps_c[:, r, n, :], c_in[:, r, n, :, :].rearrange("q h p -> q (h p)"), ident[:, :])
            for n in range(2):
                for x in range(2):
                    last = nc.tensor.transpose(ps_h[:, n, x, :], h_in[:, n, x, :, :].rearrange("q h p -> q (h p)"), ident[:, :])
            last.then_inc(flipped, 1)
            pe.wait_ge(mats, 1)
            for g4 in range(8):
                if g4 >= 2:
                    pe.wait_ge(n_out, g4 - 1)
                    pe.wait_ge(kq_out, g4 - 1)
                for n in range(4):
                    g = g4 * 4 + n
                    last = nc.tensor.transpose(ps_n[:, g4 % 2, n * P:(n + 1) * P], NB[:, g, :, :].rearrange("q j c -> q (j c)"), ident[:, :])
                last.then_inc(n_mm, 1)
                for n in range(4):
                    g = g4 * 4 + n
                    last = nc.tensor.matmul(ps_k[0:GC, g4 % 2, n * P:(n + 1) * P], NB[:, g, L - 1, :],
                                            CL[:, g, 0:L, :].rearrange("q t c -> q (t c)"), start=True, stop=True)
                last.then_inc(kq_mm, 1)

        @blk.vector
        def _(dve):
            st_ = Steps(dve, step)
            then = st_.then
            vec = nc.vector

            def ts(out, a, s1, s2, o1, o2):
                then(vec.tensor_scalar(out, a, s1, s2, o1, o2))

            def tt(out, a, b, op):
                then(vec.tensor_tensor(out, a, b, op))

            def stt(out, a, c, b, o1, o2):
                then(vec.scalar_tensor_tensor(out, a, c, b, o1, o2))

            def exp(out, x):
                k, f, p = V("k"), V("f"), V("p")
                ts(k, x, 1.0 / math.log(2.0), MAGIC, ALU.mult, ALU.add)
                ts(k, k, -MAGIC, -126.0, ALU.add, ALU.max)
                ts(k, k, 127.0, None, ALU.min, ALU.bypass)
                stt(f, k, -LN2_HI, x, ALU.mult, ALU.add)
                stt(f, k, -LN2_LO, f, ALU.mult, ALU.add)
                ts(p, f, 1.0 / 5040, 1.0 / 720, ALU.mult, ALU.add)
                tt(p, p, f, ALU.mult)
                for n in (5, 4, 3, 2, 1):
                    stt(p, p, 1.0 / math.factorial(n), f, ALU.add, ALU.mult)
                ts(k, k, 127.0, float(2 ** 23), ALU.add, ALU.mult)
                then(vec.tensor_copy(vi[:, :], k))
                stt(out, p, 1.0, vi[:, :].bitcast(F32), ALU.add, ALU.mult)

            def reduce_angle(name, a):
                n, r, c = V("k"), V("red" + name), V("cred" + name)
                ts(n, a, 1.0 / TAU, MAGIC, ALU.mult, ALU.add)
                ts(n, n, -MAGIC, None, ALU.add, ALU.bypass)
                stt(r, n, -TAU_1, a, ALU.mult, ALU.add)
                stt(r, n, -TAU_2, r, ALU.mult, ALU.add)
                stt(r, n, -TAU_3, r, ALU.mult, ALU.add)
                ts(r, r, PI_BELOW, -PI_BELOW, ALU.min, ALU.max)
                stt(c, r, -1.0, r, ALU.mult, ALU.max)
                ts(c, c, -1.0, math.pi / 2, ALU.mult, ALU.add)

            def cmul(ore, oim, ar, ai, br, bi, x, y):
                st_.mark(vec.tensor_tensor(x, ar, br, ALU.mult))
                then(vec.tensor_tensor(y, ai, bi, ALU.mult))
                then(vec.tensor_tensor(x, x, y, ALU.subtract))
                then(vec.tensor_tensor(y, ar, bi, ALU.mult))
                then(vec.tensor_tensor(oim, ai, br, ALU.mult))
                then(vec.tensor_tensor(oim, oim, y, ALU.add))
                then(vec.tensor_copy(ore, x))

            dve.wait_ge(params, 16 * 16)
            for j in range(L):
                last = vec.tensor_copy(d_rep[:, j, :], d_in[:, :])
            last.then_inc(d_copied, 1)
            dve.wait_ge(flipped, 1)
            lr, li, dcol = V("lr"), V("li"), V("dcol")
            then(vec.tensor_copy(lr, ps_a[:, 0:NG]))
            then(vec.tensor_copy(li, ps_a[:, NG:2 * NG]))
            then(vec.tensor_copy(dcol, ps_a[:, 2 * NG:3 * NG]))
            for r in range(2):
                then(vec.tensor_copy(Cm[:, r, :, :].rearrange("q g c -> q (g c)"), ps_c[:, r, :, :].rearrange("q n x -> q (n x)")))
            for x in range(2):
                for n in range(2):
                    then(vec.tensor_copy(h0[:, x, 4 * n:4 * n + 4, :].rearrange("q b g -> q (b g)"), ps_h[:, n, x, :]))
            exp(V("dt"), V("logdt"))
            ar, ai = V("ar"), V("ai")
            tt(ar, lr, V("dt"), ALU.mult)
            tt(ai, li, V("dt"), ALU.mult)
            reduce_angle("1", ai)
            ts(V("ai8"), ai, 8.0, None, ALU.mult, ALU.bypass)
            reduce_angle("8", V("ai8"))
            dve.sem_inc(reduced, 1)
            exp(V("r1"), ar)
            ts(V("ar8"), ar, 8.0, None, ALU.mult, ALU.bypass)
            exp(V("r8"), V("ar8"))
            dve.wait_ge(sins, 4)
            then(vec.memset(pw[:, 0, 0, :], 1.0))
            then(vec.memset(pw[:, 1, 0, :], 0.0))
            tt(pw[:, 0, 1, :], V("r1"), V("cos1"), ALU.mult)
            tt(pw[:, 1, 1, :], V("r1"), V("sin1"), ALU.mult)
            for m in (1, 2, 4):
                dst, src = slice(m + 1, 2 * m + 1), slice(1, m + 1)
                base = [pw[:, r, m, :].unsqueeze(1).broadcast_to([P, m, NG]) for r in range(2)]
                x, y = (t[:, 0:m * NG].rearrange("p (m g) -> p m g", m=m) for t in (t1, t2))
                cmul(pw[:, 0, dst, :], pw[:, 1, dst, :], pw[:, 0, src, :], pw[:, 1, src, :], base[0], base[1], x, y)
            lo, hi = slice(0, NST), slice(NST, P)
            then(vec.tensor_copy(PP[lo, :, :], pw[lo, 0, :, :]))
            then(vec.tensor_copy(PP[hi, :, :], pw[hi, 1, :, :]))
            ts(QQ[lo, :, :], pw[lo, 1, :, :], -1.0, None, ALU.mult, ALU.bypass)
            then(vec.tensor_copy(QQ[hi, :, :], pw[hi, 0, :, :]))
            dve.sem_inc(powers, 1)
            st_.mark(vec.tensor_scalar(PS[:, :, :], PP[:, :, :], sgn[:, 0:1], None, ALU.mult))
            st_.mark(vec.tensor_scalar(QS[:, :, :], QQ[:, :, :], sgn[:, 0:1], None, ALU.mult))
            for j in range(L):
                st_.mark(vec.tensor_copy(PR[:, j, :], PP[:, L - 1 - j, :]))
                st_.mark(vec.tensor_copy(QR[:, j, :], QQ[:, L - 1 - j, :]))
            nr, den, fr, fi, x = V("nr"), V("den"), V("fr"), V("fi"), V("x")
            ts(nr, pw[:, 0, 1, :], -1.0, None, ALU.add, ALU.bypass)
            ni = pw[:, 1, 1, :]
            tt(den, lr, lr, ALU.mult)
            tt(x, li, li, ALU.mult)
            tt(den, den, x, ALU.add)
            then(vec.reciprocal(den, den))
            tt(fr, nr, lr, ALU.mult)
            tt(x, ni, li, ALU.mult)
            tt(fr, fr, x, ALU.add)
            tt(fr, fr, den, ALU.mult)
            tt(fi, ni, lr, ALU.mult)
            tt(x, nr, li, ALU.mult)
            tt(fi, fi, x, ALU.subtract)
            tt(fi, fi, den, ALU.mult)
            dve.wait_ge(bc_in, 64)
            wide = [P, NG, GC]
            x, y = (t[:, 0:NG * GC].rearrange("p (g c) -> p g c", g=NG) for t in (t1, t2))
            cmul(Bb[:, 0], Bb[:, 1], Bm[:, 0], Bm[:, 1], fr.unsqueeze(2).broadcast_to(wide), fi.unsqueeze(2).broadcast_to(wide), x, y)
            def powers_times(out, m0, m1, p, q, n):
                wide = [P, NG, n, GC]
                x, y = (t[:, 0:NG * n * GC].rearrange("p (g t c) -> p g t c", g=NG, t=n) for t in (t1, t2))
                p, q = (a.rearrange("p t g -> p g t").unsqueeze(3).broadcast_to(wide) for a in (p, q))
                st_.mark(vec.tensor_tensor(x, m0.unsqueeze(2).broadcast_to(wide), p, ALU.mult))
                then(vec.tensor_tensor(y, m1.unsqueeze(2).broadcast_to(wide), q, ALU.mult))
                tt(out, x, y, ALU.add)

            HL = L // 2
            for j in (0, HL):
                js = slice(j, j + HL)
                powers_times(NB[:, :, js, :], Bb[:, 0], Bb[:, 1], PR[:, js, :], QR[:, js, :], HL)
            for tau, n in ((0, HL), (HL, HL), (L, 1)):
                ts_ = slice(tau, tau + n)
                powers_times(CL[:, :, ts_, :], Cm[:, 0], Cm[:, 1], PS[:, ts_, :], QS[:, ts_, :], n)
            dve.sem_inc(mats, 1)
            for E, first in ((E1, None), (E16, E1)):
                then(vec.memset(E[:, 0, :, 0], 1.0))
                then(vec.memset(E[:, 1, :, 0], 0.0))
                if first is None:
                    then(vec.tensor_copy(E[:, 0, :, 1], V("cos8")))
                    then(vec.tensor_copy(E[:, 1, :, 1], V("sin8")))
                else:
                    cmul(E[:, 0, :, 1], E[:, 1, :, 1], E1[:, 0, :, 8], E1[:, 1, :, 8], E1[:, 0, :, 8], E1[:, 1, :, 8],
                         t1[:, 0:NG], t2[:, 0:NG])
                for m in (0, 1, 2, 4, 8):
                    if m:
                        n = min(m, 15 - m)
                        dst, src = slice(m + 1, m + n + 1), slice(1, n + 1)
                        base = [E[:, r, :, m].unsqueeze(2).broadcast_to([P, NG, n]) for r in range(2)]
                        x, y = (t[:, 0:n * NG].rearrange("p (g m) -> p g m", g=NG) for t in (t1, t2))
                        cmul(E[:, 0, :, dst], E[:, 1, :, dst], E[:, 0, :, src], E[:, 1, :, src], base[0], base[1], x, y)
                    else:
                        n, dst = 1, slice(1, 2)
                        x, y = (t[:, 0:NG].rearrange("p (g m) -> p g m", g=NG) for t in (t1, t2))
                    er, ei = E[:, 0, :, dst], E[:, 1, :, dst]
                    tt(x, er, er, ALU.mult)
                    tt(y, ei, ei, ALU.mult)
                    tt(x, x, y, ALU.add)
                    ts(x, x, -0.5, 1.5, ALU.mult, ALU.add)
                    tt(er, er, x, ALU.mult)
                    tt(ei, ei, x, ALU.mult)
            ts(ES[:, :, :, :].rearrange("q r g a -> q (r g a)"), E16[:, :, :, :].rearrange("q r g a -> q (r g a)"), sgn[:, 0:1], None, ALU.mult, ALU.bypass)
            dve.sem_inc(e_ready, 1)
            def skip():
                dve.wait_ge(kq_moved, 8 * 16)
                for n in range(4):
                    gs = slice(n * 8, n * 8 + 8)
                    x = t1[:, 0:1024].rearrange("p (g n) -> p g n", g=8)
                    tt(x, ident[:, :].unsqueeze(1).broadcast_to([P, 8, P]), dcol[:, gs].unsqueeze(2).broadcast_to([P, 8, P]), ALU.mult)
                    tt(TT[:, gs, :], TT[:, gs, :], x, ALU.add)
                dve.sem_inc(t_ready, 1)

            wide = [P, DB, NG]
            then(vec.tensor_copy(hs[:, :, :], h0[:, 0, :, :].rearrange("q b g -> q g b")))
            ts(V("si"), pw[:, 1, L, :], sgn[:, 0:1], -1.0, ALU.mult, ALU.mult)
            tt(hpre[:, :, :], h0[:, 0, :, :], pw[:, 0, L, :].unsqueeze(1).broadcast_to(wide), ALU.mult)
            x = t1[:, 0:DB * NG].rearrange("p (b g) -> p b g", b=DB)
            tt(x, h0[:, 1, :, :], V("si").unsqueeze(1).broadcast_to(wide), ALU.mult)
            tt(hpre[:, :, :], hpre[:, :, :], x, ALU.add)
            dve.sem_inc(hpre_ready, 2)
            for u, (name, n) in enumerate(by_vector):
                if u == 4:
                    skip()
                phases(st_, vec, name, n, t1, t2, phv[:, u % 2, :, :],
                       lambda: dve.wait_ge(odd_out if u % 2 else even_out, u // 2 * 16) if u >= 2 else None).then_inc(phv_ready, 1)
                dve.wait_ge(phv_ready, u + 1)


BW = 3 * WIN
RB = NH * BW


def bucket_onehot():
    out = np.zeros((NBUCKET + 1, BW), np.float32)
    half = NBUCKET // 2
    for m in range(BW):
        d = 2 * WIN - 1 - m
        if 0 <= d <= WIN:
            log = math.log(max(d, 1) / half) / math.log(WIN / half)
            out[d if d < half else min(half + int(log * (NBUCKET - half)), NBUCKET - 1), m] = 1.0
        else:
            out[NBUCKET, m] = 1.0
    return out


class AttentionBias:

    def __init__(self, s, bank):
        self.tab, self.wide, self.hot = s.sb("tab", [NBUCKET + 1, NH]), s.sb("wide", [NBUCKET + 1, NH, P]), s.sb("hot", [NBUCKET + 1, BW])
        self.rows, self.bank = s.sb("rows", [P, NH, BW]), bank
        self.loaded, self.masked, self.widened, self.done, self.moved = (s.sem(n) for n in ("tab_loaded", "masked", "widened", "bias_done", "bias_moved"))

    def load(self, sp, T):
        sp.dma_start(self.tab[0:NBUCKET, :], T["rel_bias_table"]).then_inc(self.loaded, 16)
        sp.dma_start(self.hot[:, :], T["onehot"]).then_inc(self.loaded, 16)

    def store(self, sp, T, stored):
        sp.wait_ge(self.moved, NH)
        sp.dma_start(T["bias_rows"], self.rows[:, :, :].rearrange("p h m -> p (h m)")).then_inc(stored, 16)

    def widen_and_move(self, nc, dve):
        nc.vector.memset(self.tab[NBUCKET:NBUCKET + 1, :], MASKED).then_inc(self.masked, 1)
        dve.wait_ge(self.loaded, 32)
        dve.wait_ge(self.masked, 1)
        nc.vector.tensor_copy(self.wide[:, :, :], self.tab[:, :].unsqueeze(2).broadcast_to([NBUCKET + 1, NH, P])).then_inc(self.widened, 1)
        for h in range(NH):
            dve.wait_ge(self.done, h + 1)
            nc.vector.tensor_copy(self.rows[:, h, :], self.bank[:, 0:BW]).then_inc(self.moved, 1)

    def spread(self, nc, pe):
        pe.wait_ge(self.widened, 1)
        for h in range(NH):
            if h:
                pe.wait_ge(self.moved, h)
            nc.tensor.matmul(self.bank[:, 0:BW], self.wide[:, h, :], self.hot[:, :], start=True, stop=True).then_inc(self.done, 1)


U5 = 4


def s5(nc, T, top):
    with Stage(nc, top, "s5") as s:
        ident, swap = s.sb("ident", [P, P]), s.sb("swap", [P, P])
        u, us = s.sb("u", [P, 2, L, SW]), s.sb("us", [DB, L, SW])
        y, ys = s.sb("y", [P, 2, L, SW]), s.sb("ys", [DB, L, SW])
        rec = s.sb("rec", [P, U5, RECW])
        ug = s.sb("ug", [P, U5, 3, P])
        uT = s.sb("uT", [P, U5, NCH + DB])
        w1, w2, G = s.sb("w1", [P, 2, NCH]), s.sb("w2", [P, 2, NCH]), s.sb("G", [P, 2, NCH])
        A, B = s.sb("A", [P, 2, NCH + 1]), s.sb("B", [P, 2, NCH + 1])
        r8 = s.sb("r8", [P, NG])
        lastA, lastB, ss = s.sb("lastA", [P, NG]), s.sb("lastB", [P, NG]), s.sb("ss", [P, DB, NG])
        hp = s.sb("hp", [P, DB, NG])
        fin, fins = s.sb("fin", [NG, P]), s.sb("fins", [P, 2, P])
        ps_u, ps_s, ps_w = s.ps("ps_u", [P, 3, P]), s.ps("ps_s", [P, 2, 512]), s.ps("ps_w", [P, 2, 512])
        ps_y, ps_f = s.ps("ps_y", [P, 2, 512]), s.ps("ps_f", [P, 512])
        loaded = s.sem("loaded")
        rec_in = [s.sem(f"rec{q}") for q in range(U5)]
        ug_ready, flipped, uT_ready = s.sem("ug_ready"), s.sem("flipped"), s.sem("uT_ready")
        states, y_done, y_out = s.sem("states"), s.sem("y_done"), s.sem("y_out")
        turned, added, g_ready, a_ready, b_ready = (s.sem(n) for n in ("turned", "added", "g_ready", "a_ready", "b_ready"))
        last_ready, edges, fin_mm, fin_out, stored = (s.sem(n) for n in ("last_ready", "edges", "fin_mm", "fin_out", "stored"))
        y_a, edges0, lastb_ready = s.sem("y_a"), s.sem("edges0"), s.sem("lastb_ready")
        bias = AttentionBias(s, ps_f)
        blk = s.block()
        up = T["proj"][0:SEQ, 0:SW].rearrange("(i p j) c -> p i j c", i=2, j=L)
        usv = T["proj"][SEQ:SEQ + NS, 0:SW].rearrange("(b j) c -> b j c", j=L)
        yp = T["y"][0:SEQ, :].rearrange("(i p j) c -> p i j c", i=2, j=L)
        ysv = T["y"][SEQ:SEQ + NS, :].rearrange("(b j) c -> b j c", j=L)

        def R(q, name):
            a, w = REC[name]
            return rec[:, q, a:a + w]

        @blk.sync
        def _(sp):
            bias.load(sp, T)
            for dst, name in ((ident, "ident"), (swap, "swap"), (r8, "r8")):
                sp.dma_start(dst[:, :], T[name]).then_inc(loaded, 16)
            sp.dma_start(hp[:, :, :].rearrange("q b g -> q (b g)"), T["hpre"]).then_inc(loaded, 16)
            for i in range(2):
                sp.dma_start(u[:, i, :, :], up[:, i]).then_inc(loaded, 16)
            sp.dma_start(us[:, :, :], usv).then_inc(loaded, 16)
            with sp.Fori(0, NG // U5) as i:
                for q in range(U5):
                    sp.wait_ge(y_done, i * U5 + q + 1)
                    sp.dma_start(rec[:, q, :].unsqueeze(1), T["rec"].rearrange("g q w -> q g w")[:, bass.ds(i * U5 + q, 1), :]).then_inc(rec_in[q], 16)
            bias.store(sp, T, stored)
            sp.wait_ge(y_out, NG + 1)
            sp.dma_start(ysv, ys[:, :, :]).then_inc(stored, 16)
            for i in range(2):
                sp.dma_start(yp[:, i], y[:, i, :, :]).then_inc(stored, 16)
            sp.wait_ge(fin_out, 2)
            for r, part in enumerate(("re", "im")):
                cols = slice(r * NST, (r + 1) * NST)
                sp.dma_start(T[f"o_ssm_{part}_prompt"][0, 0], fin[:, cols]).then_inc(stored, 16)
                for n in range(2):
                    dst = T[f"o_ssm_{part}_sample"].rearrange("a b g p -> (a b g) p")[n * P:(n + 1) * P, :]
                    sp.dma_start(dst, fins[:, n, cols]).then_inc(stored, 16)
            sp.wait_ge(stored, 10 * 16)

        @blk.scalar
        def _(act):
            act.sem_inc(y_out, 1)
            act.wait_ge(loaded, 7 * 16)

            def group(g, q, first=False):
                cols = bass.ds(g * GC, GC)
                if not first:
                    act.wait_ge(flipped, g - U5 + 1)
                nc.scalar.activation(ug[:, q, 0:2, :].rearrange("p i (j c) -> p i j c", j=L), u[:, :, :, cols], ACT.Copy).then_inc(ug_ready, 1)
                nc.scalar.activation(ug[0:DB, q, 2, :].rearrange("p (j c) -> p j c", j=L), us[:, :, cols], ACT.Copy).then_inc(ug_ready, 1)

            def out(g, par):
                cols = bass.ds(g * GC, GC)
                act.wait_ge(y_done, g + U5 + 1)
                nc.scalar.activation(y[:, :, :, cols], ps_y[:, par, 0:2 * P].rearrange("p (i j c) -> p i j c", i=2, j=L), ACT.Copy).then_inc(y_a, 1)
                nc.scalar.activation(ys[:, :, cols], ps_y[0:DB, par, 2 * P:3 * P].rearrange("p (j c) -> p j c", j=L), ACT.Copy).then_inc(y_out, 1)

            for g in range(U5):
                group(g, g, True)
            out(0, 0)
            with act.Fori(0, NG // U5 - 1) as i:
                for q in range(U5):
                    group(i * U5 + q + U5, q)
                    out(i * U5 + q + 1, (q + 1) % 2)
            for g in range(NG - U5 + 1, NG):
                out(g, g % 2)

        @blk.tensor
        def _(pe):
            pe.sem_inc(y_done, U5)
            bias.spread(nc, pe)
            pe.wait_ge(loaded, 7 * 16)

            def flip(g, q, first=False):
                pe.wait_ge(ug_ready, g * 2 + 2)
                if not first:
                    pe.wait_ge(uT_ready, g)
                for i in range(2):
                    nc.tensor.transpose(ps_u[:, i, :], ug[:, q, i, :], ident[:, :])
                nc.tensor.transpose(ps_u[:, 2, 0:DB], ug[0:DB, q, 2, :], ident[0:DB, 0:DB]).then_inc(flipped, 1)

            def contribute(g, q, n):
                pe.wait_ge(uT_ready, g + 1)
                pe.wait_ge(rec_in[q], n)
                a = REC["N"][0]
                nc.tensor.matmul(ps_s[:, q % 2, 0:NCH + DB], rec[:, q, a:a + P], uT[:, q, :], start=True, stop=True)
                nc.tensor.matmul(ps_w[:, q % 2, 0:NCH + DB], rec[:, q, a + NST:a + NST + P], uT[:, q, :], start=True, stop=True).then_inc(states, 1)

            def back(g, q):
                par = q % 2
                pe.wait_ge(y_out, g)
                pe.wait_ge(a_ready, g + 1)
                pe.wait_ge(b_ready, g + 1)
                for i in range(2):
                    c = slice(i * P, (i + 1) * P)
                    nc.tensor.matmul(ps_y[:, par, c], uT[:, q, c], R(q, "T"), start=True, stop=False)
                    nc.tensor.matmul(ps_y[:, par, c], A[:, par, c], R(q, "M"), start=False, stop=False)
                    nc.tensor.matmul(ps_y[:, par, c], B[:, par, c], R(q, "MS"), start=False, stop=True)
                c = slice(2 * P, 3 * P)
                nc.tensor.matmul(ps_y[0:DB, par, c], uT[:, q, NCH:NCH + DB], R(q, "T"), start=True, stop=False)
                nc.tensor.matmul(ps_y[0:DB, par, c], R(q, "H0"), R(q, "M"), start=False, stop=True).then_inc(y_done, 1)

            flip(0, 0, True)
            contribute(0, 0, 16)
            flip(1, 1)
            contribute(1, 1, 16)
            with pe.Fori(0, NG // U5 - 1) as i:
                for q in range(U5):
                    g, ahead = i * U5 + q, (q + 2) % U5
                    flip(g + 2, ahead)
                    back(g, q)
                    contribute(g + 2, ahead, i * 16 + (16 if q < 2 else 32))
            for g in range(NG - U5, NG):
                if g + 2 < NG:
                    flip(g + 2, (g + 2) % U5)
                back(g, g % U5)
                if g + 2 < NG:
                    contribute(g + 2, (g + 2) % U5, NG // U5 * 16)
            pe.wait_ge(edges, 1)
            pe.wait_ge(bias.moved, NH)
            nc.tensor.matmul(ps_f[0:NG, 0:P], lastA[:, :], ident[:, :], start=True, stop=False)
            nc.tensor.matmul(ps_f[0:NG, 0:P], lastB[:, :], swap[:, :], start=False, stop=True)
            for n in range(2):
                last = nc.tensor.transpose(ps_f[:, (n + 1) * P:(n + 2) * P], ss[:, 4 * n:4 * n + 4, :].rearrange("q b g -> q (b g)"), ident[:, :])
            last.then_inc(fin_mm, 1)

        @blk.gpsimd
        def _(pool):
            with pool.Fori(0, NG // U5) as i:
                for q in range(U5):
                    g, par = i * U5 + q, q % 2
                    pool.wait_ge(g_ready, g + 1)
                    nc.gpsimd.tensor_tensor(lastB[:, bass.ds(g, 1)], G[:, par, NCH - 1:], R(q, "SIN")[:, NCH - 1:], ALU.mult).then_inc(lastb_ready, 1)
                    nc.gpsimd.tensor_tensor(B[:, par, 1:], G[:, par, :], R(q, "SIN"), ALU.mult).then_inc(b_ready, 1)

        @blk.vector
        def _(dve):
            vec = nc.vector
            vec.memset(A[:, :, 0:1], 0.0)
            vec.memset(B[:, :, 0:1], 0.0).then_inc(edges0, 1)
            bias.widen_and_move(nc, dve)
            dve.wait_ge(edges0, 1)
            dve.wait_ge(loaded, 7 * 16)

            def turn(g, q, first=False):
                dve.wait_ge(flipped, g + 1)
                if not first:
                    dve.wait_ge(y_done, g + 1)
                vec.tensor_copy(uT[:, q, :], ps_u[:, :, :].rearrange("p i n -> p (i n)")[:, 0:NCH + DB]).then_inc(uT_ready, 1)

            def scan(g, q):
                par = q % 2
                dve.wait_ge(states, g + 1)
                vec.tensor_tensor(w1[:, par, :], ps_s[:, par, 0:NCH], R(q, "COS"), ALU.mult).then_inc(turned, 1)
                vec.tensor_tensor(w2[:, par, :], ps_w[:, par, 0:NCH], R(q, "SIN"), ALU.mult).then_inc(turned, 1)
                vec.tensor_copy(ss[:, :, bass.ds(g, 1)], ps_s[:, par, NCH:NCH + DB].unsqueeze(2)).then_inc(turned, 1)
                dve.wait_ge(turned, g * 3 + 3)
                vec.tensor_tensor(w1[:, par, :], w1[:, par, :], w2[:, par, :], ALU.add).then_inc(added, 1)
                dve.wait_ge(added, g + 1)
                vec.tensor_tensor_scan(G[:, par, :], r8[:, bass.ds(g, 1)].broadcast_to([P, NCH]), w1[:, par, :], 0.0, ALU.mult, ALU.add).then_inc(g_ready, 1)
                dve.wait_ge(g_ready, g + 1)
                vec.tensor_tensor(lastA[:, bass.ds(g, 1)], G[:, par, NCH - 1:], R(q, "COS")[:, NCH - 1:], ALU.mult).then_inc(last_ready, 1)
                vec.tensor_tensor(A[:, par, 1:], G[:, par, :], R(q, "COS"), ALU.mult).then_inc(a_ready, 1)

            for g in range(2):
                turn(g, g, True)
            scan(0, 0)
            turn(2, 2, True)
            scan(1, 1)
            turn(3, 3, True)
            with dve.Fori(0, NG // U5 - 1) as i:
                for k in range(2, U5 + 2):
                    scan(i * U5 + k, k % U5)
                    turn(i * U5 + k + 2, (k + 2) % U5)
            scan(NG - 2, U5 - 2)
            scan(NG - 1, U5 - 1)
            dve.wait_ge(last_ready, NG)
            dve.wait_ge(turned, 3 * NG)
            dve.wait_ge(lastb_ready, NG)
            vec.tensor_tensor(ss[:, :, :], ss[:, :, :], hp[:, :, :], ALU.add).then_inc(edges, 1)
            dve.wait_ge(fin_mm, 1)
            vec.tensor_copy(fin[:, :], ps_f[0:NG, 0:P]).then_inc(fin_out, 1)
            vec.tensor_copy(fins[:, :, :], ps_f[:, P:3 * P].rearrange("p (n q) -> p n q", n=2)).then_inc(fin_out, 1)


NR = NEG_ + NE
class MixingWeights:

    def __init__(self, held):
        sb = held.sb
        self.w_rt = sb("w_rt", [P, KD, NR])
        self.hi, self.lo = sb("hi", [P, 2 + KD, D], F32R), sb("lo", [P, 2 + KD, D], F32R)
        self.glu_hi, self.glu_lo = (a[:, 0:2, :].rearrange("p a (b n) -> p (a b) n", b=2) for a in (self.hi, self.lo))
        self.out_hi, self.out_lo = (a[:, 2:, :] for a in (self.hi, self.lo))
        self.b_glu, self.g_s, self.g_a = sb("b_glu", [P, SW]), sb("g_s", [P, SW]), sb("g_a", [P, AW])
        self.mod = sb("mod", [P, 2, 3, D])
        self.raw = None
        self.even, self.odd, self.rounded, self.rest, self.rows_in, self.smods = (
            held.sem(n) for n in ("even", "odd", "rounded", "rest", "rows_in", "smods"))

    def load(self, sp, T):
        by_row = lambda a: a.rearrange("a (k p) n -> p (a k) n", p=P)
        for dst, name in ((self.b_glu, "b_glu"), (self.g_s, "g_ssm_out"), (self.g_a, "g_attn_out")):
            sp.dma_start(dst[:, :], T[name][0, :].partition_broadcast(P)).then_inc(self.rows_in, 16)
        for r in range(3):
            sp.dma_start(self.mod[:, 0, r, :], mod_row(T, 2 + r)).then_inc(self.rows_in, 16)
        sp.dma_start(self.w_rt[:, :, 0:NEG_], by_row(T["w_group_router"])).then_inc(self.rows_in, 16)
        sp.dma_start(self.w_rt[:, :, NEG_:], T["w_expert_router"].rearrange("a (k p) g e -> p (a k) (g e)", p=P)).then_inc(self.rows_in, 16)

    def load_raw(self, pool, T, k):
        dst, arrived = self.raw[:, k % 2, :], self.odd if k % 2 else self.even
        if k < 2:
            pool.dma_start(dst.rearrange("p (b n) -> p b n", b=2), T["w_glu"][0, 2 * k * P:2 * (k + 1) * P, :].rearrange("(b p) n -> p b n", p=P)).then_inc(arrived, 16)
        else:
            pool.dma_start(dst, T["w_out"][0, (k - 2) * P:(k - 1) * P, :]).then_inc(arrived, 16)

    def split(self, nc, pool, T):
        for r in range(3):
            load_sample_mod(pool, T, self.mod[:, 1, r, :], 2 + r, self.smods)
        self.load_raw(pool, T, 0)
        self.load_raw(pool, T, 1)
        for k in range(2 + KD):
            pool.wait_ge(self.odd if k % 2 else self.even, (k // 2 + 1) * 16)
            nc.gpsimd.tensor_copy(self.hi[:, k, :], self.raw[:, k % 2, :]).then_inc(self.rounded, 1)
            pool.wait_ge(self.rounded, k + 1)
            nc.gpsimd.tensor_tensor(self.lo[:, k, :], self.raw[:, k % 2, :], self.hi[:, k, :].bitcast(F32), ALU.subtract).then_inc(self.rest, 1)
            pool.wait_ge(self.rest, k + 1)
            if k < KD:
                self.load_raw(pool, T, k + 2)
        pool.wait_ge(self.smods, 3 * 2 * DB * 16)
        pool.wait_ge(self.rows_in, 8 * 16)


def bias_view(T, rows, head, keys):
    flat = T["bias_rows"].rearrange("p m -> (p m)")[P - 1:P - 1 + rows * (RB - 1)]
    return flat.rearrange("(q m) -> q m", m=RB - 1)[:, head * BW:head * BW + keys]


def prompt_attention(nc, T, top, mw):
    with Stage(nc, top, "at") as s:
        ident = s.sb("ident", [P, P])
        mw.raw = s.sb("raw", [P, 2, D])
        bias = s.sb("bias", [P, NH, 2 * WIN])
        sink, nsink = s.sb("sink", [P, NH]), s.sb("nsink", [P, NH])
        qk, v = s.sb("qk", [P, 2, AW + KVW]), s.sb("v", [P, 2, KVW])
        qT, kT = s.sb("qT", [P, 2, GQ, P]), s.sb("kT", [P, 2, P])
        sc, pT = s.sb("sc", [P, 2, NH, 2 * WIN]), s.sb("pT", [P, NH, 2, P])
        mx, nm, ds = s.sb("mx", [P, 2, NH]), s.sb("nm", [P, 2, NH]), s.sb("ds", [P, 2, NH])
        sm, es, rd = s.sb("sm", [P, 2, NH]), s.sb("es", [P, 2, NH]), s.sb("rd", [P, 2, NH])
        o = s.sb("o", [P, 2, AW])
        ps_s, ps_q, ps_t, ps_o = s.ps("ps_s", [P, 4, 512]), s.ps("ps_q", [P, 512]), s.ps("ps_t", [P, 2, 512]), s.ps("ps_o", [P, 512])
        (consts, in_even, in_odd, sunk, flipped, q_moved, k_moved, v_even, v_odd, scored, biased, negated, shifted, exped, es_ready,
         turned, pt_a, pt_v, attended, den, rden, o_out, st_even, st_odd) = (s.sem(n) for n in (
             "consts", "in_even", "in_odd", "sunk", "flipped", "q_moved", "k_moved", "v_even", "v_odd", "scored", "biased", "negated",
             "shifted", "exped", "es_ready", "turned", "pt_a", "pt_v", "attended", "den", "rden", "o_out", "st_even", "st_odd"))
        passed, kv_stored = s.sem("passed"), s.sem("kv_stored")
        blk = s.block()
        pv = T["proj"][:, SW:].rearrange("(n p) d -> p n d", p=P)
        av = T["attn"].rearrange("(n p) d -> p n d", p=P)
        HALF = NPT // 2

        @blk.sync
        def _(sp):
            def load(t, par, arrived):
                sp.dma_start(qk[:, par, :].unsqueeze(1), pv[:, bass.ds(t, 1), 0:AW + KVW]).then_inc(arrived, 16)

            def load_v(t, par):
                sp.dma_start(v[:, par, :].unsqueeze(1), pv[:, bass.ds(t, 1), AW + KVW:]).then_inc(v_odd if par else v_even, 16)

            def store(t, par, stored):
                sp.wait_ge(o_out, t + 2)
                sp.dma_start(av[:, bass.ds(t, 1), :], o[:, par, :].unsqueeze(1)).then_inc(stored, 16)

            sp.sem_inc(st_even, 16)
            sp.sem_inc(st_odd, 16)
            sp.dma_start(ident[:, :], T["ident"]).then_inc(consts, 16)
            sp.dma_start(sink[:, :], T["attn_sinks"][0, :].partition_broadcast(P)).then_inc(consts, 16)
            load(0, 0, in_even)
            load(1, 1, in_odd)
            load_v(0, 0)
            for h in range(NH):
                sp.dma_start(bias[:, h, :], bias_view(T, P, h, 2 * WIN)).then_inc(consts, 16)
            mw.load(sp, T)
            for n, name in enumerate("kv"):
                c0 = SW + AW + n * KVW
                cut = T["proj"][:, c0:c0 + KVW]
                sp.dma_start(T[f"o_{name}_prompt"].rearrange("a b w h d -> (a b w) (h d)"), cut[SEQ - WIN:SEQ, :]).then_inc(kv_stored, 16)
                old = T[f"cache_{name}"].rearrange("a b w h d -> (a b) w (h d)")
                new = T[f"o_{name}_sample"].rearrange("a b w h d -> (a b) w (h d)")
                sp.dma_start(new[:, 0:WIN - DT, :], old[:, DT:WIN, :]).then_inc(kv_stored, 16)
                sp.dma_start(new[:, WIN - DT:WIN, :], cut[SEQ:SEQ + NS, :].rearrange("(b t) c -> b t c", t=DT)).then_inc(kv_stored, 16)
            with sp.Fori(0, HALF - 1) as i:
                for par, arrived, stored in ((0, in_even, st_even), (1, in_odd, st_odd)):
                    t = i * 2 + par
                    sp.wait_ge(flipped, t + 1)
                    load(t + 2, par, arrived)
                    sp.wait_ge(attended, t + 2)
                    load_v(t + 1, 1 - par)
                    store(t, par, stored)
            sp.wait_ge(attended, NPT)
            load_v(NPT - 1, 1)
            store(NPT - 2, 0, st_even)
            store(NPT - 1, 1, st_odd)
            sp.wait_ge(st_even, (HALF + 1) * 16)
            sp.wait_ge(st_odd, (HALF + 1) * 16)
            sp.wait_ge(kv_stored, 6 * 16)

        @blk.gpsimd
        def _(pool):
            mw.split(nc, pool, T)

        @blk.scalar
        def _(act):
            def queries(t, par):
                act.wait_ge(flipped, t + 1)
                nc.scalar.activation(kT[:, par, :], ps_t[:, 0, 0:P], ACT.Copy).then_inc(k_moved, 1)
                nc.scalar.activation(qT[:, par, :, :].rearrange("p g n -> p (g n)"), ps_q[:, :], ACT.Copy, scale=HD ** -0.5).then_inc(q_moved, 1)

            def exps(t, par, k0):
                act.wait_ge(negated, t + 1)
                for h in range(NH):
                    nc.scalar.activation(sc[:, par, h, k0:], sc[:, par, h, k0:], ACT.Exp, bias=nm[:, par, h:h + 1],
                                         accum_out=sm[:, par, h:h + 1]).then_inc(exped, 1)
                act.wait_ge(shifted, t + 1)
                nc.scalar.activation(es[:, par, :], ds[:, par, :], ACT.Exp).then_inc(es_ready, 1)

            def probs(t, k0):
                for b in (0, 2):
                    act.wait_ge(turned, t * 4 + b + 1)
                    src = ps_t[:, 0, :].rearrange("p (h k n) -> p h k n", h=2, k=2)
                    nc.scalar.activation(pT[:, 2 * b:2 * b + 2, k0 // WIN:, :], src[:, :, k0 // WIN:, :], ACT.Copy).then_inc(pt_a, 1)

            queries(0, 0)
            queries(1, 1)
            exps(0, 0, WIN)
            probs(0, WIN)
            queries(2, 0)
            exps(1, 1, 0)
            with act.Fori(0, HALF - 2) as i:
                for par in (1, 0):
                    t = i * 2 + 2 - par
                    probs(t, 0)
                    queries(t + 2, par)
                    exps(t + 1, 1 - par, 0)
            probs(NPT - 3, 0)
            queries(NPT - 1, 1)
            exps(NPT - 2, 0, 0)
            probs(NPT - 2, 0)
            exps(NPT - 1, 1, 0)
            probs(NPT - 1, 0)

        @blk.vector
        def _(dve):
            vec = nc.vector
            dve.sem_inc(biased, 8)
            dve.sem_inc(o_out, 1)
            dve.wait_ge(consts, 10 * 16)
            vec.tensor_scalar(nsink[:, :], sink[:, :], -1.0, None, ALU.mult).then_inc(sunk, 1)
            dve.wait_ge(sunk, 1)

            def maxima(t, par, k0, heads):
                for h in heads:
                    if h % 2 == 0:
                        dve.wait_ge(scored, t * 4 + h // 2 + 1)
                        dve.sem_inc(passed, 1)
                    at = h % 2 * 2 * WIN
                    vec.tensor_tensor_reduce(out=sc[:, par, h, k0:], in0=ps_s[:, h // 2, at + k0:at + 2 * WIN], in1=bias[:, h, k0:],
                                             scale=1.0, scalar=MASKED, op0=ALU.add, op1=ALU.max,
                                             accum_out=mx[:, par, h:h + 1]).then_inc(biased, 1)

            def negate(t, par):
                dve.wait_ge(biased, t * 8 + 16)
                vec.scalar_tensor_tensor(nm[:, par, :], mx[:, par, :], -1.0, nsink[:, :], ALU.mult, ALU.min).then_inc(negated, 1)
                dve.wait_ge(negated, t + 1)
                vec.tensor_tensor(ds[:, par, :], sink[:, :], nm[:, par, :], ALU.add).then_inc(shifted, 1)

            def probs(t, k0, b):
                dve.wait_ge(turned, t * 4 + b + 1)
                src = ps_t[:, 1, :].rearrange("p (h k n) -> p h k n", h=2, k=2)
                vec.tensor_copy(pT[:, 2 * b:2 * b + 2, k0 // WIN:, :], src[:, :, k0 // WIN:, :]).then_inc(pt_v, 1)

            def out(t, par, stored, n):
                dve.wait_ge(es_ready, t + 1)
                vec.tensor_tensor(sm[:, par, :], sm[:, par, :], es[:, par, :], ALU.add).then_inc(den, 1)
                dve.wait_ge(den, t + 1)
                vec.reciprocal(rd[:, par, :], sm[:, par, :]).then_inc(rden, 1)
                dve.wait_ge(rden, t + 1)
                dve.wait_ge(attended, t + 2)
                dve.wait_ge(stored, n)
                vec.tensor_tensor(o[:, par, :].rearrange("p (h d) -> p h d", h=NH), ps_o[:, :].rearrange("p (h d) -> p h d", h=NH),
                                  rd[:, par, :].unsqueeze(2).broadcast_to([P, NH, HD]), ALU.mult).then_inc(o_out, 1)

            def step(t, par, k0, stored, n):
                for half, b in enumerate((1, 3)):
                    maxima(t + 1, 1 - par, 0, range(4 * half, 4 * half + 4))
                    probs(t, k0, b)
                negate(t + 1, 1 - par)
                out(t, par, stored, n)

            maxima(0, 0, WIN, range(NH))
            negate(0, 0)
            step(0, 0, WIN, st_even, 16)
            with dve.Fori(0, HALF - 1) as i:
                for par, stored in ((1, st_odd), (0, st_even)):
                    step(i * 2 + 2 - par, par, 0, stored, i * 16 + (16 if par else 32))
            for b in (1, 3):
                probs(NPT - 1, 0, b)
            out(NPT - 1, 1, st_odd, HALF * 16)

        @blk.tensor
        def _(pe):
            pe.sem_inc(attended, 1)
            pe.wait_ge(consts, 10 * 16)

            def flip(t, par, arrived, n, first, turned_before=None):
                pe.wait_ge(arrived, n)
                if not first:
                    pe.wait_ge(q_moved, t)
                for g in range(GQ):
                    nc.tensor.transpose(ps_q[:, g * P:(g + 1) * P], qk[:, par, g * P:(g + 1) * P], ident[:, :])
                if turned_before is not None:
                    pe.wait_ge(pt_a, turned_before * 2 + 2)
                nc.tensor.transpose(ps_t[:, 0, 0:P], qk[:, par, AW:], ident[:, :]).then_inc(flipped, 1)

            def scores(t, par, blocks, heads=range(NH)):
                if heads[0] == 0:
                    pe.wait_ge(q_moved, t + 1)
                    pe.wait_ge(k_moved, t + 1)
                for h in heads:
                    kv, g = divmod(h, GQ)
                    rows = slice(kv * HD, (kv + 1) * HD)
                    if h % 2 == 0:
                        pe.wait_ge(biased, t * 8 + h + 2)
                    for k in blocks:
                        slot = par if k else 1 - par
                        at = (h % 2 * 2 + k) * WIN
                        last = nc.tensor.matmul(ps_s[:, h // 2, at:at + WIN], qT[rows, par, g, :], kT[rows, slot, :], start=True, stop=True)
                    if h % 2:
                        last.then_inc(scored, 1)

            def turn(t, par, blocks, pairs=range(4)):
                for b in pairs:
                    pe.wait_ge(exped, t * 8 + 2 * b + 2)
                    if b >= 2:
                        pe.wait_ge(*((pt_a, t * 2 + 1) if b == 2 else (pt_v, t * 2 + 1)))
                    for h in (2 * b, 2 * b + 1):
                        for k in blocks:
                            at = (h % 2 * 2 + k) * P
                            last = nc.tensor.transpose(ps_t[:, b % 2, at:at + P], sc[:, par, h, k * WIN:(k + 1) * WIN], ident[:, :])
                    last.then_inc(turned, 1)

            def attend(t, par, blocks, n):
                pe.wait_ge(v_odd if par else v_even, n)
                pe.wait_ge(o_out, t + 1)
                for h in range(NH):
                    if h % 4 == 0:
                        pe.wait_ge(pt_a, t * 2 + 1 + h // 4)
                    if h % 4 == 2:
                        pe.wait_ge(pt_v, t * 2 + 1 + h // 4)
                    kv = h // GQ
                    for k in blocks:
                        slot = par if k else 1 - par
                        last = nc.tensor.matmul(ps_o[:, h * HD:(h + 1) * HD], pT[:, h, k, :], v[:, slot, kv * HD:(kv + 1) * HD],
                                                start=(k == blocks[0]), stop=(k == blocks[-1]))
                last.then_inc(attended, 1)

            def step(t, par, blocks, n, n_ahead):
                for b in range(4):
                    scores(t + 1, 1 - par, (0, 1), (2 * b, 2 * b + 1))
                    turn(t, par, blocks, (b,))
                if n_ahead is not None:
                    flip(t + 2, par, in_odd if par else in_even, n_ahead, False, t)
                attend(t, par, blocks, n)

            flip(0, 0, in_even, 16, True)
            scores(0, 0, (1,))
            flip(1, 1, in_odd, 16, False)
            step(0, 0, (1,), 16, 32)
            with pe.Fori(0, HALF - 2) as i:
                for par in (1, 0):
                    at = i * 16 + (16 if par else 32)
                    step(i * 2 + 2 - par, par, (0, 1), at, at + 16)
            step(NPT - 3, 1, (0, 1), HALF * 16 - 16, HALF * 16)
            step(NPT - 2, 0, (0, 1), HALF * 16, None)
            turn(NPT - 1, 1, (0, 1))
            attend(NPT - 1, 1, (0, 1), HALF * 16)


def sample_attention(nc, T, top):
    QKV = AW + 2 * KVW
    NB = 2 * NKV
    KEYS = WIN + DT
    G4 = GQ * DT
    with Stage(nc, top, "as") as s:
        ident = s.sb("ident", [P, P])
        bias = s.sb("bias", [P, NKV, KEYS])
        hsel, sink_c, sink, nsink = s.sb("hsel", [NH, NKV, P]), s.sb("sink_c", [NH, 1]), s.sb("sink", [P, NB]), s.sb("nsink", [P, NB])
        qkv = s.sb("qkv", [NS, QKV])
        kc, vc, vn = s.sb("kc", [P, DB, KVW]), s.sb("vc", [P, DB, KVW]), s.sb("vn", [DT, DB, KVW])
        qT, kT = s.sb("qT", [P, DB, GQ, DT]), s.sb("kT", [P, DB, KEYS])
        sc, pc, pn = s.sb("sc", [P, NB, KEYS]), s.sb("pc", [P, NB, P]), s.sb("pn", [DT, NB, P])
        mx, nm, ds, sm, es, rd = (s.sb(n, [P, NB]) for n in ("mx", "nm", "ds", "sm", "es", "rd"))
        o = s.sb("o", [P, NB, HD])
        ps_k, ps_q, ps_s, ps_o, ps_h = s.ps("ps_k", [P, 2, 512]), s.ps("ps_q", [P, 512]), s.ps("ps_s", [P, 2, 512]), s.ps("ps_o", [P, 512]), s.ps("ps_h", [P, 512])
        (loaded, biases, copied, flipped, moved, scored, step, negated, shifted, exped, turned, pmoved, attended, o_out, stored) = (
            s.sem(n) for n in ("loaded", "biases", "copied", "flipped", "moved", "scored", "step", "negated", "shifted", "exped",
                               "turned", "pmoved", "attended", "o_out", "stored"))
        blk = s.block()

        def store(eng, half):
            for b in range(half * 4, half * 4 + 4):
                for kv in range(NKV):
                    for g in range(GQ):
                        r, row, c = b % 4 * G4 + g * DT, SEQ + b * DT, (kv * GQ + g) * HD
                        eng.dma_start(T["attn"][row:row + DT, c:c + HD], o[r:r + DT, b // 4 * NKV + kv, :]).then_inc(stored, 16)

        @blk.sync
        def _(sp):
            sp.dma_start(ident[:, :], T["ident"]).then_inc(loaded, 16)
            sp.dma_start(hsel[:, :, :], T["hsel"]).then_inc(loaded, 16)
            sp.dma_start(sink_c[:, :], T["attn_sinks"].rearrange("a h -> h a"), allow_slow_non_contiguous=True).then_inc(loaded, 16)
            new = T["proj"][SEQ:SEQ + NS, :]
            sp.dma_start(qkv[:, :], new[:, SW:]).then_inc(loaded, 16)
            sp.dma_start(kc[:, :, :], T["cache_k"].rearrange("a b w h d -> w (a b) (h d)")).then_inc(loaded, 16)
            sp.dma_start(vc[:, :, :], T["cache_v"].rearrange("a b w h d -> w (a b) (h d)")).then_inc(loaded, 16)
            sp.dma_start(vn[:, :, :], new[:, SW + AW + KVW:].rearrange("(b t) c -> t b c", t=DT)).then_inc(loaded, 16)
            for kv in range(NKV):
                for g in range(GQ):
                    sp.dma_start(bias[g * DT:(g + 1) * DT, kv, :], bias_view(T, DT, kv * GQ + g, KEYS)).then_inc(biases, 16)
            sp.wait_ge(biases, NH * 16)
            for n in range(1, 4):
                sp.dma_start(bias[n * G4:(n + 1) * G4, :, :], bias[0:G4, :, :]).then_inc(copied, 16)
            sp.wait_ge(o_out, 1)
            store(sp, 0)
            sp.wait_ge(stored, DB * NH * 16)

        @blk.scalar
        def _(act):
            act.wait_ge(flipped, 1)
            nc.scalar.activation(qT[:, :, :, :].rearrange("p b g t -> p g b t"), ps_q[:, 0:GQ * NS].rearrange("p (g b t) -> p g b t", g=GQ, b=DB),
                                 ACT.Copy, scale=HD ** -0.5).then_inc(moved, 1)
            act.wait_ge(negated, 1)
            for n in range(NB):
                nc.scalar.activation(sc[:, n, :], sc[:, n, :], ACT.Exp, bias=nm[:, n:n + 1], accum_out=sm[:, n:n + 1]).then_inc(exped, 1)
            act.wait_ge(shifted, 1)
            nc.scalar.activation(es[:, :], ds[:, :], ACT.Exp).then_inc(exped, 1)
            act.wait_ge(o_out, 1)
            store(act, 1)

        @blk.vector
        def _(dve):
            vec = nc.vector
            st_ = Steps(dve, step)
            dve.wait_ge(flipped, 1)
            vec.tensor_copy(kT[:, :, 0:WIN], ps_k[:, :, :].rearrange("p b (c n) -> p (b c) n", c=4)).then_inc(moved, 1)
            vec.tensor_copy(kT[:, :, WIN:], ps_h[:, 0:NS].rearrange("p (b t) -> p b t", b=DB)).then_inc(moved, 1)
            for n in range(2):
                st_.then(vec.tensor_copy(sink[:, n * NKV:(n + 1) * NKV], ps_h[:, 64:64 + NKV]))
            st_.then(vec.tensor_scalar(nsink[:, :], sink[:, :], -1.0, None, ALU.mult))
            dve.wait_ge(copied, 3 * 16)
            dve.wait_ge(scored, 1)
            for n in range(NB):
                st_.then(vec.tensor_tensor_reduce(out=sc[:, n, :], in0=ps_s[:, n % 2, n // 2 * 256:n // 2 * 256 + KEYS], in1=bias[:, n % 2, :],
                                                  scale=1.0, scalar=MASKED, op0=ALU.add, op1=ALU.max, accum_out=mx[:, n:n + 1]))
            vec.scalar_tensor_tensor(nm[:, :], mx[:, :], -1.0, nsink[:, :], ALU.mult, ALU.min).then_inc(negated, 1)
            dve.wait_ge(negated, 1)
            vec.tensor_tensor(ds[:, :], sink[:, :], nm[:, :], ALU.add).then_inc(shifted, 1)
            dve.wait_ge(turned, 1)
            vec.tensor_copy(pc[:, :, :], ps_q[:, :].rearrange("p (n r) -> p n r", n=NB)).then_inc(pmoved, 1)
            vec.tensor_copy(pn[:, :, :], ps_k[0:DT, 0, :].rearrange("p (n r) -> p n r", n=NB)).then_inc(pmoved, 1)
            dve.wait_ge(exped, NB + 1)
            st_.then(vec.tensor_tensor(sm[:, :], sm[:, :], es[:, :], ALU.add))
            st_.then(vec.reciprocal(rd[:, :], sm[:, :]))
            dve.wait_ge(attended, 1)
            vec.tensor_tensor(o[:, :, :], ps_o[:, 0:NB * HD].rearrange("p (n d) -> p n d", n=NB), rd[:, :].unsqueeze(2).broadcast_to([P, NB, HD]),
                              ALU.mult).then_inc(o_out, 1)

        @blk.tensor
        def _(pe):
            pe.wait_ge(loaded, 7 * 16)
            for b in range(DB):
                nc.tensor.transpose(ps_k[:, b // 4, b % 4 * P:(b % 4 + 1) * P], kc[:, b, :], ident[:, :])
            for g in range(GQ):
                nc.tensor.transpose(ps_q[:, g * NS:(g + 1) * NS], qkv[:, g * P:(g + 1) * P], ident[0:NS, 0:NS])
            nc.tensor.transpose(ps_h[:, 0:NS], qkv[:, AW:AW + KVW], ident[0:NS, 0:NS])
            for kv in range(NKV):
                last = nc.tensor.matmul(ps_h[:, 64 + kv:65 + kv], hsel[:, kv, :], sink_c[:, :], start=True, stop=True)
            last.then_inc(flipped, 1)
            pe.wait_ge(moved, 3)
            for b in range(DB):
                for kv in range(NKV):
                    rows, r0 = slice(kv * HD, (kv + 1) * HD), b % 4 * G4
                    last = nc.tensor.matmul(ps_s[r0:r0 + G4, kv, b // 4 * 256:b // 4 * 256 + KEYS], qT[rows, b, :, :].rearrange("p g t -> p (g t)"),
                                            kT[rows, b, :], start=True, stop=True)
            last.then_inc(scored, 1)
            pe.wait_ge(exped, NB)
            for n in range(NB):
                nc.tensor.transpose(ps_q[:, n * P:(n + 1) * P], sc[:, n, 0:WIN], ident[:, :])
                last = nc.tensor.transpose(ps_k[0:DT, 0, n * P:(n + 1) * P], sc[:, n, WIN:], ident[:, :])
            last.then_inc(turned, 1)
            pe.wait_ge(pmoved, 2)
            for b in range(DB):
                for kv in range(NKV):
                    n, r0, cv = b // 4 * NKV + kv, b % 4 * G4, slice(kv * HD, (kv + 1) * HD)
                    dst = ps_o[r0:r0 + G4, n * HD:(n + 1) * HD]
                    nc.tensor.matmul(dst, pc[:, n, r0:r0 + G4], vc[:, b, cv], start=True, stop=False)
                    last = nc.tensor.matmul(dst, pn[:, n, r0:r0 + G4], vn[:, b, cv], start=False, stop=True)
            last.then_inc(attended, 1)


GELU_C = 2.0 * math.sqrt(2.0 / math.pi) / 2.0


def mixing(nc, T, top, m):
    with Stage(nc, top, "mx") as s:
        ident = s.sb("ident", [P, P])
        w_rt, b_glu, g_s, g_a, mod = m.w_rt, m.b_glu, m.g_s, m.g_a, m.mod
        y, at, x = s.sb("y", [P, 2, SW]), s.sb("at", [P, 2, AW]), s.sb("x", [P, 2, D])
        sq, gq, gw, th1 = s.sb("sq", [P, SW]), s.sb("gq", [P, SW]), s.sb("gw", [P, SW]), s.sb("th1", [P, SW])
        z2, zT = s.sb("z2", [P, 2, SW]), s.sb("zT", [P, 4, P], F32R)
        z_lo, h_lo = s.sb("z_lo", [P, 4, P], F32R), s.sb("h_lo", [P, KD, P], F32R)
        gv, th2, o4 = s.sb("gv", [P, SW]), s.sb("th2", [P, SW]), s.sb("o4", [P, SW])
        j1, j2, j3, j4 = s.sb("j1", [P, D], BF16), s.sb("j2", [P, D], BF16), s.sb("j3", [P, SW], BF16), s.sb("j4", [P, AW], BF16)
        hc, hT = s.sb("hc", [P, 2, D]), s.sb("hT", [P, KD, P], F32R)
        tmp, hn, hnT = s.sb("tmp", [P, D]), s.sb("hn", [P, 2, D]), s.sb("hnT", [P, KD, P])
        st = s.sb("st", [P, 2, 12])
        half = s.sb("half", [P, 2])
        lg = s.sb("lg", [P, NT, NR])
        ps_t, ps_g, ps_m, ps_z = s.ps("ps_t", [P, 2, 512]), s.ps("ps_g", [P, 512]), s.ps("ps_m", [P, 2, D]), s.ps("ps_z", [P, 512])
        names = ("in_even in_odd x_even x_odd stx_even stx_odd sth_even sth_odd consts sq_ready g_step w_ready th1_ready "
                 "z_ready z_flipped z_hi z_moved glu_done glu_used th2_ready o_ready ss5 ss34 p3 r34 hc_ready hc_part h_flipped h_moved_a h_moved_v mix_done "
                 "ss1 p1 r1 mix_used x2_ready ss2 p2 r2 hn_part hn_ready n_flipped n_moved_a n_moved_v routed lg_used passed halved scaled lg_stored").split()
        S = {n: s.sem(n) for n in names}
        blk = s.block()
        HALF = NPT // 2
        LAST = NT - 1
        NCONST = 1

        class Tile:

            def __init__(self, i, k):
                self.t, self.par, self.q = i * 2 + k, k % 2, i + k // 2
                self.last = isinstance(i, int) and self.t == LAST

            def sem(self, name):
                return S[f"{name}_{'odd' if self.par else 'even'}"]

        def run(eng, step, pairs=HALF - 1):
            around = lambda i, k: [Tile(i, k + d) if not isinstance(i, int) or 0 <= i * 2 + k + d <= LAST else None for d in (-1, 0, 1, 2)]
            step(*around(0, 0))
            with eng.Fori(0, pairs) as i:
                for k in (1, 2):
                    step(*around(i, k))
            for t in range(2 * pairs + 1, NT):
                step(*around(0, t))

        tiles = lambda a: a.rearrange("(n p) d -> p n d", p=P)
        yv, av, x2v, hnv = tiles(T["y"]), tiles(T["attn"]), tiles(T["x2"]), tiles(T["hn2"])
        xp = T["x_prompt"].rearrange("a (n p) d -> p (a n) d", p=P)
        xs = T["x_sample"].rearrange("b t d -> (b t) d")

        @blk.sync
        def _(sp):
            def load_ya(u, first=False):
                if not first:
                    sp.wait_ge(S["hc_ready"], u.t - 1)
                if u.last:
                    for h in range(2):
                        rows = slice(h * NS, (h + 1) * NS)
                        sp.dma_start(y[rows, u.par, :], T["y"][SEQ:SEQ + NS, :]).then_inc(u.sem("in"), 16)
                        sp.dma_start(at[rows, u.par, :], T["attn"][SEQ:SEQ + NS, :]).then_inc(u.sem("in"), 16)
                else:
                    sp.dma_start(y[:, u.par, :].unsqueeze(1), yv[:, bass.ds(u.t, 1), :]).then_inc(u.sem("in"), 16)
                    sp.dma_start(at[:, u.par, :].unsqueeze(1), av[:, bass.ds(u.t, 1), :]).then_inc(u.sem("in"), 16)

            def load_x(u):
                sp.wait_ge(u.sem("stx"), u.q * 16 + 16)
                if u.last:
                    for h in range(2):
                        sp.dma_start(x[h * NS:(h + 1) * NS, u.par, :], xs).then_inc(u.sem("x"), 16)
                else:
                    sp.dma_start(x[:, u.par, :].unsqueeze(1), xp[:, bass.ds(u.t, 1), :]).then_inc(u.sem("x"), 16)

            def store(u):
                sp.wait_ge(S["hn_ready"], u.t + 1)
                sp.dma_start(x2v[:, bass.ds(u.t, 1), :], x[:, u.par, :].unsqueeze(1)).then_inc(u.sem("stx"), 16)
                sp.dma_start(hnv[:, bass.ds(u.t, 1), :], hn[:, u.par, :].unsqueeze(1)).then_inc(u.sem("sth"), 16)

            def step(before, tile, after, after2):
                if after2:
                    load_ya(after2)
                if before:
                    store(before)
                    if after:
                        load_x(after)

            for n in ("stx_even", "stx_odd", "sth_even", "sth_odd"):
                sp.sem_inc(S[n], 16)
            load_ya(Tile(0, 0), True)
            load_ya(Tile(0, 1), True)
            sp.dma_start(ident[:, :], T["ident"]).then_inc(S["consts"], 16)
            load_x(Tile(0, 0))
            load_x(Tile(0, 1))
            run(sp, step, HALF - 2)
            store(Tile(0, LAST))
            sp.wait_ge(S["lg_used"], NT + 1)
            sp.dma_start(T["logits"], lg[:, :, :].rearrange("p t r -> p (t r)")).then_inc(S["lg_stored"], 16)
            sp.wait_ge(S["lg_stored"], 16)
            for n in ("stx", "sth"):
                sp.wait_ge(S[n + "_even"], (HALF + 2) * 16)
                sp.wait_ge(S[n + "_odd"], (HALF + 1) * 16)

        @blk.gpsimd
        def _(pool):
            nc.gpsimd.memset(half[:, :], -0.5).then_inc(S["halved"], 1)
            pool.wait_ge(S["halved"], 1)

            def power(u, src, col, n, scales, part, ready):
                pool.wait_ge(S[src], u.t + 1)
                pool.sem_inc(S["passed"], 1)
                a = st[:, u.par, :]
                for m, c in enumerate(scales):
                    last = nc.gpsimd.tensor_scalar(a[:, col + m:col + m + 1], a[:, col + m:col + m + 1], c, EPS, ALU.mult, ALU.add)
                    last.then_inc(S[part], 1)
                pool.wait_ge(S[part], u.t * len(scales) + len(scales))
                nc.gpsimd.tensor_tensor(a[:, col + n:col + 2 * n], a[:, col:col + n], half[:, 0:n], ALU.pow).then_inc(S[ready], 1)

            def norms_out(u):
                power(u, "ss1", 0, 1, (1.0 / D,), "p1", "r1")
                power(u, "ss2", 2, 1, (1.0 / D,), "p2", "r2")

            def norms_in(u):
                power(u, "ss34", 4, 2, (1.0 / (16 * SW), 1.0 / AW), "p3", "r34")

            def step(before, tile, after, after2):
                if before:
                    norms_out(before)
                if after:
                    norms_in(after)

            norms_in(Tile(0, 0))
            run(pool, step)
            norms_out(Tile(0, LAST))

        @blk.scalar
        def _(act):
            A = nc.scalar.activation

            def gelu(u):
                act.wait_ge(u.sem("in"), (HALF + 2) * 32 if u.last else u.q * 32 + 32)
                A(sq[:, :], y[:, u.par, :], ACT.Square).then_inc(S["sq_ready"], 1)
                act.wait_ge(S["w_ready"], u.t + 1)
                A(th1[:, :], gw[:, :], ACT.Tanh).then_inc(S["th1_ready"], 1)

            def square_attn(u):
                A(j4[:, :], at[:, u.par, :], ACT.Square, accum_out=st[:, u.par, 5:6]).then_inc(S["ss5"], 1)

            def glu(u):
                act.wait_ge(S["glu_used"], u.t + 2)
                A(th2[:, :], gv[:, :], ACT.Tanh, scale=0.5).then_inc(S["th2_ready"], 1)
                act.wait_ge(S["o_ready"], u.t + 1)
                A(j3[:, :], o4[:, :], ACT.Square, accum_out=st[:, u.par, 4:5]).then_inc(S["ss34"], 1)

            def square_mix(u):
                act.wait_ge(S["mix_done"], u.t + 1)
                A(j1[:, :], ps_m[:, u.par, :], ACT.Square, accum_out=st[:, u.par, 0:1]).then_inc(S["ss1"], 1)

            def square_x2(u):
                act.wait_ge(S["x2_ready"], u.t + 1)
                A(j2[:, :], x[:, u.par, :], ACT.Square, accum_out=st[:, u.par, 2:3]).then_inc(S["ss2"], 1)

            def move(u, dst, flipped, moved):
                act.wait_ge(S[flipped], u.t + 1)
                A(dst[:, 0:4, :], ps_t[:, 0, :].rearrange("p (k n) -> p k n", k=4), ACT.Copy).then_inc(S[moved], 1)

            def round_z(u):
                act.wait_ge(S["z_flipped"], u.t + 1)
                A(zT[:, :, :], ps_z[:, :].rearrange("p (k n) -> p k n", k=4), ACT.Copy).then_inc(S["z_hi"], 1)

            def round_h(u):
                act.wait_ge(S["h_flipped"], u.t + 1)
                for h in range(2):
                    A(hT[:, 4 * h:4 * h + 4, :], ps_t[:, h, :].rearrange("p (k n) -> p k n", k=4), ACT.Copy).then_inc(S["h_moved_a"], 1)

            def step(before, tile, after, after2):
                if before:
                    square_mix(before)
                if after:
                    square_attn(after)
                if before:
                    square_x2(before)
                if after:
                    glu(after)
                if after2:
                    gelu(after2)
                if before:
                    move(before, hnT, "n_flipped", "n_moved_a")
                if after2:
                    round_z(after2)
                if after:
                    round_h(after)

            gelu(Tile(0, 0))
            round_z(Tile(0, 0))
            square_attn(Tile(0, 0))
            glu(Tile(0, 0))
            gelu(Tile(0, 1))
            round_z(Tile(0, 1))
            round_h(Tile(0, 0))
            run(act, step, HALF - 2)
            square_mix(Tile(0, LAST))
            square_x2(Tile(0, LAST))
            move(Tile(0, LAST), hnT, "n_flipped", "n_moved_a")

        @blk.vector
        def _(dve):
            vec = nc.vector

            def gelu(u):
                dve.wait_ge(S["sq_ready"], u.t + 1)
                vec.tensor_scalar(gq[:, :], sq[:, :], GELU_C * 0.044715, GELU_C, ALU.mult, ALU.add).then_inc(S["g_step"], 1)
                dve.wait_ge(S["g_step"], u.t + 1)
                vec.tensor_tensor(gw[:, :], gq[:, :], y[:, u.par, :], ALU.mult).then_inc(S["w_ready"], 1)
                dve.wait_ge(S["th1_ready"], u.t + 1)
                vec.scalar_tensor_tensor(z2[:, u.par, :], th1[:, :], 1.0, y[:, u.par, :], ALU.add, ALU.mult).then_inc(S["z_ready"], 1)

            def move_z(u):
                dve.wait_ge(S["z_hi"], u.t + 1)
                vec.tensor_tensor(z_lo[:, :, :], ps_z[:, :].rearrange("p (k n) -> p k n", k=4), zT[:, :, :].bitcast(F32), ALU.subtract).then_inc(S["z_moved"], 1)

            def move_h(u):
                for h in range(2):
                    part = slice(4 * h, 4 * h + 4)
                    dve.wait_ge(S["h_moved_a"], u.t * 2 + h + 1)
                    vec.tensor_tensor(h_lo[:, part, :], ps_t[:, h, :].rearrange("p (k n) -> p k n", k=4), hT[:, part, :].bitcast(F32),
                                      ALU.subtract).then_inc(S["h_moved_v"], 1)

            def glu(u):
                dve.wait_ge(S["glu_done"], u.t + 1)
                vec.scalar_tensor_tensor(gv[:, :], ps_g[:, :], 0.5, b_glu[:, :], ALU.mult, ALU.add).then_inc(S["glu_used"], 1)
                dve.wait_ge(S["th2_ready"], u.t + 1)
                vec.scalar_tensor_tensor(o4[:, :], th2[:, :], 1.0, z2[:, u.par, :], ALU.add, ALU.mult).then_inc(S["o_ready"], 1)

            def norms(u):
                dve.wait_ge(S["r34"], u.t + 1)
                vec.scalar_tensor_tensor(hc[:, u.par, 0:SW], o4[:, :], st[:, u.par, 6:7], g_s[:, :], ALU.mult, ALU.mult)
                vec.scalar_tensor_tensor(hc[:, u.par, SW:], at[:, u.par, :], st[:, u.par, 7:8], g_a[:, :], ALU.mult, ALU.mult).then_inc(S["hc_ready"], 1)

            def residual(u):
                kind = 1 if u.last else 0
                dve.wait_ge(S["r1"], u.t + 1)
                vec.scalar_tensor_tensor(tmp[:, :], ps_m[:, u.par, :], st[:, u.par, 1:2], mod[:, kind, 0, :], ALU.mult, ALU.mult).then_inc(S["mix_used"], 1)
                dve.wait_ge(S["mix_used"], u.t + 3)
                dve.wait_ge(u.sem("x"), (HALF + 2) * 16 if u.last else u.q * 16 + 16)
                vec.tensor_tensor(x[:, u.par, :], x[:, u.par, :], tmp[:, :], ALU.add).then_inc(S["x2_ready"], 1)

            def modulated(u):
                kind = 1 if u.last else 0
                dve.wait_ge(S["r2"], u.t + 1)
                dve.wait_ge(u.sem("sth"), u.q * 16 + 16)
                vec.scalar_tensor_tensor(hn[:, u.par, :], x[:, u.par, :], st[:, u.par, 3:4], mod[:, kind, 1, :], ALU.mult, ALU.mult).then_inc(S["hn_part"], 1)
                dve.wait_ge(S["hn_part"], u.t + 1)
                vec.tensor_tensor(hn[:, u.par, :], hn[:, u.par, :], mod[:, kind, 2, :], ALU.add).then_inc(S["hn_ready"], 1)

            def move(u, dst, flipped, moved):
                dve.wait_ge(S[flipped], u.t + 1)
                vec.tensor_copy(dst[:, 4:8, :], ps_t[:, 1, :].rearrange("p (k n) -> p k n", k=4)).then_inc(S[moved], 1)

            def logits(u):
                dve.wait_ge(S["routed"], u.t + 1)
                vec.tensor_copy(lg[:, bass.ds(u.t, 1), :], ps_t[:, 1, 0:NR].unsqueeze(1)).then_inc(S["lg_used"], 1)

            def step(before, tile, after, after2):
                if before:
                    residual(before)
                if after:
                    glu(after)
                if before:
                    modulated(before)
                if after:
                    norms(after)
                if after2:
                    gelu(after2)
                if before:
                    move(before, hnT, "n_flipped", "n_moved_v")
                if before:
                    logits(before)
                if after2:
                    move_z(after2)
                if after:
                    move_h(after)

            for n, k in (("glu_used", 1), ("mix_used", 2), ("lg_used", 1)):
                dve.sem_inc(S[n], k)
            first = Tile(0, 0)
            gelu(first)
            dve.wait_ge(S["consts"], NCONST * 16)
            vec.tensor_scalar(g_s[:, :], g_s[:, :], 0.25, None, ALU.mult).then_inc(S["scaled"], 1)
            dve.wait_ge(S["scaled"], 1)
            move_z(first)
            glu(first)
            norms(first)
            gelu(Tile(0, 1))
            move_z(Tile(0, 1))
            move_h(first)
            run(dve, step, HALF - 2)
            residual(Tile(0, LAST))
            modulated(Tile(0, LAST))
            move(Tile(0, LAST), hnT, "n_flipped", "n_moved_v")
            logits(Tile(0, LAST))

        @blk.tensor
        def _(pe):
            def flip(src, u, flipped):
                for k in range(KD):
                    last = nc.tensor.transpose(ps_t[:, k // 4, k % 4 * P:(k % 4 + 1) * P], src[:, u.par, k * P:(k + 1) * P], ident[:, :])
                last.then_inc(S[flipped], 1)

            def flip_z(u, first=False):
                pe.wait_ge(S["z_ready"], u.t + 1)
                if not first:
                    pe.wait_ge(S["z_moved"], u.t)
                for k in range(4):
                    last = nc.tensor.transpose(ps_z[:, k * P:(k + 1) * P], z2[:, u.par, k * P:(k + 1) * P], ident[:, :])
                last.then_inc(S["z_flipped"], 1)

            def glu(u):
                pe.wait_ge(S["z_moved"], u.t + 1)
                pe.wait_ge(S["glu_used"], u.t + 1)
                for k in range(4):
                    last = three_products(nc, ps_g[:, :], zT[:, k, :], z_lo[:, k, :], m.glu_hi[:, k, :], m.glu_lo[:, k, :], k == 0, k == 3)
                last.then_inc(S["glu_done"], 1)

            def flip_h(u, before):
                pe.wait_ge(S["hc_ready"], u.t + 1)
                if before:
                    pe.wait_ge(S["lg_used"], before.t + 2)
                flip(hc, u, "h_flipped")

            def mix(u, c):
                if c == 0:
                    pe.wait_ge(S["h_moved_v"], u.t * 2 + 2)
                    pe.wait_ge(S["mix_used"], u.t + 1)
                at_ = slice(c * 512, (c + 1) * 512)
                for k in range(KD):
                    last = three_products(nc, ps_m[:, u.par, at_], hT[:, k, :], h_lo[:, k, :], m.out_hi[:, k, at_], m.out_lo[:, k, at_],
                                          k == 0, k == KD - 1)
                if c == 1:
                    last.then_inc(S["mix_done"], 1)

            def flip_n(u, later=True):
                pe.wait_ge(S["hn_ready"], u.t + 1)
                if later:
                    pe.wait_ge(S["h_moved_v"], u.t * 2 + 4)
                flip(hn, u, "n_flipped")

            def route(u):
                pe.wait_ge(S["n_moved_a"], u.t + 1)
                pe.wait_ge(S["n_moved_v"], u.t + 1)
                pe.wait_ge(S["lg_used"], u.t + 1)
                for k in range(KD):
                    last = nc.tensor.matmul(ps_t[:, 1, 0:NR], hnT[:, k, :], w_rt[:, k, :], start=(k == 0), stop=(k == KD - 1))
                last.then_inc(S["routed"], 1)

            def step(before, tile, after, after2):
                if after:
                    glu(after)
                mix(tile, 0)
                mix(tile, 1)
                if before:
                    flip_n(before)
                if after2:
                    flip_z(after2)
                if before:
                    route(before)
                if after:
                    flip_h(after, before)

            pe.wait_ge(S["consts"], NCONST * 16)
            flip_z(Tile(0, 0), True)
            glu(Tile(0, 0))
            flip_z(Tile(0, 1))
            flip_h(Tile(0, 0), None)
            run(pe, step, HALF - 2)
            flip_n(Tile(0, LAST), False)
            route(Tile(0, LAST))


PAIRS = 2 * (SEQ + NS)
NTILE = (PAIRS + NE * (P - 1)) // P
NSLOT = NTILE * P
NSL = 3
U = 4
NSLOT_ALL = NSLOT + 2 * P


def routing(nc, T, top):
    E16 = [P, NT, NE]
    with Stage(nc, top, "rt") as s:
        lg, bias = s.sb("lg", [P, NT, NR]), s.sb("bias", [P, NR])
        ident, before, ones = s.sb("ident", [P, P]), s.sb("before", [P, P]), s.sb("ones", [P, P])
        valid, dump, rows, tau = s.sb("valid", [P, NT]), s.sb("dump", [P, 2, NT]), s.sb("rows", [P, 2, NT]), s.sb("tau", [1, NTILE])
        f17 = {n: s.sb(n, [P, NT]) for n in ("mg", "gp", "m1", "m2", "e2", "den", "taken")}
        f68 = {n: s.sb(n, [P, NT, 4]) for n in ("ohg", "eq", "ex", "sel", "tmp", "oh1", "oh2")}
        OH, A, slot, prod = s.sb("OH", [P, 2, NT, NE]), s.sb("A", E16), s.sb("slot", E16), s.sb("prod", E16)
        tp = s.sb("tp", [P, NT + 1, NE])
        nt, end, base = s.sb("nt", [P, NE]), s.sb("end", [P, NE]), s.sb("base", [P, NE])
        sf, su = s.sb("sf", [P, 2, NT]), s.sb("su", [P, 2, NT], U32)
        wts = s.sb("wts", [P, 2, NT])
        smap, tok, part = s.sb("smap", [NTILE, P]), s.sb("tok", [P, NTILE]), s.sb("part", [P, NTILE])
        rows_u = s.sb("rows_u", [P, 2, NTILE], U32)
        cmp, et, et_i = s.sb("cmp", [1, NTILE, NE]), s.sb("et", [1, 3, NTILE]), s.sb("et_i", [1, 3, NTILE], I32)
        et_n = s.sb("et_n", [1, NTILE])
        ps_r, ps_c, ps_s = s.ps("ps_r", [P, 512]), s.ps("ps_c", [P, 512]), s.ps("ps_s", [P, 512])
        (loaded, cleared, step, de, exped, hot, counted, slots, scattered, read, turned, tiles_out, stored) = (
            s.sem(n) for n in ("loaded", "cleared", "step", "de", "exped", "hot", "counted", "slots", "scattered",
                               "read", "turned", "tiles_out", "stored"))
        blk = s.block()
        srcs = [(lg[:, :, :].rearrange("p t r -> p (t r)"), T["logits"]), (ident[:, :], T["ident"]), (before[:, :], T["before"]),
                (valid[:, :], T["valid"]), (dump[:, :, :], T["dump"]), (rows[:, :, :], T["rows"]), (tau[:, :], T["tau"]),
                (bias[:, 0:NEG_], T["b_group_router"][0, :].partition_broadcast(P)),
                (bias[:, NEG_:], T["b_expert_router"].rearrange("a g e -> (a g e)").partition_broadcast(P))]

        @blk.sync
        def _(sp):
            for dst, src in srcs:
                sp.dma_start(dst, src).then_inc(loaded, 16)
            sp.dma_start(T["slotmap"], T["unused"]).then_inc(cleared, 16)
            sp.wait_ge(slots, 1)
            sp.dma_start(T["weights"], wts[:, :, :].rearrange("p k t -> p (k t)")).then_inc(stored, 16)
            sp.wait_ge(scattered, 2 * NT * 16)
            sp.dma_start(smap[:, :], T["slotmap"][0:NSLOT, :].rearrange("(n p) a -> n (p a)", p=P)).then_inc(read, 16)
            sp.wait_ge(tiles_out, 2)
            sp.dma_start(T["tile_rows"], rows_u[:, :, :]).then_inc(stored, 16)
            sp.dma_start(T["tile_plan"], et_i[:, :, :]).then_inc(stored, 16)
            sp.wait_ge(stored, 3 * 16)

        @blk.gpsimd
        def _(pool):
            pool.wait_ge(cleared, 16)
            pool.wait_ge(slots, 1)
            for k in range(2):
                for t in range(NT):
                    pool.indirect_dma_start(T["slotmap"], bass.IndirectOffsetOnAxis(su[:, k, t:t + 1], 0), rows[:, k, t:t + 1], None).then_inc(scattered, 16)
            pool.wait_ge(scattered, 2 * NT * 16)

        @blk.scalar
        def _(act):
            act.wait_ge(de, 1)
            nc.scalar.activation(f68["ex"][:, :, :], f68["ex"][:, :, :], ACT.Exp).then_inc(exped, 1)
            act.wait_ge(de, 2)
            nc.scalar.activation(f17["e2"][:, :], f17["e2"][:, :], ACT.Exp).then_inc(exped, 1)

        @blk.tensor
        def _(pe):
            pe.wait_ge(hot, 1)
            a = A[:, :, :].rearrange("p t e -> p (t e)")
            nc.tensor.matmul(ps_r[:, 0:NT * NE], before[:, :], a, start=True, stop=True)
            nc.tensor.matmul(ps_c[:, 0:NT * NE], ones[:, :], a, start=True, stop=True).then_inc(counted, 1)
            pe.wait_ge(read, 16)
            nc.tensor.transpose(ps_s[:, 0:NTILE], smap[:, :], ident[0:NTILE, 0:NTILE]).then_inc(turned, 1)

        @blk.vector
        def _(dve):
            vec = nc.vector
            st_ = Steps(dve, step)
            tt = lambda o, a, b, op: st_.then(vec.tensor_tensor(o, a, b, op))
            ts = lambda o, a, x, y, p, q: st_.then(vec.tensor_scalar(o, a, x, y, p, q))
            red = lambda o, a, op: st_.then(vec.tensor_reduce(o, a, AX.X, op))
            st_.then(vec.memset(ones[:, :], 1.0))
            dve.wait_ge(loaded, len(srcs) * 16)
            mg, gp, m1, m2, e2, den, taken = (f17[n][:, :] for n in ("mg", "gp", "m1", "m2", "e2", "den", "taken"))
            ohg, eq, ex, sel, tmp, oh1, oh2 = (f68[n] for n in ("ohg", "eq", "ex", "sel", "tmp", "oh1", "oh2"))
            over4 = lambda a: a.unsqueeze(2).broadcast_to([P, NT, 4])

            def first_max(out, vals, m):
                red(m, vals, ALU.max)
                tt(eq[:, :, :], vals, over4(m), ALU.is_equal)
                st_.then(vec.tensor_copy(out[:, :, 0:1], eq[:, :, 0:1]))
                st_.then(vec.tensor_copy(taken.unsqueeze(2), eq[:, :, 0:1]))
                for k in range(1, 4):
                    tt(out[:, :, k:k + 1], eq[:, :, k:k + 1], taken.unsqueeze(2), ALU.is_gt)
                    if k < 3:
                        tt(taken.unsqueeze(2), eq[:, :, k:k + 1], taken.unsqueeze(2), ALU.max)

            tt(lg[:, :, :], lg[:, :, :], bias[:, :].unsqueeze(1).broadcast_to([P, NT, NR]), ALU.add)
            gl, el = lg[:, :, 0:NEG_], lg[:, :, NEG_:]
            first_max(ohg, gl, mg)
            vec.tensor_tensor(ex[:, :, :], gl, over4(mg), ALU.subtract).then_inc(de, 1)
            dve.wait_ge(exped, 1)
            red(gp, ex[:, :, :], ALU.add)
            st_.then(vec.reciprocal(gp, gp))
            for g in range(NEG_):
                dst = sel if g == 0 else tmp
                tt(dst[:, :, :], el[:, :, g * EPG:(g + 1) * EPG], over4(ohg[:, :, g]), ALU.mult)
                if g:
                    tt(sel[:, :, :], sel[:, :, :], tmp[:, :, :], ALU.add)
            first_max(oh1, sel[:, :, :], m1)
            st_.then(vec.scalar_tensor_tensor(tmp[:, :, :], oh1[:, :, :], MASKED, sel[:, :, :], ALU.mult, ALU.add))
            first_max(oh2, tmp[:, :, :], m2)
            vec.tensor_tensor(e2, m2, m1, ALU.subtract).then_inc(de, 1)
            for k, oh in enumerate((oh1, oh2)):
                o = OH[:, k, :, :].rearrange("p t (g e) -> p t g e", g=NEG_)
                wide = [P, NT, NEG_, EPG]
                tt(o, ohg[:, :, :].unsqueeze(3).broadcast_to(wide), oh[:, :, :].unsqueeze(2).broadcast_to(wide), ALU.mult)
                tt(OH[:, k, :, :], OH[:, k, :, :], valid[:, :].unsqueeze(2).broadcast_to(E16), ALU.mult)
            vec.tensor_tensor(A[:, :, :], OH[:, 0, :, :], OH[:, 1, :, :], ALU.add).then_inc(hot, 1)
            dve.wait_ge(exped, 2)
            ts(den, e2, 1.0, None, ALU.add, ALU.bypass)
            st_.then(vec.reciprocal(den, den))
            tt(wts[:, 0, :], gp, den, ALU.mult)
            tt(wts[:, 1, :], wts[:, 0, :], e2, ALU.mult)
            dve.wait_ge(counted, 1)
            st_.then(vec.memset(tp[:, 0, :], 0.0))
            for t in range(NT):
                tt(tp[:, t + 1, :], tp[:, t, :], ps_c[:, t * NE:(t + 1) * NE], ALU.add)
            ts(nt[:, :], tp[:, NT, :], 1.0 / P, (P - 1.0) / P - 0.5 + 0.5 / P, ALU.mult, ALU.add)
            ts(nt[:, :], nt[:, :], MAGIC, None, ALU.add, ALU.bypass)
            ts(nt[:, :], nt[:, :], -MAGIC, None, ALU.add, ALU.bypass)
            st_.then(vec.tensor_tensor_scan(end[:, :], ones[:, 0:NE], nt[:, :], 0.0, ALU.mult, ALU.add))
            tt(base[:, :], end[:, :], nt[:, :], ALU.subtract)
            ts(base[:, :], base[:, :], float(P), None, ALU.mult, ALU.bypass)
            tt(slot[:, :, :], tp[:, 0:NT, :], ps_r[:, 0:NT * NE].rearrange("p (t e) -> p t e", t=NT), ALU.add)
            tt(slot[:, :, :], slot[:, :, :], base[:, :].unsqueeze(1).broadcast_to(E16), ALU.add)
            for k in range(2):
                tt(prod[:, :, :], OH[:, k, :, :], slot[:, :, :], ALU.mult)
                red(sf[:, k, :], prod[:, :, :], ALU.add)
            tt(sf[:, :, :], sf[:, :, :], dump[:, :, :], ALU.add)
            vec.tensor_copy(su[:, :, :], sf[:, :, :]).then_inc(slots, 1)
            tt(cmp[:, :, :], tau[:, :].unsqueeze(2).broadcast_to([1, NTILE, NE]), end[0:1, :].unsqueeze(1).broadcast_to([1, NTILE, NE]), ALU.is_ge)
            expert, fresh, slot_w = (et[:, n, :] for n in range(3))
            red(expert, cmp[:, :, :], ALU.add)
            ts(expert, expert, NE - 1.0, None, ALU.min, ALU.bypass)
            st_.then(vec.memset(fresh[:, 0:1], 1.0))
            tt(fresh[:, 1:], expert[:, 1:], expert[:, 0:NTILE - 1], ALU.not_equal)
            st_.then(vec.tensor_tensor_scan(et_n[:, :], ones[0:1, 0:NTILE], fresh, -1.0, ALU.mult, ALU.add))
            ts(slot_w, et_n[:, :], 1.0 / NSL, 0.5 / NSL - 0.5, ALU.mult, ALU.add)
            ts(slot_w, slot_w, MAGIC, None, ALU.add, ALU.bypass)
            ts(slot_w, slot_w, -MAGIC, None, ALU.add, ALU.bypass)
            st_.then(vec.scalar_tensor_tensor(slot_w, slot_w, -float(NSL), et_n[:, :], ALU.mult, ALU.add))
            vec.tensor_copy(et_i[:, :, :], et[:, :, :]).then_inc(tiles_out, 1)
            dve.wait_ge(turned, 1)
            row = ps_s[:, 0:NTILE]
            st_.mark(vec.tensor_copy(rows_u[:, 1, :], row))
            ts(part[:, :], row, float(TOK), -float(TOK), ALU.is_ge, ALU.mult)
            tt(tok[:, :], row, part[:, :], ALU.add)
            ts(part[:, :], row, float(2 * TOK), None, ALU.is_lt, ALU.bypass)
            tt(tok[:, :], tok[:, :], part[:, :], ALU.mult)
            vec.tensor_copy(rows_u[:, 0, :], tok[:, :]).then_inc(tiles_out, 1)


def experts(nc, T, top):
    with Stage(nc, top, "ex") as s:
        ident, rows, plan = s.sb("ident", [P, P]), s.sb("rows", [P, 2, NTILE], U32), s.sb("plan", [1, 3, NTILE], I32)
        wgu, wd = s.sb("wgu", [P, NSL * KD * 2 * DE]), s.sb("wd", [P, NSL * 2 * D])
        idx, to = s.sb("idx", [P, U], U32), s.sb("to", [P, 2], U32)
        x, xT = s.sb("x", [P, U, D]), s.sb("xT", [P, KD, P])
        th, sg, a, aT = s.sb("th", [P, DE]), s.sb("sg", [P, DE]), s.sb("a", [P, DE]), s.sb("aT", [P, 2, P])
        o, free = s.sb("o", [P, 2, D]), s.sb("free", [16, 4])
        ps_t, ps_h, ps_a, ps_o = s.ps("ps_t", [P, 2, 512]), s.ps("ps_h", [P, 2, 512]), s.ps("ps_a", [P, 512]), s.ps("ps_o", [P, D])
        names = ("loaded picked to_picked passed x_flipped x_moved_a x_moved_v gu_done th_ready "
                 "sg_ready a_ready a_flipped a_moved d_done o_out_a o_out_v st_even st_odd").split()
        S = {n: s.sem(n) for n in names}
        blk = s.block()
        for n in range(U):
            for name in ("gu", "d", "x"):
                S[name, n] = s.sem(f"{name}{n}")
        HT = NTILE // 2
        sem = lambda name, par: S[f"{name}_{'odd' if par else 'even'}"]
        gv, uv = (T[n].rearrange("a e (k p) f -> p (a e) k f", p=P) for n in ("w_exp_gate", "w_exp_up"))
        dv = T["w_exp_down"].rearrange("a e (k p) n -> p (a e) k n", p=P)
        gu_slots = wgu[:, :].rearrange("p (s k f) -> p s k f", s=NSL, k=KD)
        d_slots = wd[:, :].rearrange("p (s k f) -> p s k f", s=NSL, k=2)

        @blk.sync
        def _(sp):
            sp.dma_start(ident[:, :], T["ident"]).then_inc(S["loaded"], 16)
            sp.dma_start(rows[:, :, :], T["tile_rows"]).then_inc(S["loaded"], 16)
            sp.dma_start(plan[:, :, :], T["tile_plan"]).then_inc(S["loaded"], 16)
            sp.wait_ge(S["loaded"], 48)
            with sp.Fori(0, NTILE // U) as i:
                for n in range(U):
                    t = i * U + n
                    e = sp.value_load(plan[0:1, 0, bass.ds(t, 1)], min_val=0, max_val=NE - 1)
                    fresh = sp.value_load(plan[0:1, 1, bass.ds(t, 1)], min_val=0, max_val=1)
                    slot = sp.value_load(plan[0:1, 2, bass.ds(t, 1)], min_val=0, max_val=NSL - 1)
                    sp.wait_ge(S["gu_done"], t + 1)
                    for half, view in enumerate((gv, uv)):
                        sp.dma_start(gu_slots[:, bass.ds(slot, 1), :, half * DE:(half + 1) * DE], view[:, bass.ds(e, 1), :, :], cond=fresh).then_inc(S["gu", n], 16)
                    sp.wait_ge(S["d_done"], t + 1)
                    sp.dma_start(d_slots[:, bass.ds(slot, 1), :, :], dv[:, bass.ds(e, 1), :, :], cond=fresh).then_inc(S["d", n], 16)

        @blk.gpsimd
        def _(pool):
            pool.dma_start(free[0:16, 0:2], T["rows"][0:16, 0, 0:2]).then_inc(S["st_even"], 16)
            pool.dma_start(free[0:16, 2:4], T["rows"][0:16, 0, 2:4]).then_inc(S["st_odd"], 16)
            pool.wait_ge(S["loaded"], 48)

            def gather(t, n):
                nc.gpsimd.tensor_copy(idx[:, n:n + 1], rows[:, 0, bass.ds(t, 1)]).then_inc(S["picked"], 1)
                pool.wait_ge(S["picked"], t + 1)
                pool.sem_inc(S["passed"], 1)
                pool.indirect_dma_start(x[:, n, :], None, T["hn2"], bass.IndirectOffsetOnAxis(idx[:, n:n + 1], 0)).then_inc(S["x", n], 16)

            def scatter(t, par):
                pool.wait_ge(S["o_out_a"], t + 2)
                pool.wait_ge(S["o_out_v"], t + 2)
                pool.sem_inc(S["passed"], 1)
                nc.gpsimd.tensor_copy(to[:, par:par + 1], rows[:, 1, bass.ds(t, 1)]).then_inc(S["to_picked"], 1)
                pool.wait_ge(S["to_picked"], t + 1)
                pool.sem_inc(S["passed"], 1)
                pool.indirect_dma_start(T["moe"], bass.IndirectOffsetOnAxis(to[:, par:par + 1], 0), o[:, par, :], None).then_inc(sem("st", par), 16)

            def refill(t, n):
                pool.wait_ge(S["x_flipped"], t + 1)
                pool.sem_inc(S["passed"], 1)
                gather(t + U, n)

            for n in range(U):
                gather(n, n)
            refill(0, 0)
            refill(1, 1)
            with pool.Fori(0, NTILE // U - 2) as i:
                for n in range(U):
                    refill(i * U + n + 2, (n + 2) % U)
                    scatter(i * U + n, n % 2)
            for t in range(NTILE - 2 * U, NTILE):
                if t + 2 < NTILE - U:
                    refill(t + 2, (t + 2) % U)
                scatter(t, t % 2)
            pool.wait_ge(S["st_even"], (HT + 1) * 16)
            pool.wait_ge(S["st_odd"], (HT + 1) * 16)

        @blk.scalar
        def _(act):
            act.sem_inc(S["o_out_a"], 1)
            A = nc.scalar.activation

            def move_x(t):
                act.wait_ge(S["x_flipped"], t + 1)
                A(xT[:, 0:4, :], ps_t[:, 0, :].rearrange("p (k n) -> p k n", k=4), ACT.Copy).then_inc(S["x_moved_a"], 1)

            def gate(t, par):
                act.wait_ge(S["gu_done"], t + NSL + 1)
                A(th[:, :], ps_h[:, par, 0:DE], ACT.Tanh, scale=0.5).then_inc(S["th_ready"], 1)

            def move_a(t):
                act.wait_ge(S["a_flipped"], t + 1)
                A(aT[:, :, :], ps_a[:, 0:2 * P].rearrange("p (k n) -> p k n", k=2), ACT.Copy, scale=0.5).then_inc(S["a_moved"], 1)

            def out(t, par, q):
                act.wait_ge(S["d_done"], t + NSL + 1)
                act.wait_ge(sem("st", par), q * 16 + 16)
                A(o[:, par, 0:512], ps_o[:, 0:512], ACT.Copy).then_inc(S["o_out_a"], 1)

            move_x(0)
            gate(0, 0)
            move_x(1)
            move_a(0)
            def step(t, k, i):
                par = k % 2
                gate(t, par)
                move_x(t + 1)
                out(t - 1, 1 - par, i * (U // 2) + (k - 1) // 2)
                move_a(t)

            with act.Fori(0, NTILE // U - 1) as i:
                for k in range(1, U + 1):
                    step(i * U + k, k, i)
            for k in range(1, U - 1):
                step(NTILE - U + k, k, NTILE // U - 1)
            gate(NTILE - 1, 1)
            out(NTILE - 2, 0, HT - 1)
            move_a(NTILE - 1)
            out(NTILE - 1, 1, HT - 1)

        @blk.vector
        def _(dve):
            vec = nc.vector
            dve.sem_inc(S["o_out_v"], 1)

            def move_x(t):
                dve.wait_ge(S["x_flipped"], t + 1)
                vec.tensor_copy(xT[:, 4:8, :], ps_t[:, 1, :].rearrange("p (k n) -> p k n", k=4)).then_inc(S["x_moved_v"], 1)

            def gate(t, par):
                dve.wait_ge(S["th_ready"], t + 1)
                vec.scalar_tensor_tensor(sg[:, :], th[:, :], 1.0, ps_h[:, par, 0:DE], ALU.add, ALU.mult).then_inc(S["sg_ready"], 1)
                dve.wait_ge(S["sg_ready"], t + 1)
                vec.tensor_tensor(a[:, :], sg[:, :], ps_h[:, par, DE:], ALU.mult).then_inc(S["a_ready"], 1)

            def out(t, par, q):
                dve.wait_ge(S["d_done"], t + NSL + 1)
                dve.wait_ge(sem("st", par), q * 16 + 16)
                vec.tensor_copy(o[:, par, 512:], ps_o[:, 512:]).then_inc(S["o_out_v"], 1)

            move_x(0)
            gate(0, 0)
            move_x(1)
            def step(t, k, i):
                par = k % 2
                gate(t, par)
                move_x(t + 1)
                out(t - 1, 1 - par, i * (U // 2) + (k - 1) // 2)

            with dve.Fori(0, NTILE // U - 1) as i:
                for k in range(1, U + 1):
                    step(i * U + k, k, i)
            for k in range(1, U - 1):
                step(NTILE - U + k, k, NTILE // U - 1)
            gate(NTILE - 1, 1)
            out(NTILE - 2, 0, HT - 1)
            out(NTILE - 1, 1, HT - 1)

        @blk.tensor
        def _(pe):
            pe.sem_inc(S["gu_done"], NSL)
            pe.sem_inc(S["d_done"], NSL)
            pe.wait_ge(S["loaded"], 48)

            def flip_x(t, n, q, first=False):
                pe.wait_ge(S["x", n], q * 16 + 16)
                if not first:
                    pe.wait_ge(S["x_moved_a"], t)
                    pe.wait_ge(S["x_moved_v"], t)
                for k in range(KD):
                    last = nc.tensor.transpose(ps_t[:, k // 4, k % 4 * P:(k % 4 + 1) * P], x[:, n, k * P:(k + 1) * P], ident[:, :])
                last.then_inc(S["x_flipped"], 1)

            def gate_up(t, n, q, slot):
                pe.wait_ge(S["x_moved_a"], t + 1)
                pe.wait_ge(S["x_moved_v"], t + 1)
                pe.wait_ge(S["gu", n], q * 32 + 32)
                for k in range(KD):
                    last = nc.tensor.matmul(ps_h[:, n % 2, :], xT[:, k, :], wgu[:, bass.ds((slot * KD + k) * 2 * DE, 2 * DE)],
                                            start=(k == 0), stop=(k == KD - 1))
                last.then_inc(S["gu_done"], 1)

            def flip_a(t):
                pe.wait_ge(S["a_ready"], t + 1)
                for k in range(2):
                    last = nc.tensor.transpose(ps_a[:, k * P:(k + 1) * P], a[:, k * P:(k + 1) * P], ident[:, :])
                last.then_inc(S["a_flipped"], 1)

            def down(t, n, q, slot):
                pe.wait_ge(S["a_moved"], t + 1)
                pe.wait_ge(S["d", n], q * 16 + 16)
                pe.wait_ge(S["o_out_a"], t + 1)
                pe.wait_ge(S["o_out_v"], t + 1)
                for c in range(2):
                    for k in range(2):
                        last = nc.tensor.matmul(ps_o[:, c * 512:(c + 1) * 512], aT[:, k, :], wd[:, bass.ds((slot * 2 + k) * D + c * 512, 512)], start=(k == 0), stop=(k == 1))
                last.then_inc(S["d_done"], 1)

            def slot_of(t):
                return pe.value_load(plan[0:1, 2, bass.ds(t, 1)], min_val=0, max_val=NSL - 1)

            def steps(t0, i, n):
                slot = {0: slot_of(t0), 1: slot_of(t0 + 1)}
                for k in range(1, n + 1):
                    gate_up(t0 + k, k % U, i + k // U, slot[k])
                    if k < n or n < U:
                        slot[k + 1] = slot_of(t0 + k + 1)
                    flip_x(t0 + k + 1, (k + 1) % U, i + (k + 1) // U)
                    down(t0 + k - 1, k - 1, i, slot[k - 1])
                    flip_a(t0 + k)
                return slot

            flip_x(0, 0, 0, True)
            gate_up(0, 0, 0, slot_of(0))
            flip_x(1, 1, 0)
            flip_a(0)
            with pe.Fori(0, NTILE // U - 1) as i:
                steps(i * U, i, U)
            last_i = NTILE // U - 1
            slot = steps(NTILE - U, last_i, U - 2)
            gate_up(NTILE - 1, U - 1, last_i, slot[U - 1])
            down(NTILE - 2, U - 2, last_i, slot[U - 2])
            flip_a(NTILE - 1)
            down(NTILE - 1, U - 1, last_i, slot[U - 1])


def combine(nc, T, top):
    with Stage(nc, top, "cb") as s:
        wts, G2, half = s.sb("wts", [P, 2, NT]), s.sb("G2", [P, 2, D]), s.sb("half", [P, 1])
        r, x = s.sb("r", [P, U, 2, D]), s.sb("x", [P, U, D])
        f1, f, j, g = s.sb("f1", [P, 2, D]), s.sb("f", [P, 2, D]), s.sb("j", [P, 2, D], BF16), s.sb("g", [P, D])
        o, st = s.sb("o", [P, 2, D]), s.sb("st", [P, 2, 4])
        names = "loaded smods halved step1 f_ready squared passed p1 rstd g_ready o_ready st_even st_odd".split()
        S = {n: s.sem(n) for n in names}
        r_in, x_in = [s.sem(f"r{n}") for n in range(U)], [s.sem(f"x{n}") for n in range(U)]
        blk = s.block()
        LAST = NT - 1
        stored = lambda n: S["st_odd" if n % 2 else "st_even"]
        mv = T["moe"][0:2 * TOK, :].rearrange("(n p) d -> p n d", p=P)
        x2v = T["x2"].rearrange("(n p) d -> p n d", p=P)
        ov = T["o_y_prompt"].rearrange("a (n p) d -> p (a n) d", p=P)

        @blk.sync
        def _(sp):
            def load(t, n):
                for k in range(2):
                    sp.dma_start(r[:, n, k, :].unsqueeze(1), mv[:, bass.ds(t + k * NT, 1), :]).then_inc(r_in[n], 16)
                sp.dma_start(x[:, n, :].unsqueeze(1), x2v[:, bass.ds(t, 1), :]).then_inc(x_in[n], 16)

            def store(t, n):
                sp.wait_ge(S["o_ready"], t + 1)
                sp.dma_start(ov[:, bass.ds(t, 1), :], o[:, n % 2, :].unsqueeze(1)).then_inc(stored(n), 16)

            sp.sem_inc(S["st_even"], 16)
            sp.sem_inc(S["st_odd"], 16)
            load(0, 0)
            sp.dma_start(wts[:, :, :].rearrange("p k t -> p (k t)"), T["weights"]).then_inc(S["loaded"], 16)
            sp.dma_start(G2[:, 0, :], mod_row(T, 5)).then_inc(S["loaded"], 16)
            for n in range(1, U):
                load(n, n)
            with sp.Fori(0, NPT // U - 1) as i:
                for n in range(U):
                    store(i * U + n, n)
                    load(i * U + n + U, n)
            for n in range(U):
                store(NPT - U + n, n)
                if n == 0:
                    for k in range(2):
                        sp.dma_start(r[0:NS, 0, k, :], T["moe"][k * TOK + SEQ:k * TOK + SEQ + NS, :]).then_inc(r_in[0], 16)
                    sp.dma_start(x[0:NS, 0, :], T["x2"][SEQ:SEQ + NS, :]).then_inc(x_in[0], 16)
            sp.wait_ge(S["o_ready"], NT)
            sp.dma_start(T["o_y_sample"].rearrange("b t d -> (b t) d"), o[0:NS, 0, :]).then_inc(S["st_even"], 16)
            sp.wait_ge(S["st_even"], (NPT // 2 + 2) * 16)
            sp.wait_ge(S["st_odd"], (NPT // 2 + 1) * 16)

        @blk.gpsimd
        def _(pool):
            nc.gpsimd.memset(half[:, :], -0.5).then_inc(S["halved"], 1)
            pool.wait_ge(S["halved"], 1)
            load_sample_mod(pool, T, G2[:, 1, :], 5, S["smods"])

            def power(t, par, rows=P):
                a = st[0:rows, par, :]
                pool.wait_ge(S["squared"], t + 1)
                pool.sem_inc(S["passed"], 1)
                nc.gpsimd.tensor_scalar(a[:, 1:2], a[:, 0:1], 1.0 / D, EPS, ALU.mult, ALU.add).then_inc(S["p1"], 1)
                pool.wait_ge(S["p1"], t + 1)
                nc.gpsimd.tensor_tensor(a[:, 2:3], a[:, 1:2], half[0:rows, :], ALU.pow).then_inc(S["rstd"], 1)

            with pool.Fori(0, NPT // 2) as i:
                for par in range(2):
                    power(i * 2 + par, par)
            power(LAST, 0, NS)

        @blk.scalar
        def _(act):
            def square(t, par, rows=P):
                act.wait_ge(S["f_ready"], t + 1)
                nc.scalar.activation(j[0:rows, par, :], f[0:rows, par, :], ACT.Square, accum_out=st[0:rows, par, 0:1]).then_inc(S["squared"], 1)

            with act.Fori(0, NPT // 2) as i:
                for par in range(2):
                    square(i * 2 + par, par)
            square(LAST, 0, NS)

        @blk.vector
        def _(dve):
            vec = nc.vector
            dve.wait_ge(S["loaded"], 2 * 16)

            def weigh(t, n, q, rows=P):
                R = slice(0, rows)
                dve.wait_ge(r_in[n], q * 32 + 32)
                vec.tensor_scalar(f1[R, n % 2, :], r[R, n, 0, :], wts[R, 0, bass.ds(t, 1)], None, ALU.mult).then_inc(S["step1"], 1)
                dve.wait_ge(S["step1"], t + 1)
                vec.scalar_tensor_tensor(f[R, n % 2, :], r[R, n, 1, :], wts[R, 1, bass.ds(t, 1)], f1[R, n % 2, :], ALU.mult, ALU.add).then_inc(S["f_ready"], 1)

            def finish(t, n, q, rows=P, kind=0):
                R = slice(0, rows)
                dve.wait_ge(S["rstd"], t + 1)
                vec.scalar_tensor_tensor(g[R, :], f[R, n % 2, :], st[R, n % 2, 2:3], G2[R, kind, :], ALU.mult, ALU.mult).then_inc(S["g_ready"], 1)
                dve.wait_ge(S["g_ready"], t + 1)
                dve.wait_ge(x_in[n], q * 16 + 16)
                dve.wait_ge(stored(n), (q * (U // 2) + n // 2) * 16 + 16)
                vec.tensor_tensor(o[R, n % 2, :], g[R, :], x[R, n, :], ALU.add).then_inc(S["o_ready"], 1)

            weigh(0, 0, 0)
            with dve.Fori(0, NPT // U - 1) as i:
                for n in range(U):
                    weigh(i * U + n + 1, (n + 1) % U, i + (n + 1) // U)
                    finish(i * U + n, n, i)
            q = NPT // U - 1
            for n in range(U - 1):
                weigh(NPT - U + n + 1, n + 1, q)
                finish(NPT - U + n, n, q)
            weigh(LAST, 0, q + 1, NS)
            finish(NPT - 1, U - 1, q)
            dve.wait_ge(S["smods"], 2 * DB * 16)
            dve.wait_ge(S["o_ready"], LAST)
            finish(LAST, 0, q + 1, NS, 1)


def constants():
    q = np.arange(P)
    swap = np.zeros((P, P), np.float32)
    swap[q, (q + NST) % P] = 1
    hsel = np.zeros((NH, NKV, P), np.float32)
    for r in range(P):
        for kv in range(NKV):
            hsel[kv * GQ + r // DT % GQ, kv, r] = 1
    valid = np.ones((P, NT), np.float32)
    valid[NS:, NT - 1] = 0
    dump = np.zeros((P, 2, NT), np.float32)
    for k in range(2):
        dump[NS:, k, NT - 1] = NSLOT + k * P + q[NS:]
    return {"ident": np.eye(P, dtype=np.float32), "swap": swap, "sgn": np.where(q < NST, 1, -1).astype(np.float32)[:, None],
            "onehot": bucket_onehot(), "hsel": hsel, "before": (q[:, None] < q[None, :]).astype(np.float32), "valid": valid, "dump": dump,
            "rows": (np.arange(2)[None, :, None] * TOK + np.arange(NT)[None, None, :] * P + q[:, None, None]).astype(np.float32),
            "unused": (2 * TOK + np.arange(NSLOT_ALL)).astype(np.float32)[:, None], "tau": np.arange(NTILE, dtype=np.float32)[None, :]}


SCRATCH = {"mods": ((1 + DB, 6, D), F32), "proj": ((TOK, INW), F32), "rec": ((NG, P, RECW), F32),
           "hpre": ((P, NG * DB), F32), "r8": ((P, NG), F32), "y": ((TOK, SW), F32), "bias_rows": ((P, RB), F32),
           "attn": ((TOK, AW), F32), "x2": ((TOK, D), F32), "hn2": ((TOK, D), F32), "logits": ((P, NT * NR), F32),
           "slotmap": ((NSLOT_ALL, 1), F32), "weights": ((P, 2 * NT), F32),
           "tile_rows": ((P, 2, NTILE), U32), "tile_plan": ((1, 3, NTILE), I32), "moe": ((2 * TOK + NSLOT, D), F32)}


def hybrid_layer(nc, T):
    for name, (shape, dt) in SCRATCH.items():
        T[name] = nc.dram_tensor(f"scratch_{name}", shape, dt).ap()
    with Semaphores(nc) as top:
        with Stage(nc, top, "wi") as held:
            w_in = InputWeights(held)
            modulation(nc, T, top, w_in)
            projection(nc, T, top, w_in)
        s5_tables(nc, T, top)
        s5(nc, T, top)
    with Semaphores(nc) as top:
        with Stage(nc, top, "mw") as held:
            mw = MixingWeights(held)
            prompt_attention(nc, T, top, mw)
            sample_attention(nc, T, top)
            mixing(nc, T, top, mw)
    with Semaphores(nc) as top:
        routing(nc, T, top)
        experts(nc, T, top)
        combine(nc, T, top)


INS = ["x_prompt", "x_sample", "cache_k", "cache_v", "state_ssm_re", "state_ssm_im", "c_prompt", "c_sample",
       "rel_bias_table", "w_ada", "b_ada", "g_pre_mix", "g_post_mix", "g_pre_ffn", "g_post_ffn", "w_in",
       "ssm_lam_re", "ssm_lam_im", "ssm_log_dt", "ssm_b_re", "ssm_b_im", "ssm_c_re", "ssm_c_im", "ssm_d",
       "w_glu", "b_glu", "attn_sinks", "g_ssm_out", "g_attn_out", "w_out", "w_group_router", "b_group_router",
       "w_expert_router", "b_expert_router", "w_exp_gate", "w_exp_up", "w_exp_down"]
OUTS = [("y_prompt", (1, SEQ, D)), ("y_sample", (DB, DT, D)),
        ("k_prompt", (1, 1, WIN, NKV, HD)), ("v_prompt", (1, 1, WIN, NKV, HD)),
        ("ssm_re_prompt", (1, 1, NG, NST)), ("ssm_im_prompt", (1, 1, NG, NST)),
        ("k_sample", (1, DB, WIN, NKV, HD)), ("v_sample", (1, DB, WIN, NKV, HD)),
        ("ssm_re_sample", (1, DB, NG, NST)), ("ssm_im_sample", (1, DB, NG, NST))]


def kernel(**inputs):
    import concourse.bacc as bacc
    from concourse.bass_utils import run_bass_kernel_spmd

    nc = bacc.Bacc("TRN2", target_bir_lowering=False, num_devices=1)
    arrays, T = {}, {}
    for name, a in {**{n: inputs[n] for n in INS}, **constants()}.items():
        a = np.ascontiguousarray(a)
        arrays[f"in_{name}_dram"] = a
        T[name] = nc.dram_tensor(f"in_{name}_dram", a.shape, mybir.dt.from_np(a.dtype), kind="ExternalInput").ap()
    for name, shape in OUTS:
        T["o_" + name] = nc.dram_tensor(f"out_{name}_dram", shape, F32, kind="ExternalOutput").ap()
    hybrid_layer(nc, T)
    r = run_bass_kernel_spmd(nc, [arrays], core_ids=[0])
    return tuple(r.results[0][f"out_{name}_dram"] for name, _ in OUTS)
```
